# Optimizing a Trainium2 kernel written in Bass

```python
import math
import jax
import jax.numpy as jnp
from jax import lax
import numpy as np
import jax, jax.numpy as jnp

D_MODEL = 1024
BATCH = 1
SEQ = 512
DEPTH = 1

D_MIX = D_MODEL
D_S5 = D_MIX // 2
S5_GROUP = 16
N_S5_GROUPS = D_S5 // S5_GROUP
S5_STATE = 64
D_GDN = D_MIX - D_S5
GDN_HEAD_DIM = 128
N_GDN_HEADS = D_GDN // GDN_HEAD_DIM
CONV_WIDTH = 4
CHUNK = 64
D_IN = D_S5 + 4 * D_GDN + 2 * N_GDN_HEADS
N_EXPERT_GROUPS = 4
EXPERTS_PER_GROUP = 8
N_EXPERTS = N_EXPERT_GROUPS * EXPERTS_PER_GROUP
TOP_K_IN_GROUP = 2
D_EXPERT = D_MODEL // 4
N_MOD = 6
EPS = 1e-6


def rmsnorm(x, g):
    x32 = x.astype(jnp.float32)
    y = x32 * lax.rsqrt(jnp.mean(x32 * x32, axis=-1, keepdims=True) + EPS)
    return (y * g.astype(jnp.float32)).astype(x.dtype)

def l2norm(x):
    return x * lax.rsqrt(jnp.sum(x * x, axis=-1, keepdims=True) + EPS)

def modulate(h, shift, scale):
    return h * (1.0 + scale[:, None, :]) + shift[:, None, :]

def _linear_recurrence_combine(e1, e2):
    a1, b1 = e1
    a2, b2 = e2
    return a1 * a2, a2 * b1 + b2

def s5_mixer(u, lam_re, lam_im, log_step, b_re, b_im, c_re, c_im, d_skip, w_glu, b_glu):
    f32 = jnp.float32
    bsz, seq, _ = u.shape
    u32 = u.astype(f32)
    ug = u32.reshape(bsz, seq, N_S5_GROUPS, S5_GROUP)
    lam = lax.complex(lam_re.astype(f32), lam_im.astype(f32))
    step = jnp.exp(log_step.astype(f32))[:, None]
    lam_bar = jnp.exp(lam * step)
    b_c = lax.complex(b_re.astype(f32), b_im.astype(f32))
    b_bar = ((lam_bar - 1.0) / lam)[..., None] * b_c
    bu = lax.complex(jnp.einsum('gph,blgh->blgp', b_bar.real, ug),
                     jnp.einsum('gph,blgh->blgp', b_bar.imag, ug))
    a = jnp.broadcast_to(lam_bar, bu.shape)
    _, states = lax.associative_scan(_linear_recurrence_combine, (a, bu), axis=1)
    c_c = lax.complex(c_re.astype(f32), c_im.astype(f32))
    y = jnp.einsum('ghp,blgp->blgh', c_c, states).real.reshape(bsz, seq, D_S5)
    y = y + d_skip.astype(f32) * u32
    y = jax.nn.gelu(y)
    y = y * jax.nn.sigmoid(y @ w_glu.astype(f32) + b_glu.astype(f32))
    return y.astype(u.dtype)

def causal_depthwise_conv(x, w):
    k, ch = w.shape
    return lax.conv_general_dilated(x, w[:, None, :], window_strides=(1,),
                                    padding=[(k - 1, 0)],
                                    dimension_numbers=('NWC', 'WIO', 'NWC'),
                                    feature_group_count=ch)

def gated_delta_rule(q, k, v, g, beta):
    bsz, nh, seq, dk = q.shape
    dv = v.shape[-1]
    n_chunks = seq // CHUNK
    q = q.reshape(bsz, nh, n_chunks, CHUNK, dk)
    k = k.reshape(bsz, nh, n_chunks, CHUNK, dk)
    v = v.reshape(bsz, nh, n_chunks, CHUNK, dv)
    beta = beta.reshape(bsz, nh, n_chunks, CHUNK)
    g = jnp.cumsum(g.reshape(bsz, nh, n_chunks, CHUNK), axis=-1)
    idx = jnp.arange(CHUNK)
    causal = idx[:, None] >= idx[None, :]
    strict = idx[:, None] > idx[None, :]
    decay = jnp.exp(jnp.where(causal, g[..., :, None] - g[..., None, :], -jnp.inf))
    k_beta = k * beta[..., None]
    v_beta = v * beta[..., None]
    kkt = jnp.einsum('bhncd,bhnsd->bhncs', k_beta, k) * decay
    a_mat = jnp.where(strict, kkt, 0.0) + jnp.eye(CHUNK, dtype=q.dtype)
    rhs = jnp.concatenate([v_beta, k_beta * jnp.exp(g)[..., None]], axis=-1)
    sol = lax.linalg.triangular_solve(a_mat, rhs, left_side=True, lower=True,
                                      unit_diagonal=True)
    value, k_cumdecay = sol[..., :dv], sol[..., dv:]
    qk = jnp.einsum('bhncd,bhnsd->bhncs', q, k) * decay
    q_decay = q * jnp.exp(g)[..., None]
    k_tail = k * jnp.exp(g[..., -1:] - g)[..., None]
    g_last = jnp.exp(g[..., -1])

    def chunk_step(state, inp):
        qk_i, qd_i, kc_i, val_i, kt_i, gl_i = inp
        v_new = val_i - jnp.einsum('bhcd,bhde->bhce', kc_i, state)
        o_i = (jnp.einsum('bhcd,bhde->bhce', qd_i, state)
               + jnp.einsum('bhcs,bhse->bhce', qk_i, v_new))
        state = state * gl_i[..., None, None] + jnp.einsum('bhcd,bhce->bhde', kt_i, v_new)
        return state, o_i

    xs = tuple(jnp.moveaxis(t, 2, 0) for t in (qk, q_decay, k_cumdecay, value, k_tail, g_last))
    state0 = jnp.zeros((bsz, nh, dk, dv), q.dtype)
    _, o = lax.scan(chunk_step, state0, xs)
    return jnp.moveaxis(o, 0, 2).reshape(bsz, nh, seq, dv)

def gdn_mixer(qkv, z, a_gate, b_gate, conv_w, a_log, dt_bias, gdn_norm_g):
    f32 = jnp.float32
    bsz, seq, _ = qkv.shape
    qkv = jax.nn.silu(causal_depthwise_conv(qkv, conv_w)).astype(f32)
    q, k, v = jnp.split(qkv, 3, axis=-1)

    def heads(t):
        return t.reshape(bsz, seq, N_GDN_HEADS, GDN_HEAD_DIM).transpose(0, 2, 1, 3)

    q = l2norm(heads(q)) * (GDN_HEAD_DIM ** -0.5)
    k = l2norm(heads(k))
    v = heads(v)
    beta = jax.nn.sigmoid(b_gate.astype(f32)).transpose(0, 2, 1)
    g = (-jnp.exp(a_log.astype(f32))
         * jax.nn.softplus(a_gate.astype(f32) + dt_bias.astype(f32))).transpose(0, 2, 1)
    o = gated_delta_rule(q, k, v, g, beta).transpose(0, 2, 1, 3)
    zh = z.astype(f32).reshape(bsz, seq, N_GDN_HEADS, GDN_HEAD_DIM)
    o = rmsnorm(o, gdn_norm_g) * jax.nn.silu(zh)
    return o.reshape(bsz, seq, D_GDN).astype(z.dtype)

def hybrid_mixer(h, w_in, lam_re, lam_im, log_step, s5_b_re, s5_b_im, s5_c_re, s5_c_im,
                 s5_d, w_glu, b_glu, conv_w, a_log, dt_bias, gdn_norm_g, w_out):
    proj = h @ w_in
    splits = [D_S5, D_S5 + 3 * D_GDN, D_S5 + 4 * D_GDN, D_S5 + 4 * D_GDN + N_GDN_HEADS]
    u_s5, qkv, z, a_gate, b_gate = jnp.split(proj, splits, axis=-1)
    y_s5 = s5_mixer(u_s5, lam_re, lam_im, log_step, s5_b_re, s5_b_im, s5_c_re, s5_c_im,
                    s5_d, w_glu, b_glu)
    y_gdn = gdn_mixer(qkv, z, a_gate, b_gate, conv_w, a_log, dt_bias, gdn_norm_g)
    return jnp.concatenate([y_s5, y_gdn], axis=-1) @ w_out

def hier_moe(h, w_router_grp, w_router_exp, w_gate, w_up, w_down):
    f32 = jnp.float32
    bsz, seq, d = h.shape
    hf = h.reshape(bsz * seq, d)
    grp_logits = (hf @ w_router_grp).astype(f32)
    grp_prob = jax.nn.softmax(grp_logits, axis=-1)
    grp_idx = jnp.argmax(grp_logits, axis=-1)
    grp_onehot = jax.nn.one_hot(grp_idx, N_EXPERT_GROUPS, dtype=f32)
    p_grp = jnp.sum(grp_prob * grp_onehot, axis=-1)
    exp_logits = (hf @ w_router_exp).astype(f32).reshape(-1, N_EXPERT_GROUPS, EXPERTS_PER_GROUP)
    sel_logits = jnp.einsum('tg,tge->te', grp_onehot, exp_logits)
    top_val, top_idx = lax.top_k(sel_logits, TOP_K_IN_GROUP)
    w_k = jax.nn.softmax(top_val, axis=-1) * p_grp[:, None]
    expert_id = grp_idx[:, None] * EXPERTS_PER_GROUP + top_idx
    combine = jnp.einsum('tk,tke->te', w_k,
                         jax.nn.one_hot(expert_id, N_EXPERTS, dtype=f32)).astype(h.dtype)

    def expert_step(acc, ws):
        wg, wu, wd, gate_col = ws
        y = (jax.nn.silu(hf @ wg) * (hf @ wu)) @ wd
        return acc + gate_col[:, None] * y, None

    acc0 = jnp.zeros_like(hf)
    out, _ = lax.scan(expert_step, acc0, (w_gate, w_up, w_down, combine.T))
    return out.reshape(bsz, seq, d)

def first_inputs(seed: int = 0) -> dict:
    key = jax.random.key(seed)
    ks = jax.random.split(key, 32)
    f32 = jnp.float32

    def nrm(k, shape, scale):
        return jax.random.normal(k, shape, f32) * scale

    nl = DEPTH
    gp = (nl, N_S5_GROUPS, S5_STATE)
    n_idx = jnp.arange(S5_STATE, dtype=f32)
    dt_init = jnp.exp(jax.random.uniform(ks[21], (nl, N_GDN_HEADS), f32,
                                         math.log(1e-3), math.log(1e-1)))
    return {
        'x': nrm(ks[0], (BATCH, SEQ, D_MODEL), 1.0),
        'c': nrm(ks[1], (BATCH, D_MODEL), 1.0),
        'norm1_g': 1.0 + nrm(ks[2], (nl, D_MODEL), 0.02),
        'norm2_g': 1.0 + nrm(ks[3], (nl, D_MODEL), 0.02),
        'w_ada': nrm(ks[4], (nl, D_MODEL, N_MOD * D_MODEL), 0.5 * D_MODEL ** -0.5),
        'b_ada': nrm(ks[5], (nl, N_MOD * D_MODEL), 0.02),
        'w_in': nrm(ks[6], (nl, D_MODEL, D_IN), D_MODEL ** -0.5),
        'lam_re': -0.5 + nrm(ks[7], gp, 0.01),
        'lam_im': math.pi * n_idx + nrm(ks[8], gp, 0.01),
        'log_step': jax.random.uniform(ks[9], (nl, N_S5_GROUPS), f32,
                                       math.log(1e-3), math.log(1e-1)),
        's5_b_re': nrm(ks[10], (nl, N_S5_GROUPS, S5_STATE, S5_GROUP), (2 * S5_GROUP) ** -0.5),
        's5_b_im': nrm(ks[11], (nl, N_S5_GROUPS, S5_STATE, S5_GROUP), (2 * S5_GROUP) ** -0.5),
        's5_c_re': nrm(ks[12], (nl, N_S5_GROUPS, S5_GROUP, S5_STATE), S5_STATE ** -0.5),
        's5_c_im': nrm(ks[13], (nl, N_S5_GROUPS, S5_GROUP, S5_STATE), S5_STATE ** -0.5),
        's5_d': nrm(ks[14], (nl, D_S5), 0.5),
        'w_glu': nrm(ks[15], (nl, D_S5, D_S5), D_S5 ** -0.5),
        'b_glu': nrm(ks[16], (nl, D_S5), 0.02),
        'conv_w': nrm(ks[17], (nl, CONV_WIDTH, 3 * D_GDN), CONV_WIDTH ** -0.5),
        'a_log': jnp.log(jax.random.uniform(ks[18], (nl, N_GDN_HEADS), f32, 1.0, 16.0)),
        'dt_bias': dt_init + jnp.log(-jnp.expm1(-dt_init)),
        'gdn_norm_g': 1.0 + nrm(ks[19], (nl, GDN_HEAD_DIM), 0.02),
        'w_out': nrm(ks[20], (nl, D_MIX, D_MODEL), D_MIX ** -0.5),
        'w_router_grp': nrm(ks[22], (nl, D_MODEL, N_EXPERT_GROUPS), D_MODEL ** -0.5),
        'w_router_exp': nrm(ks[23], (nl, D_MODEL, N_EXPERTS), D_MODEL ** -0.5),
        'w_gate': nrm(ks[24], (nl, N_EXPERTS, D_MODEL, D_EXPERT), D_MODEL ** -0.5),
        'w_up': nrm(ks[25], (nl, N_EXPERTS, D_MODEL, D_EXPERT), D_MODEL ** -0.5),
        'w_down': nrm(ks[26], (nl, N_EXPERTS, D_EXPERT, D_MODEL), D_EXPERT ** -0.5),
        'normf_g': 1.0 + nrm(ks[27], (D_MODEL,), 0.02),
    }

def first_block(x, c, norm1_g, norm2_g, w_ada, b_ada, w_in, lam_re, lam_im, log_step,
              s5_b_re, s5_b_im, s5_c_re, s5_c_im, s5_d, w_glu, b_glu, conv_w, a_log,
              dt_bias, gdn_norm_g, w_out, w_router_grp, w_router_exp, w_gate, w_up,
              w_down, normf_g):
    h = x
    c_act = jax.nn.silu(c)
    for l in range(DEPTH):
        mod = c_act @ w_ada[l] + b_ada[l]
        sh1, sc1, gt1, sh2, sc2, gt2 = jnp.split(mod, N_MOD, axis=-1)
        a_in = modulate(rmsnorm(h, norm1_g[l]), sh1, sc1)
        mix = hybrid_mixer(a_in, w_in[l], lam_re[l], lam_im[l], log_step[l], s5_b_re[l],
                           s5_b_im[l], s5_c_re[l], s5_c_im[l], s5_d[l], w_glu[l], b_glu[l],
                           conv_w[l], a_log[l], dt_bias[l], gdn_norm_g[l], w_out[l])
        h = h + gt1[:, None, :] * mix
        m_in = modulate(rmsnorm(h, norm2_g[l]), sh2, sc2)
        moe = hier_moe(m_in, w_router_grp[l], w_router_exp[l], w_gate[l], w_up[l], w_down[l])
        h = h + gt2[:, None, :] * moe
    return rmsnorm(h, normf_g)


DEPTH_2 = 2

N_META = 16
BLOCK = 128
PAD = BLOCK - N_META

D_RNN = D_MODEL
LRU_BLOCKS = 8
LRU_BS = D_RNN // LRU_BLOCKS
LRU_C = 8.0
CONV_A = 4

N_Q_HEADS = 16
N_KV_HEADS = 2
HEAD_DIM = 64
Q_PER_KV = N_Q_HEADS // N_KV_HEADS
WINDOW = 128
Q_DIM = N_Q_HEADS * HEAD_DIM
KV_DIM = N_KV_HEADS * HEAD_DIM

EVEN_IN = 2 * D_RNN + Q_DIM + 2 * KV_DIM
EVEN_MIX = D_RNN + Q_DIM

D_SSM = 2 * D_MODEL
SSD_HEADDIM = 64
SSD_HEADS = D_SSM // SSD_HEADDIM
SSD_GROUPS = 8
SSD_HPG = SSD_HEADS // SSD_GROUPS
SSD_STATE = 128
CONV_C = 4
SSD_CONV_DIM = D_SSM + 2 * SSD_GROUPS * SSD_STATE
ODD_IN = D_SSM + SSD_CONV_DIM + SSD_HEADS

D_FF = 2816
CONV_F = 3


def rms_norm(x, w):
    x32 = x.astype(jnp.float32)
    y = x32 * lax.rsqrt(jnp.mean(x32 * x32, axis=-1, keepdims=True) + EPS)
    return (y * w.astype(jnp.float32)).astype(x.dtype)

def causal_dwconv(x, w, b):
    k = w.shape[0]
    y = lax.conv_general_dilated(
        x, w[:, None, :].astype(x.dtype), window_strides=(1,), padding=[(k - 1, 0)],
        dimension_numbers=("NWC", "WIO", "NWC"), feature_group_count=x.shape[-1])
    return y + b.astype(x.dtype)

def alibi_slopes(n_heads):
    return 2.0 ** (-8.0 * jnp.arange(1, n_heads + 1, dtype=jnp.float32) / n_heads)

def rg_lru(x, w_a, b_a, w_x, b_x, lam):
    bsz, L, _ = x.shape
    x32 = x.astype(jnp.float32)
    xb = x32.reshape(bsz, L, LRU_BLOCKS, LRU_BS)
    r = jax.nn.sigmoid(jnp.einsum("blni,nij->blnj", xb, w_a.astype(jnp.float32)).reshape(bsz, L, D_RNN) + b_a)
    i = jax.nn.sigmoid(jnp.einsum("blni,nij->blnj", xb, w_x.astype(jnp.float32)).reshape(bsz, L, D_RNN) + b_x)
    log_a = -LRU_C * r * jax.nn.softplus(-lam.astype(jnp.float32))
    a = jnp.exp(log_a)
    u = jnp.sqrt(-jnp.expm1(2.0 * log_a)) * (i * x32)

    def combine(c1, c2):
        a1, b1 = c1
        a2, b2 = c2
        return a1 * a2, a2 * b1 + b2

    _, h = lax.associative_scan(combine, (a, u), axis=1)
    return h.astype(x.dtype)

def swa_sink_alibi(q, k, v, sinks):
    bsz, L = q.shape[:2]
    Lp = L + PAD
    nblk = Lp // BLOCK
    q = q.astype(jnp.float32)
    k = k.astype(jnp.float32)
    v = v.astype(jnp.float32)
    padw = ((0, 0), (PAD, 0), (0, 0), (0, 0))
    qb = jnp.pad(q, padw).reshape(bsz, nblk, BLOCK, N_KV_HEADS, Q_PER_KV, HEAD_DIM)
    kb = jnp.pad(k, padw).reshape(bsz, nblk, BLOCK, N_KV_HEADS, HEAD_DIM)
    vb = jnp.pad(v, padw).reshape(bsz, nblk, BLOCK, N_KV_HEADS, HEAD_DIM)
    shift = ((0, 0), (1, 0), (0, 0), (0, 0), (0, 0))
    k_band = jnp.concatenate([jnp.pad(kb, shift)[:, :-1], kb], axis=2)
    v_band = jnp.concatenate([jnp.pad(vb, shift)[:, :-1], vb], axis=2)
    k_meta = k[:, :N_META]
    v_meta = v[:, :N_META]
    scale = HEAD_DIM ** -0.5
    s_band = jnp.einsum("bnqkgd,bnskd->bnkgqs", qb, k_band) * scale
    s_meta = jnp.einsum("bnqkgd,bmkd->bnkgqm", qb, k_meta) * scale

    blk = jnp.arange(nblk)
    t = blk[:, None] * BLOCK + jnp.arange(BLOCK)[None, :] - PAD
    s = (blk[:, None] - 1) * BLOCK + jnp.arange(2 * BLOCK)[None, :] - PAD
    dist_band = t[:, :, None] - s[:, None, :]
    band_ok = (s[:, None, :] >= N_META) & (dist_band >= 0) & (dist_band < WINDOW)
    dist_meta = t[:, :, None] - jnp.arange(N_META)[None, None, :]
    meta_ok = dist_meta >= 0

    slopes = alibi_slopes(N_Q_HEADS).reshape(N_KV_HEADS, Q_PER_KV)[:, :, None, None]
    pen_band = slopes * dist_band[:, None, None].astype(jnp.float32)
    pen_meta = slopes * jnp.minimum(dist_meta, WINDOW)[:, None, None].astype(jnp.float32)
    s_band = jnp.where(band_ok[:, None, None], s_band - pen_band, -jnp.inf)
    s_meta = jnp.where(meta_ok[:, None, None], s_meta - pen_meta, -jnp.inf)

    sink = sinks.astype(jnp.float32).reshape(N_KV_HEADS, Q_PER_KV)[:, :, None, None]
    mx = jnp.maximum(jnp.maximum(s_band.max(-1, keepdims=True), s_meta.max(-1, keepdims=True)), sink)
    p_band = jnp.exp(s_band - mx)
    p_meta = jnp.exp(s_meta - mx)
    denom = p_band.sum(-1, keepdims=True) + p_meta.sum(-1, keepdims=True) + jnp.exp(sink - mx)
    p_band = p_band / denom
    p_meta = p_meta / denom
    o = (jnp.einsum("bnkgqs,bnskd->bnqkgd", p_band, v_band)
         + jnp.einsum("bnkgqm,bmkd->bnqkgd", p_meta, v_meta))
    return o.reshape(bsz, Lp, Q_DIM)[:, PAD:]

def griffin_swa_mixer(u, w_in, conv_w, conv_b, w_a, b_a, w_x, b_x, lam, sinks, w_out):
    bsz, L, _ = u.shape
    proj = u @ w_in
    gate, xr, q, k, v = jnp.split(
        proj, [D_RNN, 2 * D_RNN, 2 * D_RNN + Q_DIM, 2 * D_RNN + Q_DIM + KV_DIM], axis=-1)
    xr = causal_dwconv(xr, conv_w, conv_b)
    y_a = jax.nn.gelu(gate, approximate=True) * rg_lru(xr, w_a, b_a, w_x, b_x, lam)
    y_b = swa_sink_alibi(q.reshape(bsz, L, N_Q_HEADS, HEAD_DIM),
                         k.reshape(bsz, L, N_KV_HEADS, HEAD_DIM),
                         v.reshape(bsz, L, N_KV_HEADS, HEAD_DIM), sinks).astype(u.dtype)
    return jnp.concatenate([y_a, y_b], axis=-1) @ w_out

def ssd_chunked(x, dt, a, b_in, c_in):
    bsz, Lp = x.shape[:2]
    nc = Lp // BLOCK
    x = x.reshape(bsz, nc, BLOCK, SSD_GROUPS, SSD_HPG, SSD_HEADDIM)
    dt = dt.reshape(bsz, nc, BLOCK, SSD_GROUPS, SSD_HPG)
    bc = b_in.reshape(bsz, nc, BLOCK, SSD_GROUPS, SSD_STATE)
    cc = c_in.reshape(bsz, nc, BLOCK, SSD_GROUPS, SSD_STATE)
    cs = jnp.cumsum(dt * a.reshape(SSD_GROUPS, SSD_HPG), axis=2)
    xdt = x * dt[..., None]
    cs_t = jnp.moveaxis(cs, 2, -1)
    seg = cs_t[..., :, None] - cs_t[..., None, :]
    tril = jnp.tril(jnp.ones((BLOCK, BLOCK), dtype=bool))
    decay_in = jnp.exp(jnp.where(tril, seg, -jnp.inf))
    cb = jnp.einsum("bclgn,bcsgn->bcgls", cc, bc)
    y_diag = jnp.einsum("bcgls,bcghls,bcsghp->bclghp", cb, decay_in, xdt)
    cs_last = cs[:, :, -1:]
    chunk_states = jnp.einsum("bclgn,bclgh,bclghp->bcghpn", bc, jnp.exp(cs_last - cs), xdt)
    chunk_decay = jnp.exp(cs_last[:, :, 0])

    def step(state, inp):
        dec, st = inp
        return state * dec[..., None, None] + st, state

    init = jnp.zeros_like(chunk_states[:, 0])
    _, prev = lax.scan(step, init, (jnp.moveaxis(chunk_decay, 1, 0), jnp.moveaxis(chunk_states, 1, 0)))
    prev = jnp.moveaxis(prev, 0, 1)
    y_off = jnp.einsum("bclgn,bcghpn,bclgh->bclghp", cc, prev, jnp.exp(cs))
    return (y_diag + y_off).reshape(bsz, Lp, SSD_HEADS, SSD_HEADDIM)

def mamba2_mixer(u, w_in, conv_w, conv_b, dt_bias, a_log, d_skip, gate_norm, w_out):
    bsz, L, _ = u.shape
    proj = u @ w_in
    z, xbc, dt = jnp.split(proj, [D_SSM, D_SSM + SSD_CONV_DIM], axis=-1)
    xbc = jax.nn.silu(causal_dwconv(xbc, conv_w, conv_b))
    xs, bs, cs = jnp.split(xbc, [D_SSM, D_SSM + SSD_GROUPS * SSD_STATE], axis=-1)
    xs = xs.reshape(bsz, L, SSD_HEADS, SSD_HEADDIM).astype(jnp.float32)
    bs = bs.reshape(bsz, L, SSD_GROUPS, SSD_STATE).astype(jnp.float32)
    cs = cs.reshape(bsz, L, SSD_GROUPS, SSD_STATE).astype(jnp.float32)
    dt = jax.nn.softplus(dt.astype(jnp.float32) + dt_bias.astype(jnp.float32))
    a = -jnp.exp(a_log.astype(jnp.float32))

    def front_pad(t):
        return jnp.pad(t, ((0, 0), (PAD, 0)) + ((0, 0),) * (t.ndim - 2))

    y = ssd_chunked(front_pad(xs), front_pad(dt), a, front_pad(bs), front_pad(cs))[:, PAD:]
    y = y + d_skip.astype(jnp.float32)[:, None] * xs
    y = y.reshape(bsz, L, D_SSM) * jax.nn.silu(z.astype(jnp.float32))
    yg = y.reshape(bsz, L, SSD_GROUPS, D_SSM // SSD_GROUPS)
    yg = yg * lax.rsqrt(jnp.mean(yg * yg, axis=-1, keepdims=True) + EPS)
    y = yg.reshape(bsz, L, D_SSM) * gate_norm.astype(jnp.float32)
    return y.astype(u.dtype) @ w_out

def conv_ffn(u, w_up, conv_w, conv_b, w_down):
    h = causal_dwconv(u @ w_up, conv_w, conv_b)
    g, up = jnp.split(h, 2, axis=-1)
    return (jax.nn.gelu(g, approximate=True) * up) @ w_down

def second_inputs(seed: int = 0) -> dict:
    key = jax.random.key(seed)
    k = jax.random.split(key, 36)

    def normal(kk, shape, scale):
        return jax.random.normal(kk, shape, jnp.float32) * scale

    def gain(kk, n):
        return 1.0 + 0.05 * jax.random.normal(kk, (n,), jnp.float32)

    u = jax.random.uniform(k[11], (D_RNN,), jnp.float32, 0.9, 0.999)
    a0 = u ** (1.0 / LRU_C)
    lru_lambda = jnp.log(a0) - jnp.log1p(-a0)
    dt0 = jnp.exp(jax.random.uniform(k[25], (SSD_HEADS,), jnp.float32, math.log(1e-3), math.log(1e-1)))
    dt_bias = dt0 + jnp.log(-jnp.expm1(-dt0))
    a_log = jnp.log(jax.random.uniform(k[26], (SSD_HEADS,), jnp.float32, 1.0, 16.0))

    return {
        "x": normal(k[0], (BATCH, SEQ, D_MODEL), 1.0),
        "meta_tokens": normal(k[1], (N_META, D_MODEL), 1.0),
        "l0_mix_pre_norm": gain(k[2], D_MODEL),
        "l0_mix_post_norm": gain(k[3], D_MODEL),
        "l0_w_in": normal(k[4], (D_MODEL, EVEN_IN), D_MODEL ** -0.5),
        "l0_lru_conv_w": normal(k[5], (CONV_A, D_RNN), CONV_A ** -0.5),
        "l0_lru_conv_b": normal(k[6], (D_RNN,), 0.01),
        "l0_lru_w_a": normal(k[7], (LRU_BLOCKS, LRU_BS, LRU_BS), LRU_BS ** -0.5),
        "l0_lru_b_a": normal(k[8], (D_RNN,), 0.01),
        "l0_lru_w_x": normal(k[9], (LRU_BLOCKS, LRU_BS, LRU_BS), LRU_BS ** -0.5),
        "l0_lru_b_x": normal(k[10], (D_RNN,), 0.01),
        "l0_lru_lambda": lru_lambda,
        "l0_attn_sinks": normal(k[12], (N_Q_HEADS,), 0.5),
        "l0_w_out": normal(k[13], (EVEN_MIX, D_MODEL), EVEN_MIX ** -0.5),
        "l0_ffn_pre_norm": gain(k[14], D_MODEL),
        "l0_ffn_post_norm": gain(k[15], D_MODEL),
        "l0_ffn_w_up": normal(k[16], (D_MODEL, 2 * D_FF), D_MODEL ** -0.5),
        "l0_ffn_conv_w": normal(k[17], (CONV_F, 2 * D_FF), CONV_F ** -0.5),
        "l0_ffn_conv_b": normal(k[18], (2 * D_FF,), 0.01),
        "l0_ffn_w_down": normal(k[19], (D_FF, D_MODEL), D_FF ** -0.5),
        "l1_mix_pre_norm": gain(k[20], D_MODEL),
        "l1_mix_post_norm": gain(k[21], D_MODEL),
        "l1_w_in": normal(k[22], (D_MODEL, ODD_IN), D_MODEL ** -0.5),
        "l1_ssm_conv_w": normal(k[23], (CONV_C, SSD_CONV_DIM), CONV_C ** -0.5),
        "l1_ssm_conv_b": normal(k[24], (SSD_CONV_DIM,), 0.01),
        "l1_dt_bias": dt_bias,
        "l1_a_log": a_log,
        "l1_d_skip": 1.0 + 0.1 * jax.random.normal(k[27], (SSD_HEADS,), jnp.float32),
        "l1_gate_norm": gain(k[28], D_SSM),
        "l1_w_out": normal(k[29], (D_SSM, D_MODEL), D_SSM ** -0.5),
        "l1_ffn_pre_norm": gain(k[30], D_MODEL),
        "l1_ffn_post_norm": gain(k[31], D_MODEL),
        "l1_ffn_w_up": normal(k[32], (D_MODEL, 2 * D_FF), D_MODEL ** -0.5),
        "l1_ffn_conv_w": normal(k[33], (CONV_F, 2 * D_FF), CONV_F ** -0.5),
        "l1_ffn_conv_b": normal(k[34], (2 * D_FF,), 0.01),
        "l1_ffn_w_down": normal(k[35], (D_FF, D_MODEL), D_FF ** -0.5),
    }

def second_block(x, meta_tokens,
              l0_mix_pre_norm, l0_mix_post_norm, l0_w_in, l0_lru_conv_w, l0_lru_conv_b,
              l0_lru_w_a, l0_lru_b_a, l0_lru_w_x, l0_lru_b_x, l0_lru_lambda, l0_attn_sinks, l0_w_out,
              l0_ffn_pre_norm, l0_ffn_post_norm, l0_ffn_w_up, l0_ffn_conv_w, l0_ffn_conv_b, l0_ffn_w_down,
              l1_mix_pre_norm, l1_mix_post_norm, l1_w_in, l1_ssm_conv_w, l1_ssm_conv_b,
              l1_dt_bias, l1_a_log, l1_d_skip, l1_gate_norm, l1_w_out,
              l1_ffn_pre_norm, l1_ffn_post_norm, l1_ffn_w_up, l1_ffn_conv_w, l1_ffn_conv_b, l1_ffn_w_down):
    bsz = x.shape[0]
    meta = jnp.broadcast_to(meta_tokens.astype(x.dtype)[None], (bsz, N_META, D_MODEL))
    h = jnp.concatenate([meta, x], axis=1)
    layers = [
        (l0_mix_pre_norm, l0_mix_post_norm,
         (l0_w_in, l0_lru_conv_w, l0_lru_conv_b, l0_lru_w_a, l0_lru_b_a, l0_lru_w_x, l0_lru_b_x,
          l0_lru_lambda, l0_attn_sinks, l0_w_out),
         (l0_ffn_pre_norm, l0_ffn_post_norm, l0_ffn_w_up, l0_ffn_conv_w, l0_ffn_conv_b, l0_ffn_w_down)),
        (l1_mix_pre_norm, l1_mix_post_norm,
         (l1_w_in, l1_ssm_conv_w, l1_ssm_conv_b, l1_dt_bias, l1_a_log, l1_d_skip, l1_gate_norm, l1_w_out),
         (l1_ffn_pre_norm, l1_ffn_post_norm, l1_ffn_w_up, l1_ffn_conv_w, l1_ffn_conv_b, l1_ffn_w_down)),
    ]
    for i in range(DEPTH_2):
        pre, post, mix, ffn = layers[i]
        mixer = griffin_swa_mixer if i % 2 == 0 else mamba2_mixer
        h = h + rms_norm(mixer(rms_norm(h, pre), *mix), post)
        f_pre, f_post, w_up, c_w, c_b, w_down = ffn
        h = h + rms_norm(conv_ffn(rms_norm(h, f_pre), w_up, c_w, c_b, w_down), f_post)
    return h[:, N_META:]


def setup_inputs(seed=0):
    out = dict(first_inputs(seed))
    for name, value in second_inputs(seed + 1).items():
        if name != "x":
            out[name + "_2"] = value
    return out


def reference(
    x, c, norm1_g, norm2_g, w_ada, b_ada, w_in, lam_re, lam_im, log_step, s5_b_re, s5_b_im,
    s5_c_re, s5_c_im, s5_d, w_glu, b_glu, conv_w, a_log, dt_bias, gdn_norm_g, w_out,
    w_router_grp, w_router_exp, w_gate, w_up, w_down, normf_g, meta_tokens_2, l0_mix_pre_norm_2,
    l0_mix_post_norm_2, l0_w_in_2, l0_lru_conv_w_2, l0_lru_conv_b_2, l0_lru_w_a_2, l0_lru_b_a_2,
    l0_lru_w_x_2, l0_lru_b_x_2, l0_lru_lambda_2, l0_attn_sinks_2, l0_w_out_2, l0_ffn_pre_norm_2,
    l0_ffn_post_norm_2, l0_ffn_w_up_2, l0_ffn_conv_w_2, l0_ffn_conv_b_2, l0_ffn_w_down_2,
    l1_mix_pre_norm_2, l1_mix_post_norm_2, l1_w_in_2, l1_ssm_conv_w_2, l1_ssm_conv_b_2,
    l1_dt_bias_2, l1_a_log_2, l1_d_skip_2, l1_gate_norm_2, l1_w_out_2, l1_ffn_pre_norm_2,
    l1_ffn_post_norm_2, l1_ffn_w_up_2, l1_ffn_conv_w_2, l1_ffn_conv_b_2, l1_ffn_w_down_2,
):
    x = first_block(
        x, c, norm1_g, norm2_g, w_ada, b_ada, w_in, lam_re, lam_im, log_step, s5_b_re, s5_b_im,
        s5_c_re, s5_c_im, s5_d, w_glu, b_glu, conv_w, a_log, dt_bias, gdn_norm_g, w_out,
        w_router_grp, w_router_exp, w_gate, w_up, w_down, normf_g,
    )
    return second_block(
        x, meta_tokens_2, l0_mix_pre_norm_2, l0_mix_post_norm_2, l0_w_in_2, l0_lru_conv_w_2,
        l0_lru_conv_b_2, l0_lru_w_a_2, l0_lru_b_a_2, l0_lru_w_x_2, l0_lru_b_x_2,
        l0_lru_lambda_2, l0_attn_sinks_2, l0_w_out_2, l0_ffn_pre_norm_2, l0_ffn_post_norm_2,
        l0_ffn_w_up_2, l0_ffn_conv_w_2, l0_ffn_conv_b_2, l0_ffn_w_down_2, l1_mix_pre_norm_2,
        l1_mix_post_norm_2, l1_w_in_2, l1_ssm_conv_w_2, l1_ssm_conv_b_2, l1_dt_bias_2,
        l1_a_log_2, l1_d_skip_2, l1_gate_norm_2, l1_w_out_2, l1_ffn_pre_norm_2,
        l1_ffn_post_norm_2, l1_ffn_w_up_2, l1_ffn_conv_w_2, l1_ffn_conv_b_2, l1_ffn_w_down_2,
    )


_drawn_inputs = setup_inputs


def setup_inputs(seed=0):
    import zlib

    import numpy as np

    out = dict(_drawn_inputs(seed))
    spreads = {}
    factors = {'norm1_g': 3.403,
     'lam_re': 64.0,
     'log_step': 101.464,
     's5_b_re': 158.568,
     's5_b_im': 150.832,
     's5_c_re': 167.456,
     's5_c_im': 157.536,
     'w_glu': 2.837,
     'b_glu': 64.0,
     'gdn_norm_g': 3.889,
     'l0_lru_b_a_2': 33.578,
     'l0_lru_b_x_2': 8.0,
     'l0_ffn_conv_b_2': 5.375,
     'l1_ssm_conv_b_2': 7.726,
     'l1_ffn_conv_b_2': 8.0,
     'norm2_g': 6.214,
     'lam_im': 35.304}
    for name, (base, spread) in spreads.items():
        noise = np.random.default_rng([zlib.crc32(name.encode()), seed]).standard_normal(out[name].shape)
        drawn = base * np.exp(spread * noise) if base else spread * noise
        out[name] = jnp.asarray(drawn.astype(out[name].dtype))
    for name, factor in factors.items():
        out[name] = (out[name] * factor).astype(out[name].dtype)
    return out
```

```python
from contextlib import ExitStack

import numpy as np

import concourse.bass as bass
from concourse import mybir

F32 = mybir.dt.float32
I32 = mybir.dt.int32
U32 = mybir.dt.uint32
ALU = mybir.AluOpType
ACT = mybir.ActivationFunctionType
AX = mybir.AxisListType.X

P = 128
WORK = 29990
D = 1024
DT = D // P
SEQ = 512
META = 16
T2 = SEQ + META
HALF = T2 // 2
EPS = 1e-6

NS5 = 4
S5_TILES = 16
HEADS = 4
CHUNKS = SEQ // P
LEVELS = 7
EXPERTS = 32
GROUPS = 4
D_EXPERT = 256
FREE = 1
BLOCKS = 40

CONV_C = 4
CONV_F = 3
LRU = 8
Q_HEADS = 16
HEAD = 64
Q_TILES = Q_HEADS * HEAD // P
FF = 2816 // P
SSD_X = 16
SSD_G = 8
SSD_H = 32
CH2 = [(0, META)] + [(META + P * i, P) for i in range(4)]

WSLOTS = 4
UNIT = 16 * P
_two = lambda u: 2 * (u + 1)
_one = lambda u: u + 1
STAGES = [("ada", 24, 48, _two), ("in1", 10, 20, _two), ("glu", 1, 4, lambda u: 4), ("out1", 4, 8, _two),
          ("in0", 14, 27, lambda u: min(2 * (u + 1), 27)), ("out0", 8, 8, _one),
          ("up0", 22, 44, _two), ("down0", 16, 8, lambda u: u // 2 + 1),
          ("in2", 24, 48, _two), ("out2", 8, 8, _one),
          ("up2", 22, 44, _two), ("down2", 16, 8, lambda u: u // 2 + 1)]
U0, Q0, ENDED = {}, {}, []
for _name, _units, _tiles, _ended in STAGES:
    U0[_name], Q0[_name] = len(ENDED), (max(ENDED) if ENDED else 0)
    ENDED += [Q0[_name] + _ended(_u) for _u in range(_units)]
UNITS = len(ENDED)
DOWN_K = FF // 2

SQ0 = [0] + [20 + DT * n for n in range(10)]

PARAMS = [("c", 8), ("b_ada", 48), ("norm1_g", 8), ("norm2_g", 8), ("normf_g", 8), ("s5_d", 4), ("b_glu", 4),
          ("conv_w", 48), ("gdn_norm_g", 1), ("lam_re", 16), ("lam_im", 16), ("log_step", 16),
          ("a_log", 4), ("dt_bias", 4),
          ("pre0", 8), ("post0", 8), ("lru_w", 32), ("lru_b", 8), ("b_a", 8), ("b_x", 8), ("lam", 8),
          ("fpre0", 8), ("fpost0", 8), ("fw0", 132), ("fb0", 44), ("sinks", 16),
          ("pre2", 8), ("post2", 8), ("ssm_w", 128), ("ssm_b", 32), ("gate_norm", 16), ("d_skip", 16),
          ("dt_bias2", 32), ("a_log2", 32), ("fpre2", 8), ("fpost2", 8), ("fw2", 132), ("fb2", 44)]
PCOL, _n = {}, 0
for _name, _w in PARAMS:
    PCOL[_name] = _n
    _n += _w
NPAR = _n
CONSTS = [("ident", P), ("ones", P), ("upto", P), ("levels", LEVELS * P), ("dist1", META + P), ("dist2", META + 2 * P),
          ("dist0", META), ("strict", P), ("grp_rank", GROUPS), ("exp_rank", EXPERTS), ("row", 1), ("eps", 1), ("ln", 1)]
CCOL, _n = {}, 0
for _name, _w in CONSTS:
    CCOL[_name] = _n
    _n += _w
NCON = _n
FAR = 1e30


def shape_constants():
    out = np.zeros((P, NCON), np.float32)

    def put(name, a):
        out[:, CCOL[name]:CCOL[name] + a.shape[-1]] = a

    i, j = np.arange(P)[:, None], np.arange(P)[None, :]
    put("ident", (i == j).astype(np.float32))
    put("ones", np.ones((P, P), np.float32))
    put("upto", (i <= j).astype(np.float32))
    put("strict", (i < j).astype(np.float32))
    for v in range(LEVELS):
        b = 1 << v
        put_at = (i // (2 * b) == j // (2 * b)) & (j % (2 * b) >= b) & (i % (2 * b) < b)
        out[:, CCOL["levels"] + v * P:CCOL["levels"] + (v + 1) * P] = put_at
    m, band = np.arange(META)[None, :], np.arange(2 * P)[None, :]
    far = lambda ok, dist: np.where(ok, dist, FAR).astype(np.float32)
    put("dist0", np.concatenate([far(i >= m, i - m)], 1))
    own = far(i >= j, i - j)
    put("dist1", np.concatenate([np.minimum(META + i - m, P).astype(np.float32), own], 1))
    dist = i + P - band
    put("dist2", np.concatenate([np.full((P, META), float(P), np.float32), far((dist >= 0) & (dist < P), dist)], 1))
    put("grp_rank", np.broadcast_to(GROUPS - np.arange(GROUPS, dtype=np.float32), (P, GROUPS)))
    put("exp_rank", np.broadcast_to(EXPERTS - np.arange(EXPERTS, dtype=np.float32), (P, EXPERTS)))
    put("row", i.astype(np.float32))
    put("eps", np.full((P, 1), EPS, np.float32))
    return out


def program(nc, a):
    with ExitStack() as ctx:
        def sb(name, *shape, dt=F32):
            return ctx.enter_context(nc.sbuf_tensor(name, [P, *shape], dt))

        sems = {}

        def sem(name):
            if name not in sems:
                sems[name] = ctx.enter_context(nc.semaphore(name))
            return sems[name]

        h = sb("h", DT, T2)
        u = sb("u", DT, T2)
        ring = sb("ring", WSLOTS, UNIT)
        par = sb("par", NPAR)
        con = sb("con", NCON)
        sq = sb("sq", 2, T2)
        rs = sb("rs", T2)
        tmp = sb("tmp", 2, T2 + 4)
        mod = sb("mod", 48)
        modg = sb("modg", 2 * DT)
        cact = sb("cact", DT)
        work = sb("work", WORK)
        ps = ctx.enter_context(nc.psum_tensor("ps", [P, 8, 512], F32))

        def at(off, *shape):
            n = int(np.prod(shape))
            v = work[:, off:off + n]
            if len(shape) == 1:
                return v
            names = " ".join(f"d{i}" for i in range(len(shape)))
            return v.rearrange(f"p ({names}) -> p {names}", **{f"d{i}": s for i, s in enumerate(shape)})

        def pcol(name, i=0, n=1):
            return par[:, PCOL[name] + i:PCOL[name] + i + n]

        def ccol(name, i=0, n=1):
            return con[:, CCOL[name] + i:CCOL[name] + i + n]

        ident, ones, upto, eps = ccol("ident", 0, P), ccol("ones", 0, P), ccol("upto", 0, P), ccol("eps")

        def pair(q, half=0, n=512):
            return ps[:, 2 * (q % 2) + half, 0:n]

        def pair2(q):
            return ps[:, 2 * (q % 2):2 * (q % 2) + 2, 0:HALF]

        def halves(x):
            return x.rearrange("p (s n) -> p s n", s=2)

        mix = at(0, DT, SEQ)
        z1 = at(4096, HEADS, SEQ)
        qkv = at(6144, 12, SEQ)
        F1 = 12288
        us5 = at(F1, NS5, SEQ)
        y5 = at(F1 + 2048, NS5, SEQ)
        s5w = at(F1 + 4096, 2048)
        s5b = [at(F1 + 4096 + 512 * n, 4, P) for n in range(2)]
        s5c = [at(F1 + 4096 + 1024 + 512 * n, S5_TILES, 32) for n in range(2)]
        s5ck = [at(F1 + 6144 + 512 * n, S5_TILES, 32) for n in range(2)]
        fine = [at(F1 + 5120 + 512 * n, S5_TILES, 32) for n in range(2)]
        coarse = [at(F1 + 7168 + 256 * n, S5_TILES, 16) for n in range(2)]
        table = [[at(F1 + 7680 + 1024 * b + 512 * n, SEQ) for n in range(2)] for b in range(2)]
        tabt = [at(F1 + 9728 + 512 * n, SEQ) for n in range(2)]
        f5 = [at(F1 + 10752 + 512 * n, SEQ) for n in range(2)]
        z5 = [at(F1 + 11776 + 512 * n, SEQ) for n in range(2)]
        p5 = [at(F1 + 12800 + 512 * n, SEQ) for n in range(4)]
        st5 = [[at(F1 + 14848 + 1024 * b + 512 * n, SEQ) for n in range(2)] for b in range(2)]
        s5s = sb("s5s", 24, S5_TILES)
        sig = p5[0]
        cbuf = [tmp[:, b, 0:SEQ + 3] for b in range(2)]
        wgate = at(WORK - 64, DT, 8)
        beta, gate, csum, gtot, ecs, etail, egt, bcs, sp1, sp2, sp3, sp4 = [
            at(WORK - 64 - 16 * (n + 1), CHUNKS * HEADS) for n in range(12)]
        amat = at(F1, CHUNKS, HEADS, P)
        qk_d = at(F1 + 2048, CHUNKS, HEADS, P)
        q_dec = at(F1 + 4096, CHUNKS, HEADS, P)
        kb_g = at(F1 + 6144, CHUNKS, HEADS, P)
        k_tail = at(F1 + 8192, CHUNKS, HEADS, P)
        v_b = at(F1 + 10240, CHUNKS, HEADS, P)
        w_mat = at(F1 + 12288, CHUNKS, HEADS, P)
        a_lev = at(F1 + 14336, CHUNKS, HEADS, P)
        x_inv = at(6144, CHUNKS, HEADS, P)
        y_inv = at(8192, CHUNKS, HEADS, P)
        o_gdn = at(10240, HEADS, SEQ)
        val, kc = w_mat, a_lev
        state = at(F1 + 16384, HEADS, P)
        v_new = at(F1 + 16896, HEADS, P)
        dtmp = tmp[:, 0, 0:SEQ].rearrange("p (h n) -> p h n", h=HEADS)
        egb = tmp[:, 1, 0:SEQ].rearrange("p (h n) -> p h n", h=HEADS)
        l2r = at(F1, 8, SEQ)

        wrouter = sb("wrouter", DT, GROUPS + EXPERTS)
        zeros = at(10240, D)
        xtok = at(0, CHUNKS, D)
        mw = [at(4096 + 3 * UNIT * p, 3 * UNIT) for p in range(2)]
        xb = [at(16384 + D * p, D) for p in range(2)]
        xbt = [at(18432 + D * p, DT, P) for p in range(2)]
        yb = [at(20480 + D * p, D) for p in range(2)]
        silu_b = at(22528, 2, D_EXPERT)
        h_b = at(23040, 2, D_EXPERT)
        ht_b = at(23552, 2, P)
        R0 = 23808
        logit = at(R0, CHUNKS, GROUPS + EXPERTS)
        r32 = [at(R0 + 144 + 128 * n, CHUNKS, EXPERTS) for n in range(6)]
        r4 = [at(R0 + 912 + 16 * n, CHUNKS, GROUPS) for n in range(4)]
        r1 = [at(R0 + 976 + 4 * n, CHUNKS) for n in range(12)]
        e32 = [at(R0 + 1024 + 32 * n, EXPERTS) for n in range(6)]
        slots = at(R0 + 1216, 2 * CHUNKS)
        slot_id = at(R0 + 1224, 2 * CHUNKS).bitcast(U32)
        eid = at(R0 + 1232, P).bitcast(I32)
        ecol = at(R0 + 1360, 2)
        y1, y2, moe = at(4096, CHUNKS, D), at(8192, CHUNKS, D), at(12288, CHUNKS, D)
        rows_in = nc.dram_tensor("rows_in", (BLOCKS * P, D), F32).ap()
        rows_out = nc.dram_tensor("rows_out", (BLOCKS * P, D), F32).ap()

        wdt = sb("wdt", DT, SSD_H)
        mix0 = at(0, 2 * LRU, T2)
        q_fm = at(8448, Q_TILES, T2)
        k_fm = at(12672, 2, T2)
        v_fm = at(13728, T2)
        v_tok = at(14256, len(CH2), P)
        g_lru, x_lru, r_lru, i_lru, a_lru, t_lru = [at(14900 + 2 * T2 * n, 2, T2) for n in range(6)]
        w_lru = at(21300, 2, LRU, P)
        lam8 = sb("lam8", 4, LRU)
        prob = at(23360, 2, 2, META + 2 * P)
        prob_t = at(24448, 2, 2, 3 * P)
        stat = at(25984, 2, 8, 2)
        m_out = at(16900, DT, T2)
        prod = at(0, FF, T2)
        gact = at(21200, T2)
        uact = at(21800, T2)
        pad = [tmp[:, b, 0:T2 + 3] for b in range(2)]
        z2 = at(0, SSD_X, T2)
        xbc = at(8448, SSD_X + 2 * SSD_G, T2)
        st2 = at(25344, SSD_H, HEAD)
        T0 = 27392
        xdd = at(T0, 2, 4, HEAD)
        b_tok = at(T0 + 512, 2, P)
        cbm = at(T0 + 768, 2, P)
        dt2, da2, cs2, gt2_, tail2, egt2, sa2, sb2, sc2 = [at(T0 + 1024 + 160 * n, len(CH2), SSD_H) for n in range(9)]
        uf = u[:, :, :].rearrange("p k n -> p (k n)")
        at_u = lambda off, n: uf[:, off:off + n]
        decay2 = [at_u(512 * n, 512).rearrange("p (h n) -> p h n", h=4) for n in range(2)]
        eg2 = [at_u(1024 + 512 * n, 512).rearrange("p (h n) -> p h n", h=4) for n in range(2)]
        cdec = [at_u(2048 + 512 * n, 512).rearrange("p (h n) -> p h n", h=4) for n in range(2)]
        xdt = [at_u(3072 + 256 * n, 256).rearrange("p (h n) -> p h n", h=4) for n in range(2)]
        m2_out = at(16896, DT, T2)
        gsq = [sq[:, e, :] for e in range(2)]
        groot = [at_u(T2 * n, T2) for n in range(2)]

        block = ctx.enter_context(nc.Block())

        @block.sync
        def _(sp):
            def load_unit(n, slot, waits=True):
                if waits:
                    sp.wait_ge(sem("tile_done"), ENDED[n - WSLOTS])
                sp.dma_start(ring[:, slot, :], a["stream"][n]).then_inc(sem(f"unit_loaded{slot}"), 16)

            def stream_first(stage):
                n0, units = U0[stage], dict((s[0], s[1]) for s in STAGES)[stage]
                for n in range(n0, n0 + min(WSLOTS, units)):
                    load_unit(n, n % WSLOTS, n >= WSLOTS)

            def stream_rest(stage):
                n0, units = U0[stage] + WSLOTS, dict((s[0], s[1]) for s in STAGES)[stage] - WSLOTS
                trips = max(units, 0) // WSLOTS
                if trips > 1:
                    per = ENDED[n0] - ENDED[n0 - WSLOTS]
                    with sp.Fori(0, trips) as i:
                        for j in range(WSLOTS):
                            slot = (n0 + j) % WSLOTS
                            sp.wait_ge(sem("tile_done"), i * per + ENDED[n0 + j - WSLOTS])
                            sp.dma_start(ring[:, slot, :], a["stream"][i * WSLOTS + (n0 + j)]
                                         ).then_inc(sem(f"unit_loaded{slot}"), 16)
                else:
                    trips = 0
                for n in range(n0 + trips * WSLOTS, n0 + units):
                    load_unit(n, n % WSLOTS)

            sp.dma_start(par[:, :], a["params"]).then_inc(sem("inputs_loaded"), 16)
            sp.dma_start(con[:, :], a["consts"]).then_inc(sem("inputs_loaded"), 16)
            sp.dma_start(h[:, :, META:T2], a["x_fm"]).then_inc(sem("inputs_loaded"), 16)
            sp.dma_start(s5w, a["s5"]).then_inc(sem("inputs_loaded"), 16)
            sp.dma_start(wgate, a["w_gates"].rearrange("p (k n) -> p k n", k=DT)).then_inc(sem("inputs_loaded"), 16)
            sp.dma_start(wrouter[:, :, :], a["w_router"].rearrange("p (k n) -> p k n", k=DT)).then_inc(sem("inputs_loaded"), 16)
            sp.dma_start(h[:, :, 0:META], a["meta_fm"]).then_inc(sem("inputs_loaded"), 16)
            sp.dma_start(wdt[:, :, :], a["w_dt"].rearrange("p (k n) -> p k n", k=DT)).then_inc(sem("inputs_loaded"), 16)
            stream_first("ada")
            stream_rest("ada")
            sp.wait_ge(sem("zeros_ready"), 1)
            sp.dma_start(rows_in.rearrange("(b p) n -> p b n", p=P), zeros.unsqueeze(1).broadcast_to([P, BLOCKS, D])
                         ).then_inc(sem("rows_zeroed"), 16)
            for stage in ("in1", "glu", "out1"):
                stream_first(stage)
                stream_rest(stage)
            stream_first("in0")
            sp.wait_ge(sem("expert_ids"), 1)
            sp.wait_ge(sem("rows_scattered"), 16 * 8)

            def load_block(b, p, waits):
                expert = sp.value_load(eid[0:1, bass.ds(b, 1)], min_val=0, max_val=EXPERTS - 1)
                rows = a["experts"][bass.ds(expert * P, P), :]
                if waits:
                    sp.wait_ge(sem("xt_done"), b - 1)
                sp.dma_start(xb[p], rows_in[bass.ds(b * P, P), :]).then_inc(sem(f"rows_loaded{p}"), 16)
                if waits:
                    sp.wait_ge(sem("gu_done"), b - 1)
                sp.dma_start(mw[p][:, 0:2 * UNIT], rows[:, 0:2 * UNIT]).then_inc(sem(f"gu_loaded{p}"), 16)
                if waits:
                    sp.wait_ge(sem("dn_done"), FREE + b - 1)
                sp.dma_start(mw[p][:, 2 * UNIT:], rows[:, 2 * UNIT:]).then_inc(sem(f"dn_loaded{p}"), 16)

            load_block(0, 0, False)
            load_block(1, 1, False)
            with sp.Fori(1, BLOCKS // 2) as i:
                for p in range(2):
                    load_block(i * 2 + p, p, True)

            sp.wait_ge(sem("moe_added"), DT)
            sp.dma_start(w_lru, a["w_lru"].rearrange("p (m k n) -> p m k n", m=2, k=LRU)).then_inc(sem("lru_loaded"), 16)
            stream_rest("in0")
            for stage in ("out0", "up0", "down0", "in2", "out2", "up2", "down2"):
                stream_first(stage)
                stream_rest(stage)
            for k in range(DT):
                sp.wait_ge(sem("h_updated"), 3 * DT + k + 1)
                sp.dma_start(a["out"][:, k, :], h[:, k, META:T2]).then_inc(sem("out_stored"), 16)
            sp.wait_ge(sem("out_stored"), 16 * DT)

        INPUTS = 16 * 8

        @block.tensor
        def _(pe):
            def unit_wait(n):
                pe.wait_ge(sem(f"unit_loaded{n % WSLOTS}"), 16 * (n // WSLOTS + 1))

            def out_tile(q, n, b0, rhs, ncols, free):
                pe.wait_ge(sem("tile_read"), free)
                if ncols <= 512:
                    parts = [(0, 0, ncols)]
                else:
                    parts = [(0, 0, ncols // 2), (1, ncols // 2, ncols // 2)]
                for half, lo, cnt in parts:
                    for k, x in enumerate(rhs):
                        b = b0 + k
                        m = pe.matmul(pair(q, half, cnt), ring[:, (n + b // 16) % WSLOTS, b % 16 * P:(b % 16 + 1) * P],
                                      x[:, lo:lo + cnt], start=(k == 0), stop=(k == len(rhs) - 1))
                m.then_inc(sem("tile_done"), 1)

            def sums(count, k, first, last, ncols, half_cols, ready=None):
                pe.wait_ge(sem("squares_ready"), count)
                for s in range(2 if half_cols else 1):
                    m = pe.matmul(ps[:, 6 + s, 0:ncols], ones, sq[:, k % 2, s * ncols:(s + 1) * ncols],
                                  start=first, stop=last)
                m.then_inc(sem("squares_used"), 1)

            def norm_sums(n, two):
                for k in range(DT):
                    sums(SQ0[n] + k + 1, k, k == 0, k == DT - 1, HALF if two else SEQ, two)

            pe.wait_ge(sem("inputs_loaded"), INPUTS)
            pe.wait_ge(sem("cact_ready"), 1)
            with pe.Fori(0, 6) as i:
                for j in range(8):
                    if j % 2 == 0:
                        pe.wait_ge(sem(f"unit_loaded{j // 2}"), i * 16 + 16)
                    out_tile(j, j // 2, 8 * (j % 2), [cact[:, k:k + 1] for k in range(DT)], 1, i * 8 + (j + 1))
            norm_sums(0, False)
            pe.wait_ge(sem("normed"), DT)
            q0, n0 = Q0["in1"], U0["in1"]
            u1 = [u[:, k, 0:SEQ] for k in range(DT)]

            def in1(t):
                if t % 2 == 0:
                    unit_wait(n0 + t // 2)
                out_tile(q0 + t, n0 + t // 2, 8 * (t % 2), u1, SEQ, q0 + t + 1)

            for t in range(NS5):
                in1(t)
            for c in range(CHUNKS):
                for k in range(DT):
                    m = pe.matmul(ps[:, 1, 8 * c:8 * c + 8], u[:, k, c * P:(c + 1) * P], wgate[:, k, :],
                                  start=(k == 0), stop=(k == DT - 1))
            m.then_inc(sem("gates_done"), 1)

            def s5_in(j):
                if j == 0:
                    pe.wait_ge(sem("tile_read"), 2 + q0 + NS5)
                if j:
                    pe.wait_ge(sem("s5_in_read"), j)
                lo = 32 * (j % 4)
                for n in range(2):
                    m = pe.matmul(ps[:, 4 + n, 0:SEQ], s5b[n][lo:lo + 32, j // 4, :], us5[lo:lo + 32, j // 4, :],
                                  start=True, stop=True)
                m.then_inc(sem("s5_in_done"), 1)

            def s5_out(j):
                pe.wait_ge(sem("s5_state_ready"), j + 1)
                if j % 4 == 0 and j >= 8:
                    pe.wait_ge(sem("y5_ready"), j // 4 - 1)
                lo = 32 * (j % 4)
                for n in range(2):
                    m = pe.matmul(ps[lo:lo + 32, 6 + j // 4 % 2, 0:SEQ], s5ck[n][:, j, :], st5[j % 2][n],
                                  start=(n == 0), stop=(n == 1), tile_position=(0, lo))
                m.then_inc(sem("s5_out_done"), 1)

            for j in range(S5_TILES):
                in1(NS5 + j)
                s5_in(j)
                if j:
                    s5_out(j - 1)
            s5_out(S5_TILES - 1)
            unit_wait(U0["glu"])
            pe.wait_ge(sem("y5_gelu"), NS5)
            for t in range(NS5):
                out_tile(Q0["glu"] + t, U0["glu"], 4 * t, [y5[:, k, :] for k in range(NS5)], SEQ, Q0["glu"] + t + 1)
            for k in range(8):
                pe.wait_ge(sem("squares_ready"), 8 + k + 1)
                if k >= 2:
                    pe.wait_ge(sem("l2_read"), k - 1)
                pe.matmul(ps[:, 6 + k % 2, 0:SEQ], ones, sq[:, k % 2, 0:SEQ], start=True, stop=True
                          ).then_inc(sem("squares_used"), 1)
            pe.wait_ge(sem("gate_ready"), 1)
            pe.wait_ge(sem("beta_ready"), 1)
            pe.matmul(ps[:, 1, 64:80], upto, gate, start=True, stop=True)
            pe.matmul(ps[:, 1, 96:112], ones, gate, start=True, stop=True).then_inc(sem("csum_done"), 1)
            pe.wait_ge(sem("qk_ready"), 8)
            pe.wait_ge(sem("silu_qkv"), 12)
            pe.wait_ge(sem("csum_read"), 1)
            for c in range(CHUNKS):
                tok = slice(c * P, (c + 1) * P)
                if c:
                    pe.wait_ge(sem("chunk_read"), c)
                for hd in range(HEADS):
                    o = slice(hd * P, (hd + 1) * P)
                    g = gate[:, 4 * c + hd:4 * c + hd + 1]
                    bt = beta[:, 4 * c + hd:4 * c + hd + 1]
                    pe.matmul(ps[:, 0, o], qkv[:, 4 + hd, tok], qkv[:, 4 + hd, tok], start=True, stop=True)
                    pe.matmul(ps[:, 1, o], qkv[:, 4 + hd, tok], qkv[:, hd, tok], start=True, stop=True)
                    pe.matmul(ps[:, 2, o], g.broadcast_to([P, P]), upto, start=True, stop=True)
                    m = pe.matmul(ps[:, 3, o], bt.broadcast_to([P, P]), ident, start=True, stop=True)
                m.then_inc(sem("chunk_done"), 1)
                if c:
                    pe.wait_ge(sem("turned_read"), c)
                for hd in range(HEADS):
                    o = slice(hd * P, (hd + 1) * P)
                    pe.transpose(ps[:, 4, o], qkv[:, 4 + hd, tok], ident)
                    m = pe.transpose(ps[:, 5, o], qkv[:, 8 + hd, tok], ident)
                m.then_inc(sem("turned"), 1)
            pe.wait_ge(sem("chunk_read"), CHUNKS)
            pe.wait_ge(sem("turned_read"), CHUNKS)
            for v in range(LEVELS):
                for c in range(CHUNKS):
                    pe.wait_ge(sem("level_ready"), CHUNKS * v + c + 1)
                    pe.wait_ge(sem("inverse_ready"), CHUNKS * v + c + 1)
                    for hd in range(HEADS):
                        m = pe.matmul(ps[:, c, hd * P:(hd + 1) * P], a_lev[:, c, hd, :], x_inv[:, c, hd, :],
                                      start=True, stop=True)
                    m.then_inc(sem("ax_done"), 1)
                for c in range(CHUNKS):
                    pe.wait_ge(sem("ax_read"), CHUNKS * v + c + 1)
                    n = CHUNKS * v + c
                    if n >= 2:
                        pe.wait_ge(sem("inverse_ready"), CHUNKS + n - 1)
                    b = 4 + 2 * (c % 2)
                    for hd in range(HEADS):
                        o = slice(hd * P, (hd + 1) * P)
                        pe.matmul(ps[:, b, o], y_inv[:, c, hd, :], w_mat[:, c, hd, :], start=True, stop=True)
                        m = pe.matmul(ps[:, b + 1, o], w_mat[:, c, hd, :], y_inv[:, c, hd, :], start=True, stop=True)
                    m.then_inc(sem("xax_done"), 1)
            for c in range(CHUNKS):
                pe.wait_ge(sem("inverse_ready"), CHUNKS * LEVELS + CHUNKS)
                if c >= 2:
                    pe.wait_ge(sem("solved_read"), c - 1)
                b = 2 * (c % 2)
                for hd in range(HEADS):
                    o = slice(hd * P, (hd + 1) * P)
                    pe.matmul(ps[:, b, o], y_inv[:, c, hd, :], v_b[:, c, hd, :], start=True, stop=True)
                    m = pe.matmul(ps[:, b + 1, o], kb_g[:, c, hd, :], y_inv[:, c, hd, :], start=True, stop=True)
                m.then_inc(sem("solved"), 1)
            for c in range(CHUNKS):
                tok = slice(c * P, (c + 1) * P)
                pe.wait_ge(sem("solved_read"), c + 1)
                pe.wait_ge(sem("state_ready"), c + 1)
                for hd in range(HEADS):
                    m = pe.matmul(ps[:, 4, hd * P:(hd + 1) * P], kc[:, c, hd, :], state[:, hd, :], start=True, stop=True)
                m.then_inc(sem("seen_done"), 1)
                pe.wait_ge(sem("v_new_ready"), c + 1)
                if c:
                    pe.wait_ge(sem("o_read"), c)
                for hd in range(HEADS):
                    m = pe.matmul(ps[:, 5, hd * P:(hd + 1) * P], k_tail[:, c, hd, :], v_new[:, hd, :], start=True, stop=True)
                    pe.matmul(ps[:, 6, hd * P:(hd + 1) * P], state[:, hd, :], q_dec[:, c, hd, :], start=True, stop=False)
                    m = pe.matmul(ps[:, 6, hd * P:(hd + 1) * P], v_new[:, hd, :], qk_d[:, c, hd, :], start=False, stop=True)
                m.then_inc(sem("chunk_out_done"), 1)
            for k in range(HEADS):
                pe.wait_ge(sem("squares_ready"), 16 + k + 1)
                if k >= 2:
                    pe.wait_ge(sem("o_norm_read"), k - 1)
                pe.matmul(ps[:, k % 2, 0:SEQ], ones, sq[:, k % 2, 0:SEQ], start=True, stop=True
                          ).then_inc(sem("squares_used"), 1)
            pe.wait_ge(sem("mix1_ready"), 8)
            for t in range(DT):
                if t % 2 == 0:
                    unit_wait(U0["out1"] + t // 2)
                out_tile(Q0["out1"] + t, U0["out1"] + t // 2, 8 * (t % 2), [mix[:, k, :] for k in range(DT)], SEQ,
                         Q0["out1"] + t + 1)

            norm_sums(1, False)
            pe.wait_ge(sem("normed"), 2 * DT)
            for c in range(CHUNKS):
                for k in range(DT):
                    m = pe.matmul(ps[:, 0, 36 * c:36 * c + 36], u[:, k, c * P:(c + 1) * P], wrouter[:, k, :],
                                  start=(k == 0), stop=(k == DT - 1))
            m.then_inc(sem("router_done"), 1)
            for c in range(CHUNKS):
                for s in range(2):
                    if c >= 1:
                        pe.wait_ge(sem("xtok_read"), 2 * c + s - 1)
                    for k in range(4):
                        m = pe.transpose(ps[:, 2 + s, k * P:(k + 1) * P], u[:, 4 * s + k, c * P:(c + 1) * P], ident)
                    m.then_inc(sem("xtok_done"), 1)
            pe.wait_ge(sem("chosen_ready"), 1)
            for c in range(CHUNKS):
                for j in range(c + 1):
                    pe.matmul(ps[:, 1, 32 * c:32 * c + 32], ones if j < c else ccol("strict", 0, P), r32[5][:, j, :],
                              start=(j == 0), stop=(j == c))
            for j in range(CHUNKS):
                m = pe.matmul(ps[:, 1, 128:160], ones, r32[5][:, j, :], start=(j == 0), stop=(j == CHUNKS - 1))
            m.then_inc(sem("places_done"), 1)
            pe.wait_ge(sem("ecol_ready"), 1)
            pe.matmul(ps[0:1, 5, 0:P], ecol[:, 0:1], ident, start=True, stop=True).then_inc(sem("erow_done"), 1)
            pe.wait_ge(sem("erow_read"), 1)

            def rows_turned(b, p, wload):
                pe.wait_ge(sem(f"rows_loaded{p}"), wload)
                if b is not None:
                    pe.wait_ge(sem("xt_read"), b)
                for k in range(DT):
                    m = pe.transpose(ps[:, 2 + k // 4, k % 4 * P:(k % 4 + 1) * P], xb[p][:, k * P:(k + 1) * P], ident)
                m.then_inc(sem("xt_done"), 1)

            def gate_up(b, p, wload, waits=True):
                pe.wait_ge(sem("xt_read"), b + 1)
                pe.wait_ge(sem(f"gu_loaded{p}"), wload)
                if waits:
                    pe.wait_ge(sem("hidden_ready"), FREE + b - 1)
                for k in range(DT):
                    m = pe.matmul(ps[:, p, :], xbt[p][:, k, :], mw[p][:, k * 512:(k + 1) * 512],
                                  start=(k == 0), stop=(k == DT - 1))
                m.then_inc(sem("gu_done"), 1)

            def hidden_turned(b, p):
                pe.wait_ge(sem("hidden_ready"), FREE + b + 1)
                pe.wait_ge(sem("ht_read"), FREE + b)
                for k in range(2):
                    m = pe.transpose(ps[:, 4, k * P:(k + 1) * P], h_b[:, p, k * P:(k + 1) * P], ident)
                m.then_inc(sem("ht_done"), 1)

            def down(b, p, wload):
                pe.wait_ge(sem("ht_read"), FREE + b + 1)
                pe.wait_ge(sem(f"dn_loaded{p}"), wload)
                pe.wait_ge(sem("dn_read"), FREE + b)
                for s in range(2):
                    for k in range(2):
                        m = pe.matmul(ps[:, 5 + s, :], ht_b[:, k, :],
                                      mw[p][:, 2 * UNIT + k * D + 512 * s:2 * UNIT + k * D + 512 * (s + 1)],
                                      start=(k == 0), stop=(k == 1))
                m.then_inc(sem("dn_done"), 1)

            pe.drain().then_inc(sem("ht_done"), FREE)
            pe.drain().then_inc(sem("dn_done"), FREE)
            rows_turned(None, 0, 16)
            gate_up(0, 0, 16, False)
            rows_turned(1, 1, 16)
            with pe.Fori(0, BLOCKS // 2 - 1) as i:
                for p in range(2):
                    b = i * 2 + p
                    gate_up(b + 1, 1 - p, i * 16 + 16 * (1 + p), True)
                    hidden_turned(b, p)
                    rows_turned(b + 2, p, i * 16 + 32)
                    down(b, p, i * 16 + 16)
            n = BLOCKS - 2
            gate_up(n + 1, 1, 8 * BLOCKS)
            hidden_turned(n, 0)
            down(n, 0, 8 * BLOCKS)
            hidden_turned(n + 1, 1)
            down(n + 1, 1, 8 * BLOCKS)
            pe.wait_ge(sem("moe_ready"), CHUNKS)
            for k in range(DT):
                if k >= 2:
                    pe.wait_ge(sem("moe_added"), k - 1)
                for c in range(CHUNKS):
                    m = pe.transpose(ps[:, k % 2, c * P:(c + 1) * P], moe[:, c, k * P:(k + 1) * P], ident)
                m.then_inc(sem("moe_turned"), 1)
            norm_sums(2, False)

            norm_sums(3, True)
            pe.wait_ge(sem("normed"), 4 * DT)
            q0, n0 = Q0["in0"], U0["in0"]
            u2 = [u[:, k, :] for k in range(DT)]

            def in0(t):
                if t % 2 == 0:
                    unit_wait(n0 + t // 2)
                out_tile(q0 + t, n0 + t // 2, 8 * (t % 2), u2, T2, q0 + t + 1)

            def lru_gates(i):
                pe.wait_ge(sem("lru_conv"), i + 1)
                if i == 0:
                    pe.wait_ge(sem("lru_loaded"), 16)
                if i:
                    pe.wait_ge(sem("lru_sig"), i)
                for n in range(2):
                    for s in range(2):
                        m = pe.matmul(ps[:, 4 + 2 * n + s, 0:HALF], w_lru[:, n, i, :],
                                      x_lru[:, i % 2, s * HALF:(s + 1) * HALF], start=True, stop=True)
                m.then_inc(sem("lru_gates"), 1)

            for i in range(LRU):
                in0(2 * i)
                in0(2 * i + 1)
                if i:
                    lru_gates(i - 1)
            for t in range(2 * LRU, 2 * LRU + Q_TILES + 3):
                in0(t)
                if t == 2 * LRU:
                    lru_gates(LRU - 1)
            pe.wait_ge(sem("tile_read"), q0 + 27 + 2)
            pe.wait_ge(sem("lru_sig"), LRU)
            for c, (lo, n) in enumerate(CH2):
                m = pe.transpose(ps[0:n, 4 + c // 4, c % 4 * P:(c % 4 + 1) * P], v_fm[:, lo:lo + n], ident)
            m.then_inc(sem("v_turned"), 1)
            ATT = [(c, hp) for c in range(len(CH2)) for hp in range(Q_TILES)]

            def scores(n):
                c, hp = ATT[n]
                lo, cnt = CH2[c]
                if n >= 2:
                    pe.wait_ge(sem("scores_read"), n - 1)
                for e in range(2):
                    rows = slice(64 * e, 64 * e + 64)
                    out = ps[0:cnt, 2 * (n % 2) + e, :]
                    kk = k_fm[rows, hp // 4, :]
                    qq = q_fm[rows, hp, lo:lo + cnt]
                    if c <= 2:
                        m = pe.matmul(out[:, 0:lo + cnt], qq, kk[:, 0:lo + cnt], start=True, stop=True)
                    else:
                        pe.matmul(out[:, 0:META], qq, kk[:, 0:META], start=True, stop=True)
                        m = pe.matmul(out[:, META:META + 2 * P], qq, kk[:, lo - P:lo + P], start=True, stop=True)
                m.then_inc(sem("scores_done"), 1)

            def key_parts(c):
                return [(0, META, 0)] + [(META + P * i, P, d) for i, d in enumerate(([], [1], [1, 2], [2, 3], [3, 4])[c])]

            def turn(n):
                c, hp = ATT[n]
                cnt = CH2[c][1]
                pe.wait_ge(sem("prob_ready"), n + 1)
                if n == 0:
                    pe.wait_ge(sem("v_read"), 1)
                if n:
                    pe.wait_ge(sem("prob_turned_read"), n)
                for e in range(2):
                    for i, (k0, kn, _) in enumerate(key_parts(c)):
                        m = pe.transpose(ps[0:kn, 4 + e, i * P:i * P + cnt], prob[0:cnt, n % 2, e, k0:k0 + kn],
                                         ident[0:cnt, 0:cnt])
                m.then_inc(sem("prob_turned"), 1)

            def attend(n):
                c, hp = ATT[n]
                cnt = CH2[c][1]
                pe.wait_ge(sem("prob_turned_read"), n + 1)
                if n >= 2:
                    pe.wait_ge(sem("attended_read"), n - 1)
                parts = key_parts(c)
                for e in range(2):
                    for i, (_, kn, vc) in enumerate(parts):
                        kv = hp // 4
                        m = pe.matmul(ps[64 * e:64 * e + 64, 6 + n % 2, 0:cnt], v_tok[0:kn, vc, 64 * kv:64 * kv + 64],
                                      prob_t[0:kn, n % 2, e, i * P:i * P + cnt], start=(i == 0),
                                      stop=(i == len(parts) - 1), tile_position=(0, 64 * e))
                m.then_inc(sem("attended"), 1)

            for n in range(len(ATT) + 2):
                if n < len(ATT):
                    scores(n)
                if 1 <= n <= len(ATT):
                    turn(n - 1)
                if n >= 2:
                    attend(n - 2)

            def out_product(stage, rhs, ready, n):
                pe.wait_ge(sem(ready[0]), ready[1])
                for t in range(DT):
                    unit_wait(U0[stage] + t)
                    out_tile(Q0[stage] + t, U0[stage] + t, 0, rhs, T2, Q0[stage] + t + 1)
                    if t:
                        sums(SQ0[n] + t, t - 1, t == 1, False, HALF, True)
                sums(SQ0[n] + DT, DT - 1, False, True, HALF, True)

            def ffn(up, down, n):
                q0, n0 = Q0[up], U0[up]
                with pe.Fori(0, 5) as i:
                    for j in range(8):
                        if j % 2 == 0:
                            un = n0 + j // 2
                            pe.wait_ge(sem(f"unit_loaded{un % WSLOTS}"), i * 16 + 16 * (un // WSLOTS + 1))
                        out_tile(q0 + j, n0 + j // 2, 8 * (j % 2), u2, T2, i * 8 + (q0 + j + 1))
                for j in range(40, 44):
                    if j % 2 == 0:
                        unit_wait(n0 + j // 2)
                    out_tile(q0 + j, n0 + j // 2, 8 * (j % 2), u2, T2, q0 + j + 1)
                q0, n0 = Q0[down], U0[down]
                pe.wait_ge(sem("prod_ready"), FF * (1 if n == 6 else 2))
                for t in range(DT):
                    unit_wait(n0 + 2 * t)
                    unit_wait(n0 + 2 * t + 1)
                    pe.wait_ge(sem("tile_read"), q0 + t + 1)
                    for s in range(2):
                        for k in range(FF):
                            slot = (n0 + 2 * t + k // DOWN_K) % WSLOTS
                            b = k % DOWN_K
                            m = pe.matmul(pair(q0 + t, s, HALF), ring[:, slot, b * P:(b + 1) * P],
                                          prod[:, k, s * HALF:(s + 1) * HALF], start=(k == 0), stop=(k == FF - 1))
                    m.then_inc(sem("tile_done"), 1)
                    if t:
                        sums(SQ0[n] + t, t - 1, t == 1, False, HALF, True)
                sums(SQ0[n] + DT, DT - 1, False, True, HALF, True)

            pe.wait_ge(sem("attended_read"), len(ATT))
            out_product("out0", [mix0[:, k, :] for k in range(2 * LRU)], ("lru_out", LRU), 4)
            norm_sums(5, True)
            pe.wait_ge(sem("normed"), 5 * DT)
            ffn("up0", "down0", 6)
            norm_sums(7, True)
            pe.wait_ge(sem("normed"), 6 * DT)
            q0, n0 = Q0["in2"], U0["in2"]
            with pe.Fori(0, 6) as i:
                for j in range(8):
                    if j % 2 == 0:
                        un = n0 + j // 2
                        pe.wait_ge(sem(f"unit_loaded{un % WSLOTS}"), i * 16 + 16 * (un // WSLOTS + 1))
                    out_tile(q0 + j, n0 + j // 2, 8 * (j % 2), u2, T2, i * 8 + (q0 + j + 1))
            for c, (lo, cnt) in enumerate(CH2):
                for k in range(DT):
                    m = pe.matmul(ps[:, 4, SSD_H * c:SSD_H * (c + 1)], u[:, k, lo:lo + P], wdt[:, k, :],
                                  start=(k == 0), stop=(k == DT - 1))
            m.then_inc(sem("dt_done"), 1)
            pe.wait_ge(sem("da_ready"), 1)
            for c, (lo, cnt) in enumerate(CH2):
                pe.matmul(ps[:, 5, SSD_H * c:SSD_H * (c + 1)], upto, da2[:, c, :], start=True, stop=True)
                m = pe.matmul(ps[:, 6, SSD_H * c:SSD_H * (c + 1)], ones[0:cnt, :], da2[0:cnt, c, :], start=True, stop=True)
            m.then_inc(sem("cs2_done"), 1)
            pe.wait_ge(sem("cs2_read"), 1)
            pe.wait_ge(sem("ssm_silu"), 2 * SSD_X)
            SSD = [(c, g) for c in range(len(CH2)) for g in range(SSD_G)]

            def ssd_in(n):
                c, g = SSD[n]
                lo, cnt = CH2[c]
                tok = slice(lo, lo + cnt)
                if n >= 2:
                    pe.wait_ge(sem("ssd_in_read"), n - 1)
                b = 2 * (n % 2)
                for e in range(4):
                    pe.matmul(ps[:, b, P * e:P * e + cnt], da2[0:cnt, c, 4 * g + e:4 * g + e + 1].broadcast_to([cnt, P]),
                              upto[0:cnt, 0:cnt], start=True, stop=True)
                B, C = xbc[:, SSD_X + g, tok], xbc[:, SSD_X + SSD_G + g, tok]
                pe.matmul(ps[0:cnt, b + 1, 0:cnt], B, C, start=True, stop=True)
                pe.transpose(ps[0:cnt, b + 1, P:2 * P], B, ident)
                for e in range(2):
                    m = pe.transpose(ps[0:cnt, b + 1, (2 + e) * P:(3 + e) * P], xbc[:, 2 * g + e, tok], ident)
                m.then_inc(sem("ssd_in_done"), 1)

            def ssd_out(n):
                c, g = SSD[n]
                lo, cnt = CH2[c]
                pe.wait_ge(sem("ssd_dve"), n + 1)
                pe.wait_ge(sem("ssd_pool"), n + 1)
                if n >= 2:
                    pe.wait_ge(sem("ssd_out_read"), n - 1)
                if c:
                    pe.wait_ge(sem("st2_ready"), n - SSD_G + 1)
                for e in range(4):
                    out = ps[64 * (e % 2):64 * (e % 2) + 64, 4 + n % 2, P * (e // 2):P * (e // 2) + cnt]
                    pe.matmul(out, xdt[n % 2][0:cnt, e, :], decay2[n % 2][0:cnt, e, 0:cnt], start=True, stop=(c == 0),
                              tile_position=(0, 64 * (e % 2)))
                    if c:
                        pe.matmul(out, st2[:, 4 * g + e, :], cdec[n % 2][:, e, 0:cnt], start=False, stop=True,
                                  tile_position=(0, 64 * (e % 2)))
                pe.matmul(ps[:, 6 + n % 2, 0:256], b_tok[0:cnt, n % 2, :], xdd[0:cnt, n % 2].rearrange("p h n -> p (h n)"),
                          start=True, stop=True).then_inc(sem("ssd_out_done"), 1)

            for n in range(len(SSD) + 1):
                if n < len(SSD):
                    ssd_in(n)
                if n:
                    ssd_out(n - 1)
            for g in range(SSD_G):
                pe.wait_ge(sem("group_squares"), 2 * g + 2)
                if g >= 2:
                    pe.wait_ge(sem("group_root"), g - 1)
                if g < 2:
                    pe.wait_ge(sem("ssd_in_read"), len(SSD))
                for e in range(2):
                    for s in range(2):
                        m = pe.matmul(ps[:, 2 * (g % 2) + s, 0:HALF], ones, gsq[e][:, s * HALF:(s + 1) * HALF],
                                      start=(e == 0), stop=(e == 1))
                m.then_inc(sem("group_sums"), 1)
            out_product("out2", [xbc[:, k, :] for k in range(SSD_X)], ("mix2_ready", SSD_X), 8)
            norm_sums(9, True)
            pe.wait_ge(sem("normed"), 7 * DT)
            ffn("up2", "down2", 10)

        @block.scalar
        def _(act):
            def norm_squares(n, src, ready, count0, ncols):
                for k in range(DT):
                    s, v = ready(k)
                    act.wait_ge(sem(s), v)
                    if SQ0[n] + k >= 2:
                        act.wait_ge(sem("squares_used"), SQ0[n] + k - 1)
                    act.activation(sq[:, k % 2, 0:ncols], src(k), ACT.Square).then_inc(sem("squares_ready"), 1)

            def norm_root(n, ncols, banks=None):
                act.wait_ge(sem("squares_used"), SQ0[n] + DT)
                if n:
                    act.wait_ge(sem("norm_applied"), n)
                if ncols > 512:
                    act.activation(halves(rs[:, 0:ncols]), ps[:, 6:8, 0:HALF], ACT.Sqrt, bias=eps, scale=1.0 / D
                                   ).then_inc(sem("root_ready"), 1)
                else:
                    act.activation(rs[:, 0:ncols], ps[:, 6, 0:ncols], ACT.Sqrt, bias=eps, scale=1.0 / D
                                   ).then_inc(sem("root_ready"), 1)

            act.wait_ge(sem("inputs_loaded"), INPUTS)
            act.activation(cact[:, :], pcol("c", 0, DT), ACT.Silu).then_inc(sem("cact_ready"), 1)
            act.activation(s5s[:, 0, :], pcol("log_step", 0, 16), ACT.Exp).then_inc(sem("s5_step"), 1)
            act.wait_ge(sem("s5_angle"), 1)
            act.activation(s5s[:, 6, :], s5s[:, 5, :], ACT.Exp)
            act.activation(s5s[:, 8, :], s5s[:, 3, :], ACT.Sin)
            act.activation(s5s[:, 7, :], s5s[:, 4, :], ACT.Sin).then_inc(sem("s5_trig"), 1)
            act.wait_ge(sem("lam_arg"), 1)
            act.activation(lam8[:, 1, :], lam8[:, 1, :], ACT.Exp).then_inc(sem("lam_exp"), 1)
            act.wait_ge(sem("lam_one"), 1)
            act.activation(lam8[:, 2, :], lam8[:, 2, :], ACT.Ln).then_inc(sem("lam_ln"), 1)
            with act.Fori(0, 6) as i:
                for j in range(8):
                    act.wait_ge(sem("tile_done"), i * 8 + (j + 1))
                    act.wait_ge(sem("inputs_loaded"), INPUTS)
                    act.activation(mod[:, bass.ds(i * 8 + j, 1)], pair(j, 0, 1), ACT.Identity,
                                   bias=par[:, bass.ds(i * 8 + (PCOL["b_ada"] + j), 1)]).then_inc(sem("tile_read"), 1)
            norm_squares(0, lambda k: h[:, k, META:T2], lambda k: ("inputs_loaded", INPUTS), 0, SEQ)
            norm_root(0, SEQ)
            q0 = Q0["in1"]
            for t in range(NS5):
                act.wait_ge(sem("tile_done"), q0 + t + 1)
                act.activation(us5[:, t, :], pair(q0 + t), ACT.Copy).then_inc(sem("tile_read"), 1)
            for j in range(16):
                q = q0 + NS5 + j
                act.wait_ge(sem("tile_done"), q + 1)
                if j < 12:
                    if j >= 2:
                        act.wait_ge(sem("conv_done"), j - 1)
                    else:
                        act.wait_ge(sem("pads_ready"), 1)
                    act.activation(cbuf[j % 2][:, 3:], pair(q), ACT.Copy).then_inc(sem("tile_read"), 1)
                else:
                    act.activation(z1[:, j - 12, :], pair(q), ACT.Silu).then_inc(sem("tile_read"), 1)
                if 1 <= j < 13:
                    act.wait_ge(sem("conv_done"), j)
                    act.activation(qkv[:, j - 1, :], qkv[:, j - 1, :], ACT.Silu).then_inc(sem("silu_qkv"), 1)
            for t in range(NS5):
                act.wait_ge(sem("y5_ready"), t + 1)
                act.activation(y5[:, t, :], y5[:, t, :], ACT.Gelu_apprx_tanh).then_inc(sem("y5_gelu"), 1)
            for t in range(NS5):
                act.wait_ge(sem("tile_done"), Q0["glu"] + t + 1)
                if t:
                    act.wait_ge(sem("mix1_ready"), t)
                act.activation(sig, pair(Q0["glu"] + t), ACT.Sigmoid, bias=pcol("b_glu", t)
                               ).then_inc(sem("tile_read"), 1)
            act.wait_ge(sem("mix1_ready"), NS5)
            for k in range(8):
                act.wait_ge(sem("silu_qkv"), 12)
                act.wait_ge(sem("squares_used"), 8 + k - 1)
                act.activation(sq[:, k % 2, 0:SEQ], qkv[:, k, :], ACT.Square).then_inc(sem("squares_ready"), 1)
                if k:
                    act.wait_ge(sem("squares_used"), 8 + k)
                    act.activation(l2r[:, k - 1, :], ps[:, 6 + (k - 1) % 2, 0:SEQ], ACT.Sqrt, bias=eps
                                   ).then_inc(sem("l2_read"), 1)
            act.wait_ge(sem("squares_used"), 16)
            act.activation(l2r[:, 7, :], ps[:, 7, 0:SEQ], ACT.Sqrt, bias=eps).then_inc(sem("l2_read"), 1)
            act.wait_ge(sem("gate_arg"), 1)
            act.activation(sp2, sp2, ACT.Exp).then_inc(sem("gate_exp"), 1)
            act.wait_ge(sem("gate_one"), 1)
            act.activation(sp3, sp3, ACT.Ln)
            act.activation(sp4[:, 0:HEADS], pcol("a_log", 0, HEADS), ACT.Exp).then_inc(sem("gate_ln"), 1)
            act.activation(beta.rearrange("p (c h) -> p c h", c=CHUNKS),
                           ps[:, 1, 0:32].rearrange("p (c h) -> p c h", c=CHUNKS)[:, :, HEADS:8], ACT.Sigmoid
                           ).then_inc(sem("beta_ready"), 1)
            act.wait_ge(sem("csum_copied"), 1)
            act.activation(ecs, csum, ACT.Exp)
            act.activation(egt, gtot, ACT.Exp)
            act.activation(etail, etail, ACT.Exp).then_inc(sem("gate_exps"), 1)
            for c in range(CHUNKS):
                act.wait_ge(sem("diff_ready"), c + 1)
                act.activation(dtmp, dtmp, ACT.Exp).then_inc(sem("decay_ready"), 1)
                act.activation(egb, ps[:, 2, :].rearrange("p (h n) -> p h n", h=HEADS), ACT.Exp
                               ).then_inc(sem("egb_ready"), 1)
            for v in range(LEVELS):
                for c in range(CHUNKS):
                    act.wait_ge(sem("ax_done"), CHUNKS * v + c + 1)
                    if v:
                        act.wait_ge(sem("inverse_ready"), CHUNKS * v + c + 1)
                    act.activation(w_mat[:, c], ps[:, c, :].rearrange("p (h n) -> p h n", h=HEADS), ACT.Copy
                                   ).then_inc(sem("ax_read"), 1)
            for c in range(CHUNKS):
                act.wait_ge(sem("solved"), c + 1)
                b = 2 * (c % 2)
                act.activation(val[:, c], ps[:, b, :].rearrange("p (h n) -> p h n", h=HEADS), ACT.Copy)
                act.activation(kc[:, c], ps[:, b + 1, :].rearrange("p (h n) -> p h n", h=HEADS), ACT.Copy
                               ).then_inc(sem("solved_read"), 1)
            for c in range(CHUNKS):
                act.wait_ge(sem("chunk_out_done"), c + 1)
                act.activation(o_gdn[:, :, c * P:(c + 1) * P], ps[:, 6, :].rearrange("p (h n) -> p h n", h=HEADS),
                               ACT.Copy).then_inc(sem("o_read"), 1)
            act.drain()
            for k in range(HEADS):
                act.wait_ge(sem("squares_used"), 16 + k - 1)
                act.activation(sq[:, k % 2, 0:SEQ], o_gdn[:, k, :], ACT.Square).then_inc(sem("squares_ready"), 1)
            for k in range(HEADS):
                act.wait_ge(sem("squares_used"), 16 + k + 1)
                if k:
                    act.wait_ge(sem("mix1_ready"), NS5 + k)
                act.activation(rs[:, 0:SEQ], ps[:, k % 2, 0:SEQ], ACT.Sqrt, bias=eps, scale=1.0 / P
                               ).then_inc(sem("o_norm_read"), 1)

            norm_squares(1, lambda k: h[:, k, META:T2], lambda k: ("tile_read", Q0["out1"] + k + 3), 0, SEQ)
            norm_root(1, SEQ)
            for c in range(CHUNKS):
                for s in range(2):
                    act.wait_ge(sem("xtok_done"), 2 * c + s + 1)
                    act.activation(xtok[:, c, 512 * s:512 * (s + 1)], ps[:, 2 + s, :], ACT.Copy
                                   ).then_inc(sem("xtok_read"), 1)
            act.wait_ge(sem("grp_arg"), 1)
            act.activation(r4[1], r4[1], ACT.Exp).then_inc(sem("grp_exp"), 1)
            act.wait_ge(sem("top_arg"), 1)
            act.activation(r1[6], r1[6], ACT.Exp).then_inc(sem("top_exp"), 1)

            def rows_out_of_psum(b, p, count, waits=True):
                act.wait_ge(sem("xt_done"), count)
                if waits:
                    act.wait_ge(sem("gu_done"), b - 1)
                act.wait_ge(sem("top_exp"), 1)
                act.activation(xbt[p].rearrange("p k n -> p (k n)").rearrange("p (s n) -> p s n", s=2), ps[:, 2:4, :],
                               ACT.Copy).then_inc(sem("xt_read"), 1)

            def gate_silu(b, p):
                act.wait_ge(sem("gu_done"), b + 1)
                if not isinstance(b, int) or b >= 2:
                    act.wait_ge(sem("hidden_ready"), FREE + b - 1)
                act.wait_ge(sem("top_exp"), 1)
                act.activation(silu_b[:, p, :], ps[:, p, 0:D_EXPERT], ACT.Silu).then_inc(sem("silu_ready"), 1)

            def store_block(b, p):
                act.wait_ge(sem("dn_read"), FREE + b + 1)
                act.dma_start(rows_out[bass.ds(b * P, P), :], yb[p]).then_inc(sem(f"rows_stored{p}"), 16)

            rows_out_of_psum(0, 0, 1, False)
            gate_silu(0, 0)
            rows_out_of_psum(1, 1, 2, False)
            with act.Fori(0, BLOCKS // 2 - 1) as i:
                for p in range(2):
                    b = i * 2 + p
                    act.wait_ge(sem("hidden_ready"), FREE + b)
                    act.wait_ge(sem("gu_done"), b + 2)
                    act.wait_ge(sem("top_exp"), 1)
                    act.activation(silu_b[:, 1 - p, :], ps[:, 1 - p, 0:D_EXPERT], ACT.Silu).then_inc(sem("silu_ready"), 1)
                    rows_out_of_psum(b + 2, p, b + 3)
                    store_block(b, p)
            gate_silu(BLOCKS - 1, 1)
            store_block(BLOCKS - 2, 0)
            store_block(BLOCKS - 1, 1)
            norm_squares(2, lambda k: h[:, k, META:T2], lambda k: ("moe_added", k + 1), 0, SEQ)
            norm_root(2, SEQ)

            norm_squares(3, lambda k: h[:, k, :], lambda k: ("normed", 3 * DT), 0, T2)
            norm_root(3, T2)
            q0 = Q0["in0"]

            def tile_copy(q, out, func=ACT.Copy, scale=1.0):
                act.wait_ge(sem("tile_done"), q + 1)
                act.activation(halves(out), pair2(q), func, scale=scale).then_inc(sem("tile_read"), 1)

            def lru_functions(i):
                b = i % 2
                act.wait_ge(sem("lru_gates"), i + 1)
                if i >= 2:
                    act.wait_ge(sem("lru_out"), i - 1)
                act.activation(halves(r_lru[:, b, :]), ps[:, 4:6, 0:HALF], ACT.Sigmoid, bias=pcol("b_a", i))
                act.activation(halves(i_lru[:, b, :]), ps[:, 6:8, 0:HALF], ACT.Sigmoid, bias=pcol("b_x", i)
                               ).then_inc(sem("lru_sig"), 1)
                act.drain()
                act.activation(a_lru[:, b, :], r_lru[:, b, :], ACT.Exp, scale=lam8[:, 0, i:i + 1])
                act.activation(t_lru[:, b, :], r_lru[:, b, :], ACT.Tanh, scale=lam8[:, 3, i:i + 1]
                               ).then_inc(sem("lru_decay"), 1)
                act.wait_ge(sem("lru_square"), i + 1)
                act.activation(t_lru[:, b, :], t_lru[:, b, :], ACT.Sqrt).then_inc(sem("lru_root"), 1)

            for i in range(LRU):
                if i >= 2:
                    act.wait_ge(sem("lru_out"), i - 1)
                tile_copy(q0 + 2 * i, g_lru[:, i % 2, :], ACT.Gelu_apprx_tanh)
                if i >= 2:
                    act.wait_ge(sem("lru_conv"), i - 1)
                else:
                    act.wait_ge(sem("pads_ready"), 2)
                tile_copy(q0 + 2 * i + 1, pad[i % 2][:, 3:])
                if i:
                    lru_functions(i - 1)
            for t in range(Q_TILES):
                tile_copy(q0 + 2 * LRU + t, q_fm[:, t, :], scale=HEAD ** -0.5)
                if t == 0:
                    lru_functions(LRU - 1)
            for t in range(2):
                tile_copy(q0 + 24 + t, k_fm[:, t, :])
            tile_copy(q0 + 26, v_fm)
            act.wait_ge(sem("v_turned"), 1)
            act.activation(v_tok[0:META, 0, :], ps[0:META, 4, 0:P], ACT.Copy)
            act.activation(v_tok[:, 1:4, :], ps[:, 4, P:].rearrange("p (c n) -> p c n", c=3), ACT.Copy)
            act.activation(v_tok[:, 4, :], ps[:, 5, 0:P], ACT.Copy).then_inc(sem("v_read"), 1)
            ATT = [(c, hp) for c in range(len(CH2)) for hp in range(Q_TILES)]
            for n in range(len(ATT) + 2):
                if n < len(ATT):
                    c, hp = ATT[n]
                    cnt, nk, b = CH2[c][1], (META, META + P, META + 2 * P, META + 2 * P, META + 2 * P)[c], n % 2
                    act.wait_ge(sem("max_ready"), n + 1)
                    for e in range(2):
                        x = prob[0:cnt, b, e, 0:nk]
                        nm = stat[0:cnt, b, 1, e:e + 1]
                        act.activation(x, x, ACT.Exp, bias=nm, accum_out=stat[0:cnt, b, 2, e:e + 1])
                        m = act.activation(stat[0:cnt, b, 3, e:e + 1], pcol("sinks", 2 * hp + e)[0:cnt, :], ACT.Exp, bias=nm)
                    m.then_inc(sem("exp_ready"), 1)
                if 1 <= n <= len(ATT):
                    c, hp = ATT[n - 1]
                    cnt, b = CH2[c][1], (n - 1) % 2
                    act.wait_ge(sem("prob_turned"), n)
                    if n >= 3:
                        act.wait_ge(sem("attended"), n - 2)
                    m = act.activation(prob_t[0:META, b, :, 0:cnt], ps[0:META, 4:6, 0:cnt], ACT.Copy)
                    if c:
                        w = P if c == 1 else 2 * P
                        m = act.activation(prob_t[:, b, :, P:P + w], ps[:, 4:6, P:P + w], ACT.Copy)
                    m.then_inc(sem("prob_turned_read"), 1)
                if n >= 2:
                    c, hp = ATT[n - 2]
                    lo, cnt = CH2[c]
                    act.wait_ge(sem("attended"), n - 1)
                    act.activation(mix0[:, LRU + hp, lo:lo + cnt], ps[:, 6 + n % 2, 0:cnt], ACT.Copy
                                   ).then_inc(sem("attended_read"), 1)

            def product_out(stage, dst, n):
                for t in range(DT):
                    q = Q0[stage] + t
                    act.wait_ge(sem("tile_done"), q + 1)
                    act.wait_ge(sem("squares_used"), SQ0[n] + t - 1)
                    act.activation(halves(sq[:, t % 2, :]), pair2(q), ACT.Square).then_inc(sem("squares_ready"), 1)
                    act.activation(halves(dst[:, t, :]), pair2(q), ACT.Copy).then_inc(sem("tile_read"), 1)
                norm_root(n, T2)

            def ffn(up, down, n, run):
                norm_squares(n - 1, lambda k: h[:, k, :], lambda k: ("h_updated", DT * (n - 6) // 2 + k + 1), 0, T2)
                norm_root(n - 1, T2)
                q0, c0 = Q0[up], 2 + 2 * FF * run
                with act.Fori(0, FF // 2) as i:
                    for j in range(2):
                        for e in range(2):
                            act.wait_ge(sem("tile_done"), i * 4 + (q0 + 2 * j + e + 1))
                            act.wait_ge(sem("ffn_conv"), i * 4 + (c0 + 2 * j + e - 1))
                            act.wait_ge(sem("pads_ready"), 2)
                            act.activation(halves(pad[e][:, 3:]), pair2(q0 + e), ACT.Copy).then_inc(sem("tile_read"), 1)
                        act.wait_ge(sem("ffn_conv"), i * 4 + (c0 + 2 * j + 1))
                        act.wait_ge(sem("pads_ready"), 2)
                        act.activation(gact, gact, ACT.Gelu_apprx_tanh).then_inc(sem("ffn_gelu"), 1)
                product_out(down, m_out, n)

            product_out("out0", m_out, 4)
            ffn("up0", "down0", 6, 0)
            norm_squares(7, lambda k: h[:, k, :], lambda k: ("h_updated", 2 * DT), 0, T2)
            norm_root(7, T2)
            q0 = Q0["in2"]
            with act.Fori(0, SSD_X // 2) as i:
                for j in range(2):
                    act.wait_ge(sem("tile_done"), i * 2 + (q0 + j + 1))
                    act.wait_ge(sem("pads_ready"), 2)
                    act.activation(halves(z2[:, bass.ds(i * 2 + j, 1), :].rearrange("p o n -> p (o n)")), pair2(q0 + j), ACT.Silu
                                   ).then_inc(sem("tile_read"), 1)
            q0 += SSD_X

            def ssm_tile(t, par):
                act.wait_ge(sem("tile_done"), t + (q0 + 1))
                act.wait_ge(sem("ssm_conv"), t + 1)
                act.wait_ge(sem("pads_ready"), 2)
                act.activation(halves(pad[par][:, 3:]), pair2(q0 + par), ACT.Copy).then_inc(sem("tile_read"), 1)

            def ssm_silu(t):
                act.wait_ge(sem("ssm_conv"), t + 3)
                act.wait_ge(sem("pads_ready"), 2)
                x = xbc[:, t, :] if isinstance(t, int) else xbc[:, bass.ds(t, 1), :].rearrange("p o n -> p (o n)")
                act.activation(x, x, ACT.Silu).then_inc(sem("ssm_silu"), 1)

            ssm_tile(0, 0)
            with act.Fori(0, SSD_X - 1) as i:
                for j in range(2):
                    ssm_tile(i * 2 + (j + 1), 1 - j)
                    ssm_silu(i * 2 + j)
            ssm_tile(2 * SSD_X - 1, 1)
            ssm_silu(2 * SSD_X - 2)
            ssm_silu(2 * SSD_X - 1)
            act.wait_ge(sem("dt_arg"), 1)
            act.activation(sb2, sb2, ACT.Exp).then_inc(sem("dt_exp"), 1)
            act.wait_ge(sem("dt_one"), 1)
            act.activation(sc2, sc2, ACT.Ln)
            act.activation(egt2[:, 0, :], pcol("a_log2", 0, SSD_H), ACT.Exp).then_inc(sem("dt_ln"), 1)
            act.wait_ge(sem("tail_arg"), 1)
            act.activation(tail2, tail2, ACT.Exp)
            act.activation(egt2, gt2_, ACT.Exp).then_inc(sem("tail_ready"), 1)
            SSD = [(c, g) for c in range(len(CH2)) for g in range(SSD_G)]
            for n, (c, g) in enumerate(SSD):
                cnt = CH2[c][1]
                bank = ps[:, 2 * (n % 2), :].rearrange("p (h n) -> p h n", h=4)
                act.wait_ge(sem("ssd_in_done"), n + 1)
                if n >= 2:
                    act.wait_ge(sem("ssd_pool"), n - 1)
                act.activation(eg2[n % 2][:, :, 0:cnt], bank[:, :, 0:cnt], ACT.Exp).then_inc(sem("ssd_eg"), 1)
                act.wait_ge(sem("ssd_diff"), n + 1)
                d = decay2[n % 2][0:cnt, :, 0:cnt]
                act.activation(d, d, ACT.Exp).then_inc(sem("ssd_decay"), 1)
            for g in range(SSD_G):
                for e in range(2):
                    act.wait_ge(sem("gated"), 2 * g + e + 1)
                    if g:
                        act.wait_ge(sem("group_sums"), g)
                    act.activation(gsq[e], xbc[:, 2 * g + e, :], ACT.Square).then_inc(sem("group_squares"), 1)
                act.wait_ge(sem("group_sums"), g + 1)
                if g >= 2:
                    act.wait_ge(sem("mix2_ready"), 2 * (g - 1))
                act.activation(halves(groot[g % 2]), ps[:, 2 * (g % 2):2 * (g % 2) + 2, 0:HALF], ACT.Sqrt, bias=eps,
                               scale=1.0 / (2 * P)).then_inc(sem("group_root"), 1)
            product_out("out2", m2_out, 8)
            ffn("up2", "down2", 10, 1)

        INV_2PI = float(np.float32(1 / (2 * np.pi)))
        ROUND = 12582912.0
        PI_A = 6.28125
        PI_B = float(np.float32(np.floor((2 * np.pi - PI_A) * 2 ** 21) / 2 ** 21))
        PI_C = float(np.float32(2 * np.pi - PI_A - PI_B))

        @block.vector
        def _(dve):
            def ts(out, x, s1, s2, op0, op1=None):
                return dve.tensor_scalar(out, x, s1, s2, op0, op1) if op1 is not None else dve.tensor_scalar(out, x, s1, None, op0)

            def tt(out, x, y, op):
                return dve.tensor_tensor(out, x, y, op)

            def stt(out, x, s, y, op0, op1):
                return dve.scalar_tensor_tensor(out=out, in0=x, scalar=s, in1=y, op0=op0, op1=op1)

            mul, add, sub, lo_, hi_ = ALU.mult, ALU.add, ALU.subtract, ALU.min, ALU.max

            def norm_apply(n, gain, src, dst, ncols, shift=None):
                dve.wait_ge(sem("root_ready"), n + 1)
                dve.reciprocal(rs[:, 0:ncols], rs[:, 0:ncols])
                dve.drain()
                for k in range(DT):
                    m = stt(dst(k), src(k), gain(k), rs[:, 0:ncols], mul, mul)
                    if shift is None:
                        if k == DT - 1:
                            m.then_inc(sem("normed"), DT)
                if shift is not None:
                    dve.drain()
                    for k in range(DT):
                        m = ts(dst(k), dst(k), shift(k), None, add)
                    m.then_inc(sem("normed"), DT)
                dve.drain().then_inc(sem("norm_applied"), 1)

            def conv(out, buf, taps, w, bias, ncols):
                n = taps - 1
                if bias is None:
                    ts(out, buf[:, n:n + ncols], w(n), None, mul)
                else:
                    ts(out, buf[:, n:n + ncols], w(n), bias, mul, add)
                for t in range(n - 1, -1, -1):
                    dve.drain()
                    m = stt(out, buf[:, t:t + ncols], w(t), out, mul, add)
                return m

            def log1p_args(x, m, e):
                ts(m, x, 0.0, None, hi_)
                ts(e, x, -1.0, None, mul)
                dve.drain()
                return tt(e, e, x, lo_)

            dve.memset(zeros, 0.0).then_inc(sem("zeros_ready"), 1)
            dve.memset(tmp[:, 0, 0:3], 0.0).then_inc(sem("tile_read"), 1)
            dve.memset(tmp[:, 1, 0:3], 0.0).then_inc(sem("tile_read"), 1)
            dve.drain().then_inc(sem("pads_ready"), 1)
            dve.wait_ge(sem("inputs_loaded"), INPUTS)
            S = lambda n: s5s[:, n, :]
            lr, li = pcol("lam_re", 0, 16), pcol("lam_im", 0, 16)
            dve.wait_ge(sem("s5_step"), 1)
            tt(S(5), lr, S(0), mul)
            tt(S(1), li, S(0), mul)
            dve.drain()
            ts(S(2), S(1), INV_2PI, ROUND, mul, add)
            dve.drain()
            ts(S(2), S(2), -ROUND, None, add)
            dve.drain()
            for part in (PI_A, PI_B, PI_C):
                stt(S(1), S(2), -part, S(1), mul, add)
                dve.drain()
            ts(S(3), S(1), float(np.float32(3.1415925)), -float(np.float32(3.1415925)), lo_, hi_)
            dve.drain()
            ts(S(4), S(3), -1.0, None, mul)
            dve.drain()
            tt(S(4), S(4), S(3), hi_)
            dve.drain()
            ts(S(4), S(4), -1.0, float(np.float32(np.pi / 2)), mul, add).then_inc(sem("s5_angle"), 1)
            dve.wait_ge(sem("s5_trig"), 1)
            tt(S(15), S(6), S(7), mul)
            tt(S(10), S(6), S(8), mul)
            tt(S(11), lr, lr, mul)
            tt(S(17), li, li, mul)
            dve.drain()
            ts(S(9), S(15), -1.0, None, add)
            tt(S(11), S(11), S(17), add)
            dve.drain()
            dve.reciprocal(S(12), S(11))
            tt(S(17), S(9), lr, mul)
            tt(S(18), S(10), li, mul)
            tt(S(19), S(10), lr, mul)
            tt(S(20), S(9), li, mul)
            dve.drain()
            tt(S(17), S(17), S(18), add)
            tt(S(19), S(19), S(20), sub)
            dve.drain()
            tt(S(13), S(17), S(12), mul)
            tt(S(14), S(19), S(12), mul)
            dve.drain()
            wide = lambda x: x.unsqueeze(2).broadcast_to([P, S5_TILES, 32])
            for n, (p_, q_) in enumerate(((13, 14), (14, 13))):
                t1, t2 = p5[0].rearrange("p (j n) -> p j n", n=32), p5[1].rearrange("p (j n) -> p j n", n=32)
                tt(t1, s5c[0], wide(S(p_)), mul)
                tt(t2, s5c[1], wide(S(q_)), mul)
                dve.drain()
                if n == 0:
                    tt(s5ck[0], t1, t2, sub)
                else:
                    tt(t1, t1, t2, add)
                    dve.drain()
                    ts(s5ck[1], t1, -1.0, None, mul)
                dve.drain()
            dve.tensor_copy(S(15), S(7))
            dve.tensor_copy(S(16), S(8))
            for tab, size in ((fine, 32), (coarse, 16)):
                dve.memset(tab[0][:, :, 0:1], 1.0)
                dve.memset(tab[1][:, :, 0:1], 0.0)
                n = 1
                while n < size:
                    dve.drain()
                    wc, ws = (S(x).unsqueeze(2).broadcast_to([P, S5_TILES, n]) for x in (15, 16))
                    t = [p5[x][:, 0:S5_TILES * n].rearrange("p (j n) -> p j n", n=n) for x in range(4)]
                    tt(t[0], tab[0][:, :, 0:n], wc, mul)
                    tt(t[1], tab[1][:, :, 0:n], ws, mul)
                    tt(t[2], tab[0][:, :, 0:n], ws, mul)
                    tt(t[3], tab[1][:, :, 0:n], wc, mul)
                    tt(S(17), S(15), S(15), mul)
                    tt(S(18), S(16), S(16), mul)
                    tt(S(19), S(15), S(16), mul)
                    dve.drain()
                    tt(tab[0][:, :, n:2 * n], t[0], t[1], sub)
                    tt(tab[1][:, :, n:2 * n], t[2], t[3], add)
                    tt(S(15), S(17), S(18), sub)
                    ts(S(16), S(19), 2.0, None, mul)
                    n *= 2
                dve.drain()
            dve.drain().then_inc(sem("powers_ready"), 1)
            L = lambda n: lam8[:, n, :]
            ts(L(3), pcol("lam", 0, LRU), -1.0, None, mul)
            dve.drain()
            log1p_args(L(3), L(0), L(1)).then_inc(sem("lam_arg"), 1)
            dve.wait_ge(sem("lam_exp"), 1)
            ts(L(2), L(1), 1.0, None, add)
            dve.drain()
            stt(L(3), L(2), -1.0, L(1), add, sub)
            dve.drain()
            dve.reciprocal(L(1), L(2))
            dve.drain()
            tt(L(3), L(3), L(1), mul).then_inc(sem("lam_one"), 1)
            dve.wait_ge(sem("lam_ln"), 1)
            tt(L(2), L(2), L(3), sub)
            dve.drain()
            tt(L(2), L(2), L(0), add)
            dve.drain()
            ts(L(0), L(2), -8.0, None, mul)
            ts(L(3), L(2), 8.0, None, mul)
            dve.wait_ge(sem("tile_read"), 2 + 48)
            stt(modg[:, 0:DT], mod[:, DT:2 * DT], 1.0, pcol("norm1_g", 0, DT), add, mul)
            stt(modg[:, DT:2 * DT], mod[:, 4 * DT:5 * DT], 1.0, pcol("norm2_g", 0, DT), add, mul)
            dve.drain()
            norm_apply(0, lambda k: modg[:, k:k + 1], lambda k: h[:, k, META:T2], lambda k: u[:, k, 0:SEQ], SEQ,
                       lambda k: mod[:, k:k + 1])
            q0 = Q0["in1"]
            for j in range(S5_TILES):
                if j < 12:
                    dve.wait_ge(sem("tile_read"), q0 + NS5 + j + 3)
                    if j == 8:
                        dve.wait_ge(sem("rows_zeroed"), 16)
                    conv(qkv[:, j, :], cbuf[j % 2], CONV_C, lambda t: pcol("conv_w", 12 * t + j), None, SEQ
                         ).then_inc(sem("conv_done"), 1)
                dve.wait_ge(sem("table_ready"), j + 1)
                dve.wait_ge(sem("s5_in_done"), j + 1)
                C, Sn = table[j % 2]
                dve.drain()
                bu, bw = ps[:, 4, 0:SEQ], ps[:, 5, 0:SEQ]
                tt(f5[0], bu, C, mul)
                tt(p5[0], bw, Sn, mul)
                tt(f5[1], bw, C, mul)
                tt(p5[1], bu, Sn, mul).then_inc(sem("s5_in_read"), 1)
                dve.drain()
                tt(f5[0], f5[0], p5[0], add)
                tt(f5[1], f5[1], p5[1], sub)
                dve.drain()
                rho = s5s[:, 6, j:j + 1].broadcast_to([P, SEQ])
                dve.tensor_tensor_scan(z5[0], rho, f5[0], 0.0, mul, add)
                dve.tensor_tensor_scan(z5[1], rho, f5[1], 0.0, mul, add)
                dve.drain()
                tt(p5[0], z5[0], C, mul)
                tt(p5[1], z5[1], Sn, mul)
                tt(p5[2], z5[0], Sn, mul)
                tt(p5[3], z5[1], C, mul).then_inc(sem("table_used"), 1)
                dve.drain()
                if j >= 2:
                    dve.wait_ge(sem("s5_out_done"), j - 1)
                tt(st5[j % 2][0], p5[0], p5[1], sub)
                tt(st5[j % 2][1], p5[2], p5[3], add).then_inc(sem("s5_state_ready"), 1)
                if j >= 4 and j % 4 == 0:
                    t = j // 4 - 1
                    dve.wait_ge(sem("s5_out_done"), 4 * t + 4)
                    stt(y5[:, t, :], us5[:, t, :], pcol("s5_d", t), ps[:, 6 + t % 2, 0:SEQ], mul, add
                        ).then_inc(sem("y5_ready"), 1)
            dve.wait_ge(sem("s5_out_done"), S5_TILES)
            stt(y5[:, 3, :], us5[:, 3, :], pcol("s5_d", 3), ps[:, 7, 0:SEQ], mul, add).then_inc(sem("y5_ready"), 1)
            for t in range(NS5):
                dve.wait_ge(sem("tile_read"), Q0["glu"] + t + 3)
                tt(mix[:, t, :], y5[:, t, :], sig, mul).then_inc(sem("mix1_ready"), 1)
            for k in range(8):
                dve.wait_ge(sem("l2_read"), k + 1)
                dve.reciprocal(l2r[:, k, :], l2r[:, k, :])
                dve.drain()
                stt(qkv[:, k, :], qkv[:, k, :], float(P) ** -0.5 if k < HEADS else 1.0, l2r[:, k, :], mul, mul
                    ).then_inc(sem("qk_ready"), 1)
            ab = ps[:, 1, 0:32].rearrange("p (c h) -> p c h", c=CHUNKS)
            ch = lambda x: x.rearrange("p (c h) -> p c h", c=CHUNKS)
            per_head = lambda x: x.unsqueeze(1).broadcast_to([P, CHUNKS, HEADS])
            dve.wait_ge(sem("gates_done"), 1)
            tt(ch(sp1), ab[:, :, 0:HEADS], per_head(pcol("dt_bias", 0, HEADS)), add)
            dve.drain()
            ts(gate, sp1, 0.0, None, hi_)
            ts(sp2, sp1, -1.0, None, mul)
            dve.drain()
            tt(sp2, sp2, sp1, lo_).then_inc(sem("gate_arg"), 1)
            dve.wait_ge(sem("gate_exp"), 1)
            ts(sp3, sp2, 1.0, None, add)
            dve.drain()
            stt(bcs, sp3, -1.0, sp2, add, sub)
            dve.reciprocal(etail, sp3)
            dve.drain()
            tt(bcs, bcs, etail, mul).then_inc(sem("gate_one"), 1)
            dve.wait_ge(sem("gate_ln"), 1)
            tt(sp3, sp3, bcs, sub)
            dve.drain()
            tt(gate, gate, sp3, add)
            dve.drain()
            stt(ch(gate), ch(gate), -1.0, per_head(sp4[:, 0:HEADS]), mul, mul).then_inc(sem("gate_ready"), 1)
            dve.wait_ge(sem("csum_done"), 1)
            dve.wait_ge(sem("beta_ready"), 1)
            dve.tensor_copy(csum, ps[:, 1, 64:80])
            dve.tensor_copy(gtot, ps[:, 1, 96:112]).then_inc(sem("csum_read"), 1)
            dve.drain()
            tt(etail, gtot, csum, sub).then_inc(sem("csum_copied"), 1)
            dve.wait_ge(sem("gate_exps"), 1)
            tt(bcs, beta, ecs, mul)
            dve.drain()
            heads = lambda b: ps[:, b, :].rearrange("p (h n) -> p h n", h=HEADS)
            for c in range(CHUNKS):
                per_tok = lambda x: x[:, 4 * c:4 * c + 4].unsqueeze(2).broadcast_to([P, HEADS, P])
                all_heads = lambda x: x.unsqueeze(1).broadcast_to([P, HEADS, P])
                dve.wait_ge(sem("chunk_done"), c + 1)
                if c:
                    dve.drain()
                tt(dtmp, heads(2), per_tok(csum), sub)
                dve.drain()
                ts(dtmp, dtmp, 0.0, None, lo_).then_inc(sem("diff_ready"), 1)
                dve.wait_ge(sem("turned"), c + 1)
                tt(kb_g[:, c], heads(4), per_tok(bcs), mul)
                tt(k_tail[:, c], heads(4), per_tok(etail), mul)
                tt(v_b[:, c], heads(5), per_tok(beta), mul).then_inc(sem("turned_read"), 1)
                dve.wait_ge(sem("decay_ready"), c + 1)
                tt(amat[:, c], dtmp, heads(0), mul)
                tt(qk_d[:, c], dtmp, heads(1), mul)
                dve.drain()
                tt(qk_d[:, c], qk_d[:, c], all_heads(upto), mul)
                tt(amat[:, c], amat[:, c], heads(3), mul).then_inc(sem("a_ready"), 1)
                dve.wait_ge(sem("egb_ready"), c + 1)
                tt(q_dec[:, c], qkv[:, 0:HEADS, c * P:(c + 1) * P], egb, mul).then_inc(sem("chunk_read"), 1)
            dve.drain()
            dve.wait_ge(sem("turned"), CHUNKS)
            dve.wait_ge(sem("chunk_done"), CHUNKS)
            for c in range(CHUNKS):
                for x in (x_inv, y_inv):
                    m = dve.tensor_copy(x[:, c], ident.unsqueeze(1).broadcast_to([P, HEADS, P]))
                m.then_inc(sem("inverse_ready"), 1)
            dve.drain()
            for v in range(LEVELS):
                for c in range(CHUNKS):
                    dve.wait_ge(sem("xax_done"), CHUNKS * v + c + 1)
                    b = 4 + 2 * (c % 2)
                    tt(x_inv[:, c], x_inv[:, c], heads(b), sub)
                    tt(y_inv[:, c], y_inv[:, c], heads(b + 1), sub).then_inc(sem("inverse_ready"), 1)
                dve.drain()
            dve.memset(state, 0.0).then_inc(sem("state_ready"), 1)
            for c in range(CHUNKS):
                dve.wait_ge(sem("seen_done"), c + 1)
                if c:
                    dve.wait_ge(sem("chunk_out_done"), c)
                tt(v_new, val[:, c], heads(4), sub).then_inc(sem("v_new_ready"), 1)
                dve.wait_ge(sem("chunk_out_done"), c + 1)
                tt(state, state, egt[:, 4 * c:4 * c + 4].unsqueeze(2).broadcast_to([P, HEADS, P]), mul)
                dve.drain()
                m = tt(state, state, heads(5), add)
                if c < CHUNKS - 1:
                    m.then_inc(sem("state_ready"), 1)
                dve.drain()
            for k in range(HEADS):
                dve.wait_ge(sem("o_norm_read"), k + 1)
                dve.reciprocal(rs[:, 0:SEQ], rs[:, 0:SEQ])
                dve.drain()
                stt(mix[:, NS5 + k, :], o_gdn[:, k, :], pcol("gdn_norm_g"), rs[:, 0:SEQ], mul, mul)
                dve.drain()
                tt(mix[:, NS5 + k, :], mix[:, NS5 + k, :], z1[:, k, :], mul).then_inc(sem("mix1_ready"), 1)
            for t in range(DT):
                dve.wait_ge(sem("tile_done"), Q0["out1"] + t + 1)
                stt(h[:, t, META:T2], pair(Q0["out1"] + t), mod[:, 2 * DT + t:2 * DT + t + 1], h[:, t, META:T2], mul, add
                    ).then_inc(sem("tile_read"), 1)

            norm_apply(1, lambda k: modg[:, DT + k:DT + k + 1], lambda k: h[:, k, META:T2], lambda k: u[:, k, 0:SEQ], SEQ,
                       lambda k: mod[:, 3 * DT + k:3 * DT + k + 1])
            dve.wait_ge(sem("router_done"), 1)
            dve.tensor_copy(logit, ps[:, 0, 0:144].rearrange("p (c n) -> p c n", c=CHUNKS))
            dve.drain()
            lg, le = logit[:, :, 0:GROUPS], logit[:, :, GROUPS:]
            over = lambda x, n: x.unsqueeze(2).broadcast_to([P, CHUNKS, n])
            const = lambda name, n: ccol(name, 0, n).unsqueeze(1).broadcast_to([P, CHUNKS, n])

            def first_max(x, n, rank, m, one, t, r):
                dve.tensor_reduce(m, x, AX, hi_)
                dve.drain()
                tt(t, x, over(m, n), ALU.is_equal)
                dve.drain()
                tt(t, t, const(rank, n), mul)
                dve.drain()
                dve.tensor_reduce(r, t, AX, hi_)
                dve.drain()
                tt(one, t, over(r, n), ALU.is_equal)

            first_max(lg, GROUPS, "grp_rank", r1[0], r4[0], r4[2], r1[1])
            tt(r4[1], lg, over(r1[0], GROUPS), sub).then_inc(sem("grp_arg"), 1)
            dve.drain()
            ts(r4[2], r4[0], -1.0, FAR, add, mul)
            dve.drain()
            eight = lambda x: x.unsqueeze(3).broadcast_to([P, CHUNKS, GROUPS, 8])
            by_group = lambda x: x.rearrange("p c (g e) -> p c g e", g=GROUPS)
            tt(by_group(r32[0]), by_group(le), eight(r4[0]), mul)
            dve.drain()
            tt(by_group(r32[0]), by_group(r32[0]), eight(r4[2]), add)
            dve.drain()
            first_max(r32[0], EXPERTS, "exp_rank", r1[2], r32[1], r32[4], r1[1])
            dve.drain()
            stt(r32[2], r32[1], -2.0 * FAR, r32[0], mul, add)
            dve.drain()
            first_max(r32[2], EXPERTS, "exp_rank", r1[3], r32[3], r32[4], r1[1])
            tt(r1[6], r1[3], r1[2], sub).then_inc(sem("top_arg"), 1)
            dve.drain()
            tt(r32[5], r32[1], r32[3], add).then_inc(sem("chosen_ready"), 1)
            dve.wait_ge(sem("grp_exp"), 1)
            dve.tensor_reduce(r1[4], r4[1], AX, add)
            dve.wait_ge(sem("top_exp"), 1)
            ts(r1[5], r1[6], 1.0, None, add)
            dve.drain()
            tt(r1[4], r1[4], r1[5], mul)
            dve.drain()
            dve.reciprocal(r1[7], r1[4])
            dve.drain()
            tt(r1[8], r1[7], r1[6], mul)
            dve.wait_ge(sem("places_done"), 1)
            dve.tensor_copy(e32[0], ps[:, 1, 128:160])
            dve.memset(e32[4], 1.0)
            dve.drain()
            ts(e32[1], e32[0], 0.0, None, ALU.is_gt)
            for v in (1, 2, 3):
                dve.drain()
                stt(e32[1], e32[0], 128.0 * v, e32[1], ALU.is_gt, add)
            dve.drain()
            dve.tensor_tensor_scan(e32[2], e32[4], e32[1], 0.0, mul, add)
            dve.drain()
            tt(e32[2], e32[2], e32[1], sub)
            dve.drain()
            ts(e32[3], e32[2], ccol("row"), None, ALU.is_le)
            ts(e32[5], e32[2], float(P), None, mul)
            dve.drain()
            dve.tensor_reduce(ecol[:, 1:2], e32[3], AX, add)
            dve.drain()
            ts(ecol[:, 0:1], ecol[:, 1:2], -1.0, None, add).then_inc(sem("ecol_ready"), 1)
            tt(r32[4], ps[:, 1, 0:128].rearrange("p (c n) -> p c n", c=CHUNKS),
               e32[5].unsqueeze(1).broadcast_to([P, CHUNKS, EXPERTS]), add)
            dve.drain()
            tt(r32[0], r32[4], r32[1], mul)
            tt(r32[2], r32[4], r32[3], mul)
            dve.drain()
            dve.tensor_reduce(slots[:, 0:CHUNKS], r32[0], AX, add)
            dve.tensor_reduce(slots[:, CHUNKS:], r32[2], AX, add)
            dve.drain()
            dve.tensor_copy(slot_id, slots).then_inc(sem("slots_ready"), 1)
            dve.wait_ge(sem("erow_done"), 1)
            dve.tensor_copy(eid[0:1, :], ps[0:1, 5, 0:P]).then_inc(sem("expert_ids"), 1)
            dve.drain().then_inc(sem("erow_read"), 1)

            def hidden(b, p, count):
                dve.wait_ge(sem("silu_ready"), count)
                if not isinstance(b, int) or b >= 2:
                    dve.wait_ge(sem("ht_done"), FREE + b - 1)
                tt(h_b[:, p, :], silu_b[:, p, :], ps[:, p, D_EXPERT:], mul).then_inc(sem("hidden_ready"), 1)

            def hidden_out_of_psum(b):
                dve.wait_ge(sem("ht_done"), FREE + b + 1)
                dve.wait_ge(sem("dn_done"), FREE + b)
                dve.tensor_copy(ht_b, ps[:, 4, 0:2 * P].rearrange("p (k n) -> p k n", k=2)).then_inc(sem("ht_read"), 1)

            def rows_ready(b, p, stored):
                dve.wait_ge(sem("dn_done"), FREE + b + 1)
                dve.wait_ge(sem(f"rows_stored{p}"), stored)
                dve.tensor_copy(yb[p].rearrange("p (s n) -> p s n", s=2), ps[:, 5:7, :]).then_inc(sem("dn_read"), 1)

            dve.drain().then_inc(sem("rows_stored0"), 16 * FREE)
            dve.drain().then_inc(sem("rows_stored1"), 16 * FREE)
            dve.drain().then_inc(sem("hidden_ready"), FREE)
            dve.drain().then_inc(sem("ht_read"), FREE)
            dve.drain().then_inc(sem("dn_read"), FREE)
            hidden(0, 0, 1)
            with dve.Fori(0, BLOCKS // 2 - 1) as i:
                for p in range(2):
                    b = i * 2 + p
                    hidden_out_of_psum(b)
                    dve.wait_ge(sem("silu_ready"), b + 2)
                    dve.wait_ge(sem("ht_done"), FREE + b)
                    tt(h_b[:, 1 - p, :], silu_b[:, 1 - p, :], ps[:, 1 - p, D_EXPERT:], mul
                       ).then_inc(sem("hidden_ready"), 1)
                    rows_ready(b, p, i * 16 + 16 * FREE)
            hidden_out_of_psum(BLOCKS - 2)
            hidden(BLOCKS - 1, 1, BLOCKS)
            rows_ready(BLOCKS - 2, 0, 8 * BLOCKS - 16 + 16 * FREE)
            hidden_out_of_psum(BLOCKS - 1)
            rows_ready(BLOCKS - 1, 1, 8 * BLOCKS - 16 + 16 * FREE)
            for c in range(CHUNKS):
                dve.wait_ge(sem("rows_gathered"), 16 * 8)
                ts(moe[:, c, :], y1[:, c, :], r1[7][:, c:c + 1], None, mul)
                dve.drain()
                stt(moe[:, c, :], y2[:, c, :], r1[8][:, c:c + 1], moe[:, c, :], mul, add).then_inc(sem("moe_ready"), 1)
            for k in range(DT):
                dve.wait_ge(sem("moe_turned"), k + 1)
                stt(h[:, k, META:T2], ps[:, k % 2, :], mod[:, 5 * DT + k:5 * DT + k + 1], h[:, k, META:T2], mul, add
                    ).then_inc(sem("moe_added"), 1)
            dve.drain()
            norm_apply(2, lambda k: pcol("normf_g", k), lambda k: h[:, k, META:T2], lambda k: h[:, k, META:T2], SEQ)

            norm_apply(3, lambda k: pcol("pre0", k), lambda k: h[:, k, :], lambda k: u[:, k, :], T2)
            for b in range(2):
                dve.memset(tmp[:, b, 0:3], 0.0)
            dve.drain().then_inc(sem("pads_ready"), 1)
            dve.drain().then_inc(sem("ffn_conv"), 2)
            dve.drain().then_inc(sem("ssm_conv"), 2)
            q0 = Q0["in0"]

            def lru_tail(i):
                b = i % 2
                dve.wait_ge(sem("lru_decay"), i + 1)
                tt(r_lru[:, b, :], a_lru[:, b, :], a_lru[:, b, :], mul)
                tt(i_lru[:, b, :], i_lru[:, b, :], x_lru[:, b, :], mul)
                dve.drain()
                stt(t_lru[:, b, :], r_lru[:, b, :], 1.0, t_lru[:, b, :], add, mul).then_inc(sem("lru_square"), 1)
                dve.wait_ge(sem("lru_root"), i + 1)
                tt(i_lru[:, b, :], i_lru[:, b, :], t_lru[:, b, :], mul)
                dve.drain()
                dve.tensor_tensor_scan(r_lru[:, b, :], a_lru[:, b, :], i_lru[:, b, :], 0.0, mul, add)
                dve.drain()
                tt(mix0[:, i, :], g_lru[:, b, :], r_lru[:, b, :], mul).then_inc(sem("lru_out"), 1)

            for i in range(LRU):
                dve.wait_ge(sem("tile_read"), q0 + 2 * i + 1 + 3)
                dve.drain()
                conv(x_lru[:, i % 2, :], pad[i % 2], CONV_C, lambda t: pcol("lru_w", 8 * t + i), pcol("lru_b", i), T2
                     ).then_inc(sem("lru_conv"), 1)
                if i:
                    lru_tail(i - 1)
            lru_tail(LRU - 1)
            ATT = [(c, hp) for c in range(len(CH2)) for hp in range(Q_TILES)]
            slope = lambda head: float(np.float32(2.0) ** np.float32(-8.0 * (head + 1) / Q_HEADS))

            def normalize(n):
                c, hp = ATT[n]
                cnt, nk, b = CH2[c][1], (META, META + P, META + 2 * P, META + 2 * P, META + 2 * P)[c], n % 2
                st = lambda k: stat[0:cnt, b, k, :]
                dve.wait_ge(sem("exp_ready"), n + 1)
                tt(st(2), st(2), st(3), add)
                dve.drain()
                dve.reciprocal(st(4), st(2))
                dve.drain()
                for e in range(2):
                    x = prob[0:cnt, b, e, 0:nk]
                    m = ts(x, x, stat[0:cnt, b, 4, e:e + 1], None, mul)
                m.then_inc(sem("prob_ready"), 1)

            for n in range(len(ATT) + 1):
                if n < len(ATT):
                    c, hp = ATT[n]
                    cnt, nk, b = CH2[c][1], (META, META + P, META + 2 * P, META + 2 * P, META + 2 * P)[c], n % 2
                    dist = ccol(("dist0", "dist1", "dist2", "dist2", "dist2")[c], 0, nk)[0:cnt, :]
                    dve.wait_ge(sem("scores_done"), n + 1)
                    if n >= 2:
                        dve.wait_ge(sem("prob_turned"), n - 1)
                    for e in range(2):
                        m = stt(prob[0:cnt, b, e, 0:nk], dist, -slope(2 * hp + e), ps[0:cnt, 2 * b + e, 0:nk], mul, add)
                    m.then_inc(sem("scores_read"), 1)
                    dve.drain()
                    st = lambda k: stat[0:cnt, b, k, :]
                    dve.tensor_reduce(st(0), prob[0:cnt, b, :, 0:nk], AX, hi_)
                    dve.drain()
                    tt(st(0), st(0), pcol("sinks", 2 * hp, 2)[0:cnt, :], hi_)
                    dve.drain()
                    ts(st(1), st(0), -1.0, None, mul).then_inc(sem("max_ready"), 1)
                if n:
                    normalize(n - 1)

            def residual(n, src, gain):
                dve.wait_ge(sem("root_ready"), n + 1)
                dve.wait_ge(sem("tile_read"), tiles_of[n])
                dve.reciprocal(rs[:, :], rs[:, :])
                dve.drain()
                for k in range(DT):
                    stt(src[:, k, :], src[:, k, :], gain(k), rs[:, :], mul, mul)
                dve.drain().then_inc(sem("norm_applied"), 1)
                for k in range(DT):
                    tt(h[:, k, :], h[:, k, :], src[:, k, :], add).then_inc(sem("h_updated"), 1)
                dve.drain()

            tiles_of = {4: Q0["out0"] + DT + 2, 6: Q0["down0"] + DT + 2, 8: Q0["out2"] + DT + 2, 10: Q0["down2"] + DT + 2}

            def conv_dyn(out, buf, taps, cols, n_cols, bias, i):
                n = taps - 1
                col = lambda c: par[:, bass.ds(i + c, 1)]
                ts(out, buf[:, n:n + T2], col(cols + n * n_cols), col(bias), mul, add)
                for t in range(n - 1, -1, -1):
                    dve.drain()
                    m = stt(out, buf[:, t:t + T2], col(cols + t * n_cols), out, mul, add)
                return m

            def ffn(up, n, layer, run):
                norm_apply(n - 1, lambda k: pcol(f"fpre{layer}", k), lambda k: h[:, k, :], lambda k: u[:, k, :], T2)
                q0 = Q0[up]
                with dve.Fori(0, FF // 2) as i:
                    for j in range(2):
                        for e in range(2):
                            dve.drain()
                            dve.wait_ge(sem("tile_read"), i * 4 + (q0 + 2 * j + e + 3))
                            conv_dyn((gact, uact)[e], pad[e][:, 1:], CONV_F, PCOL[f"fw{layer}"] + 2 * j + e, 2 * FF,
                                     PCOL[f"fb{layer}"] + 2 * j + e, i * 4).then_inc(sem("ffn_conv"), 1)
                        dve.drain()
                        dve.wait_ge(sem("ffn_gelu"), i * 2 + (FF * run + j + 1))
                        tt(prod[:, bass.ds(i * 2 + j, 1), :].rearrange("p o n -> p (o n)"), gact, uact, mul
                           ).then_inc(sem("prod_ready"), 1)
                residual(n, m_out, lambda k: pcol(f"fpost{layer}", k))

            residual(4, m_out, lambda k: pcol("post0", k))
            ffn("up0", 6, 0, 0)
            norm_apply(7, lambda k: pcol("pre2", k), lambda k: h[:, k, :], lambda k: u[:, k, :], T2)
            q0 = Q0["in2"] + SSD_X
            with dve.Fori(0, SSD_X) as i:
                for j in range(2):
                    dve.wait_ge(sem("tile_read"), i * 2 + (q0 + j + 3))
                    conv_dyn(xbc[:, bass.ds(i * 2 + j, 1), :].rearrange("p o n -> p (o n)"), pad[j], CONV_C,
                             PCOL["ssm_w"] + j, 2 * SSD_X, PCOL["ssm_b"] + j, i * 2).then_inc(sem("ssm_conv"), 1)
            nc5 = len(CH2)
            chunks = lambda x: x.unsqueeze(1).broadcast_to([P, nc5, SSD_H])
            psd = lambda b: ps[:, b, 0:nc5 * SSD_H].rearrange("p (c n) -> p c n", c=nc5)
            dve.wait_ge(sem("dt_done"), 1)
            tt(sa2, psd(4), chunks(pcol("dt_bias2", 0, SSD_H)), add)
            dve.drain()
            log1p_args(sa2, dt2, sb2).then_inc(sem("dt_arg"), 1)
            dve.wait_ge(sem("dt_exp"), 1)
            ts(sc2, sb2, 1.0, None, add)
            dve.drain()
            stt(sa2, sc2, -1.0, sb2, add, sub)
            dve.reciprocal(tail2, sc2)
            dve.drain()
            tt(sa2, sa2, tail2, mul).then_inc(sem("dt_one"), 1)
            dve.wait_ge(sem("dt_ln"), 1)
            tt(sc2, sc2, sa2, sub)
            dve.drain()
            tt(dt2, dt2, sc2, add)
            dve.drain()
            stt(da2, dt2, -1.0, chunks(egt2[:, 0, :]), mul, mul).then_inc(sem("da_ready"), 1)
            dve.wait_ge(sem("cs2_done"), 1)
            dve.tensor_copy(cs2, psd(5))
            dve.tensor_copy(gt2_, psd(6)).then_inc(sem("cs2_read"), 1)
            dve.drain()
            tt(tail2, gt2_, cs2, sub)
            dve.drain()
            ts(tail2, tail2, 0.0, None, lo_).then_inc(sem("tail_arg"), 1)
            SSD = [(c, g) for c in range(nc5) for g in range(SSD_G)]

            def ssd_mask(n):
                c, g = SSD[n]
                cnt, b = CH2[c][1], n % 2
                dve.wait_ge(sem("ssd_decay"), n + 1)
                d = decay2[b][0:cnt, :, 0:cnt]
                tt(d, d, cbm[0:cnt, b, 0:cnt].unsqueeze(1).broadcast_to([cnt, 4, cnt]), mul).then_inc(sem("ssd_dve"), 1)

            def ssd_result(n):
                c, g = SSD[n]
                (lo, cnt), b = CH2[c], n % 2
                dve.wait_ge(sem("ssd_out_done"), n + 1)
                st = st2[:, 4 * g:4 * g + 4, :]
                new = ps[:, 6 + b, 0:256].rearrange("p (h n) -> p h n", h=4)
                if c:
                    tt(st, st, egt2[:, c, 4 * g:4 * g + 4].unsqueeze(2).broadcast_to([P, 4, HEAD]), mul)
                for e in range(2):
                    x = xbc[:, 2 * g + e, lo:lo + cnt]
                    stt(x, x, pcol("d_skip", 2 * g + e), ps[:, 4 + b, P * e:P * e + cnt], mul, add)
                if c:
                    dve.drain()
                    m = tt(st, st, new, add)
                else:
                    m = dve.tensor_copy(st, new)
                m.then_inc(sem("st2_ready"), 1)
                dve.drain().then_inc(sem("ssd_out_read"), 1)

            dve.wait_ge(sem("tail_ready"), 1)
            for n in range(len(SSD) + 2):
                if n < len(SSD):
                    c, g = SSD[n]
                    (lo, cnt), b = CH2[c], n % 2
                    dve.wait_ge(sem("ssd_in_done"), n + 1)
                    if n >= 2:
                        dve.wait_ge(sem("ssd_out_done"), n - 1)
                    bank = ps[:, 2 * b + 1, :]
                    tt(cbm[0:cnt, b, 0:cnt], bank[0:cnt, 0:cnt], upto[0:cnt, 0:cnt], mul)
                    dve.tensor_copy(b_tok[0:cnt, b, :], bank[0:cnt, P:2 * P])
                    tt(xdt[b][0:cnt], bank[0:cnt, 2 * P:].rearrange("p (h n) -> p h n", h=4),
                       dt2[0:cnt, c, 4 * g:4 * g + 4].unsqueeze(2).broadcast_to([cnt, 4, HEAD]), mul
                       ).then_inc(sem("ssd_xdt"), 1)
                    dve.wait_ge(sem("ssd_eg"), n + 1)
                    d = decay2[b][0:cnt, :, 0:cnt]
                    tt(d, ps[0:cnt, 2 * b, :].rearrange("p (h n) -> p h n", h=4)[:, :, 0:cnt],
                       cs2[0:cnt, c, 4 * g:4 * g + 4].unsqueeze(2).broadcast_to([cnt, 4, cnt]), sub
                       ).then_inc(sem("ssd_in_read"), 1)
                    dve.drain()
                    ts(d, d, 0.0, None, lo_).then_inc(sem("ssd_diff"), 1)
                if 1 <= n <= len(SSD):
                    ssd_mask(n - 1)
                if n >= 2:
                    ssd_result(n - 2)
            for t in range(SSD_X):
                tt(xbc[:, t, :], xbc[:, t, :], z2[:, t, :], mul).then_inc(sem("gated"), 1)
            for g in range(SSD_G):
                dve.wait_ge(sem("group_root"), g + 1)
                dve.reciprocal(groot[g % 2], groot[g % 2])
                dve.drain()
                for e in range(2):
                    x = xbc[:, 2 * g + e, :]
                    stt(x, x, pcol("gate_norm", 2 * g + e), groot[g % 2], mul, mul).then_inc(sem("mix2_ready"), 1)
            residual(8, m2_out, lambda k: pcol("post2", k))
            ffn("up2", 10, 2, 1)

        @block.gpsimd
        def _(pool):
            pool.wait_ge(sem("powers_ready"), 1)
            for j in range(S5_TILES):
                if j >= 2:
                    pool.wait_ge(sem("table_used"), j - 1)
                C, Sn = (x.rearrange("p (a b) -> p a b", b=32) for x in table[j % 2])
                t1, t2 = (x.rearrange("p (a b) -> p a b", b=32) for x in tabt)
                f = [x[:, j, :].unsqueeze(1).broadcast_to([P, 16, 32]) for x in fine]
                g = [x[:, j, :].unsqueeze(2).broadcast_to([P, 16, 32]) for x in coarse]
                pool.tensor_tensor(t1, g[0], f[0], ALU.mult)
                pool.tensor_tensor(t2, g[1], f[1], ALU.mult)
                pool.drain()
                pool.tensor_tensor(C, t1, t2, ALU.subtract)
                pool.drain()
                pool.tensor_tensor(t1, g[0], f[1], ALU.mult)
                pool.tensor_tensor(t2, g[1], f[0], ALU.mult)
                pool.drain()
                pool.tensor_tensor(Sn, t1, t2, ALU.add).then_inc(sem("table_ready"), 1)
                pool.drain()
            for v in range(LEVELS):
                mask = ccol("levels", v * P, P).unsqueeze(1).broadcast_to([P, HEADS, P])
                for c in range(CHUNKS):
                    if v == 0:
                        pool.wait_ge(sem("a_ready"), c + 1)
                    else:
                        pool.wait_ge(sem("ax_done"), CHUNKS * (v - 1) + c + 1)
                    pool.tensor_tensor(a_lev[:, c], amat[:, c], mask, ALU.mult).then_inc(sem("level_ready"), 1)

            pool.wait_ge(sem("slots_ready"), 1)
            pool.wait_ge(sem("xtok_read"), 8)
            pool.wait_ge(sem("rows_zeroed"), 16)
            for n in range(2 * CHUNKS):
                pool.indirect_dma_start(out=rows_in, out_offset=bass.IndirectOffsetOnAxis(ap=slot_id[:, n:n + 1], axis=0),
                                        in_=xtok[:, n % CHUNKS, :], in_offset=None).then_inc(sem("rows_scattered"), 16)
            pool.wait_ge(sem("rows_stored0"), 16 * FREE + 8 * BLOCKS)
            pool.wait_ge(sem("rows_stored1"), 16 * FREE + 8 * BLOCKS)
            for n in range(2 * CHUNKS):
                pool.indirect_dma_start(out=(y1 if n < CHUNKS else y2)[:, n % CHUNKS, :], out_offset=None, in_=rows_out,
                                        in_offset=bass.IndirectOffsetOnAxis(ap=slot_id[:, n:n + 1], axis=0)
                                        ).then_inc(sem("rows_gathered"), 16)

            for n in range(len(CH2) * SSD_G):
                c, g = n // SSD_G, n % SSD_G
                (lo, cnt), b = CH2[c], n % 2
                if n >= 2:
                    pool.wait_ge(sem("ssd_out_done"), n - 1)
                pool.wait_ge(sem("ssd_xdt"), n + 1)
                pool.tensor_tensor(xdd[0:cnt, b], xdt[b][0:cnt], tail2[0:cnt, c, 4 * g:4 * g + 4].unsqueeze(2).broadcast_to(
                    [cnt, 4, HEAD]), ALU.mult)
                pool.wait_ge(sem("ssd_eg"), n + 1)
                C = xbc[:, SSD_X + SSD_G + g, lo:lo + cnt]
                pool.tensor_tensor(cdec[b][:, :, 0:cnt], eg2[b][:, :, 0:cnt], C.unsqueeze(1).broadcast_to([P, 4, cnt]),
                                   ALU.mult).then_inc(sem("ssd_pool"), 1)


def _units(blocks):
    n = len(blocks) // 16
    return blocks.reshape(n, 16, P, P).transpose(0, 2, 1, 3).reshape(n, P, UNIT)


def _blocks(w, order=None):
    k, m = w.shape[0] // P, w.shape[1] // P
    b = w.reshape(k, P, m, P).transpose(2, 0, 1, 3)
    if order is not None:
        b = b[order]
    return b.reshape(-1, P, P)


def _pad(blocks):
    return np.concatenate([blocks, np.zeros(((-len(blocks)) % 16, P, P), np.float32)])


def _down(w):
    b = _blocks(w).reshape(-1, DOWN_K, P, P)
    return np.concatenate([b, np.zeros((len(b), 16 - DOWN_K, P, P), np.float32)], 1).reshape(-1, P, P)


def _stream(a):
    pairs = [t for i in range(FF) for t in (i, FF + i)]
    w0 = a["l0_w_in_2"]
    q0 = 2 * LRU * P
    kv = q0 + Q_TILES * P
    kdup = [w0[:, kv + HEAD * h:kv + HEAD * (h + 1)] for h in (0, 0, 1, 1)]
    w0 = np.concatenate([w0[:, :kv], *kdup, w0[:, kv + P:kv + 2 * P]], 1)
    order0 = [t for i in range(LRU) for t in (i, LRU + i)] + list(range(2 * LRU, 2 * LRU + Q_TILES + 3))
    parts = [_blocks(a["w_ada"][0]), _blocks(np.ascontiguousarray(a["w_in"][0][:, :20 * P])),
             _blocks(a["w_glu"][0]), _blocks(a["w_out"][0]),
             _pad(_blocks(w0, order0)), _blocks(a["l0_w_out_2"]),
             _blocks(a["l0_ffn_w_up_2"], pairs), _down(a["l0_ffn_w_down_2"]),
             _blocks(np.ascontiguousarray(a["l1_w_in_2"][:, :48 * P])), _blocks(a["l1_w_out_2"]),
             _blocks(a["l1_ffn_w_up_2"], pairs), _down(a["l1_ffn_w_down_2"])]
    out = _units(np.concatenate(parts))
    assert len(out) == UNITS, (len(out), UNITS)
    return out


def _columns(v):
    return np.asarray(v).reshape(-1, P).T


def _taps(w):
    return np.concatenate([_columns(t) for t in w], 1)


def _params(a):
    pairs = np.array([t for i in range(FF) for t in (i, FF + i)])
    rows = lambda v: np.broadcast_to(np.asarray(v).reshape(1, -1), (P, np.asarray(v).size))
    ffw = lambda w: np.concatenate([_columns(t)[:, pairs] for t in w], 1)
    state = lambda v: np.repeat(np.asarray(v).reshape(-1), 64).reshape(S5_TILES, P).T
    values = {
        "c": _columns(a["c"][0]), "b_ada": _columns(a["b_ada"][0]), "norm1_g": _columns(a["norm1_g"][0]),
        "norm2_g": _columns(a["norm2_g"][0]), "normf_g": _columns(a["normf_g"]), "s5_d": _columns(a["s5_d"][0]),
        "b_glu": _columns(a["b_glu"][0]), "conv_w": _taps(a["conv_w"][0]), "gdn_norm_g": _columns(a["gdn_norm_g"][0]),
        "lam_re": a["lam_re"][0].reshape(S5_TILES, P).T, "lam_im": a["lam_im"][0].reshape(S5_TILES, P).T,
        "log_step": state(a["log_step"][0]), "a_log": rows(a["a_log"][0]), "dt_bias": rows(a["dt_bias"][0]),
        "pre0": _columns(a["l0_mix_pre_norm_2"]), "post0": _columns(a["l0_mix_post_norm_2"]),
        "lru_w": _taps(a["l0_lru_conv_w_2"]), "lru_b": _columns(a["l0_lru_conv_b_2"]),
        "b_a": _columns(a["l0_lru_b_a_2"]), "b_x": _columns(a["l0_lru_b_x_2"]), "lam": _columns(a["l0_lru_lambda_2"]),
        "fpre0": _columns(a["l0_ffn_pre_norm_2"]), "fpost0": _columns(a["l0_ffn_post_norm_2"]),
        "fw0": ffw(a["l0_ffn_conv_w_2"]), "fb0": _columns(a["l0_ffn_conv_b_2"])[:, pairs], "sinks": rows(a["l0_attn_sinks_2"]),
        "pre2": _columns(a["l1_mix_pre_norm_2"]), "post2": _columns(a["l1_mix_post_norm_2"]),
        "ssm_w": _taps(a["l1_ssm_conv_w_2"]), "ssm_b": _columns(a["l1_ssm_conv_b_2"]),
        "gate_norm": _columns(a["l1_gate_norm_2"]), "d_skip": _columns(np.repeat(a["l1_d_skip_2"], 64)),
        "dt_bias2": rows(a["l1_dt_bias_2"]), "a_log2": rows(a["l1_a_log_2"]),
        "fpre2": _columns(a["l1_ffn_pre_norm_2"]), "fpost2": _columns(a["l1_ffn_post_norm_2"]),
        "fw2": ffw(a["l1_ffn_conv_w_2"]), "fb2": _columns(a["l1_ffn_conv_b_2"])[:, pairs],
    }
    return np.concatenate([values[name] for name, _ in PARAMS], 1)


def _s5(a):
    b, c = np.zeros((2, P, 4, P), np.float32), np.zeros((2, P, S5_TILES, 32), np.float32)
    for n, (wb, wc) in enumerate((("s5_b_re", "s5_c_re"), ("s5_b_im", "s5_c_im"))):
        wb, wc = a[wb][0], a[wc][0]
        for g in range(32):
            j, r = g // 2, g % 2
            row = 32 * (j % 4) + 16 * r
            b[n, row:row + 16, j // 4, 64 * r:64 * r + 64] = wb[g].T
            c[n, 64 * r:64 * r + 64, j, 16 * r:16 * r + 16] = wc[g].T
    return np.concatenate([b[0].reshape(P, -1), b[1].reshape(P, -1), c[0].reshape(P, -1), c[1].reshape(P, -1)], 1)


def _rows8(w):
    return w.reshape(DT, P, -1).transpose(1, 0, 2).reshape(P, -1)


def _experts(a):
    gu = np.concatenate([a["w_gate"][0], a["w_up"][0]], 2).reshape(EXPERTS, DT, P, 2 * D_EXPERT).transpose(0, 2, 1, 3)
    dn = a["w_down"][0].reshape(EXPERTS, 2, P, D).transpose(0, 2, 1, 3)
    return np.concatenate([gu.reshape(EXPERTS, P, -1), dn.reshape(EXPERTS, P, -1)], 2).reshape(EXPERTS * P, 3 * UNIT)


def layout(inputs):
    a = {k: np.asarray(v) for k, v in inputs.items()}
    return {
        "x_fm": np.ascontiguousarray(a["x"][0].T.reshape(DT, P, SEQ).transpose(1, 0, 2)),
        "meta_fm": np.ascontiguousarray(a["meta_tokens_2"].T.reshape(DT, P, META).transpose(1, 0, 2)),
        "stream": _stream(a),
        "params": np.ascontiguousarray(_params(a)),
        "consts": shape_constants(),
        "s5": _s5(a),
        "w_gates": _rows8(np.ascontiguousarray(a["w_in"][0][:, 20 * P:])),
        "w_router": _rows8(np.concatenate([a["w_router_grp"][0], a["w_router_exp"][0]], 1)),
        "w_lru": np.ascontiguousarray(np.concatenate([a["l0_lru_w_a_2"], a["l0_lru_w_x_2"]], 0).transpose(1, 0, 2)).reshape(P, -1),
        "w_dt": _rows8(np.ascontiguousarray(a["l1_w_in_2"][:, 48 * P:])),
        "experts": _experts(a),
    }


def kernel(**inputs):
    import concourse.bacc as _bacc
    from concourse.bass_utils import run_bass_kernel_spmd as _run

    nc = _bacc.Bacc("TRN2", target_bir_lowering=False, num_devices=1)
    arrays, args = {}, {}
    for name, v in layout(inputs).items():
        arrays[f"in_{name}"] = v
        args[name] = nc.dram_tensor(f"in_{name}", v.shape, mybir.dt.from_np(v.dtype), kind="ExternalInput").ap()
    args["out"] = nc.dram_tensor("out_fm", (P, DT, SEQ), F32, kind="ExternalOutput").ap()
    program(nc, args)
    got = _run(nc, [arrays], core_ids=[0]).results[0]["out_fm"]
    return np.ascontiguousarray(got.transpose(2, 1, 0).reshape(1, SEQ, D))
```

```python
from contextlib import ExitStack

import numpy as np

import concourse.bass as bass
from concourse import mybir

F32 = mybir.dt.float32
I32 = mybir.dt.int32
U32 = mybir.dt.uint32
ALU = mybir.AluOpType
ACT = mybir.ActivationFunctionType
AX = mybir.AxisListType.X

P = 128
WORK = 29990
D = 1024
DT = D // P
SEQ = 512
META = 16
T2 = SEQ + META
HALF = T2 // 2
EPS = 1e-6

NS5 = 4
S5_TILES = 16
HEADS = 4
CHUNKS = SEQ // P
LEVELS = 7
EXPERTS = 32
GROUPS = 4
D_EXPERT = 256
FREE = 1
BLOCKS = (2 * SEQ + EXPERTS * (P - 1)) // P
PAIRS = BLOCKS // 2

CONV_C = 4
CONV_F = 3
LRU = 8
Q_HEADS = 16
HEAD = 64
Q_TILES = Q_HEADS * HEAD // P
FF = 2816 // P
SSD_X = 16
SSD_G = 8
SSD_H = 32
CH2 = [(0, META)] + [(META + P * i, P) for i in range(4)]

WSLOTS = 4
UNIT = 16 * P
_two = lambda u: 2 * (u + 1)
_one = lambda u: u + 1
_MOD1, _MOD2 = 8, 16
STAGES = [("mod1", _MOD1, 0, None), ("in1", 10 + _MOD2, 20, None), ("glu", 1, 4, lambda u: 4), ("out1", 4, 8, _two),
          ("in0", 14, 27, lambda u: min(2 * (u + 1), 27)), ("out0", 8, 8, _one),
          ("up0", 22, 44, _two), ("down0", 16, 8, lambda u: u // 2 + 1),
          ("in2", 24, 48, _two), ("out2", 8, 8, _one),
          ("up2", 22, 44, _two), ("down2", 16, 8, lambda u: u // 2 + 1)]
U0, Q0, ENDED, _q = {}, {}, [], 0
for _name, _units, _tiles, _ended in STAGES:
    U0[_name], Q0[_name] = len(ENDED), _q
    if _name == "mod1":
        ENDED += [("mod_done", _u + 1) for _u in range(_units)]
    elif _name == "in1":
        ENDED += [("tile_done", 2), ("tile_done", 4)]
        for _m in range(_MOD2 // 2):
            ENDED += [("tile_done", 4 + 2 * (_m + 1)), ("mod_done", _MOD1 + 2 * _m + 1), ("mod_done", _MOD1 + 2 * _m + 2)]
    else:
        ENDED += [("tile_done", _q + _ended(_u)) for _u in range(_units)]
    _q += _tiles
UNITS = len(ENDED)
IN1_UNIT = [U0["in1"] + 2 + 3 * (j // 2) for j in range(16)]
MOD2_UNIT = [U0["in1"] + 3 + 3 * (j // 2) + j % 2 for j in range(_MOD2)]
DOWN_K = FF // 2

SQ0 = [0] + [20 + DT * n for n in range(10)]

PARAMS = [("c", 8), ("b_ada", 48), ("norm1_g", 8), ("norm2_g", 8), ("normf_g", 8), ("s5_d", 4), ("b_glu", 4),
          ("conv_w", 48), ("gdn_norm_g", 1), ("lam_re", 16), ("lam_im", 16), ("log_step", 16),
          ("a_log", 4), ("dt_bias", 4),
          ("pre0", 8), ("post0", 8), ("lru_w", 32), ("lru_b", 8), ("b_a", 8), ("b_x", 8), ("lam", 8),
          ("fpre0", 8), ("fpost0", 8), ("fw0", 132), ("fb0", 44), ("sinks", 16),
          ("pre2", 8), ("post2", 8), ("ssm_w", 128), ("ssm_b", 32), ("gate_norm", 16), ("d_skip", 16),
          ("dt_bias2", 32), ("a_log2", 32), ("fpre2", 8), ("fpost2", 8), ("fw2", 132), ("fb2", 44)]
PCOL, _n = {}, 0
for _name, _w in PARAMS:
    PCOL[_name] = _n
    _n += _w
NPAR = _n
CONSTS = [("ident", P), ("ones", P), ("upto", P), ("levels", LEVELS * P), ("dist1", META + P), ("dist2", META + 2 * P),
          ("dist0", META), ("strict", P), ("grp_rank", GROUPS), ("exp_rank", EXPERTS), ("row", 1), ("eps", 1), ("ln", 1)]
CCOL, _n = {}, 0
for _name, _w in CONSTS:
    CCOL[_name] = _n
    _n += _w
NCON = _n
FAR = 1e30


def shape_constants():
    out = np.zeros((P, NCON), np.float32)

    def put(name, a):
        out[:, CCOL[name]:CCOL[name] + a.shape[-1]] = a

    i, j = np.arange(P)[:, None], np.arange(P)[None, :]
    put("ident", (i == j).astype(np.float32))
    put("ones", np.ones((P, P), np.float32))
    put("upto", (i <= j).astype(np.float32))
    put("strict", (i < j).astype(np.float32))
    for v in range(LEVELS):
        b = 1 << v
        put_at = (i // (2 * b) == j // (2 * b)) & (j % (2 * b) >= b) & (i % (2 * b) < b)
        out[:, CCOL["levels"] + v * P:CCOL["levels"] + (v + 1) * P] = put_at
    m, band = np.arange(META)[None, :], np.arange(2 * P)[None, :]
    far = lambda ok, dist: np.where(ok, dist, FAR).astype(np.float32)
    put("dist0", np.concatenate([far(i >= m, i - m)], 1))
    own = far(i >= j, i - j)
    put("dist1", np.concatenate([np.minimum(META + i - m, P).astype(np.float32), own], 1))
    dist = i + P - band
    put("dist2", np.concatenate([np.full((P, META), float(P), np.float32), far((dist >= 0) & (dist < P), dist)], 1))
    put("grp_rank", np.broadcast_to(GROUPS - np.arange(GROUPS, dtype=np.float32), (P, GROUPS)))
    put("exp_rank", np.broadcast_to(EXPERTS - np.arange(EXPERTS, dtype=np.float32), (P, EXPERTS)))
    put("row", i.astype(np.float32))
    put("eps", np.full((P, 1), EPS, np.float32))
    return out


def program(nc, a):
    with ExitStack() as ctx:
        def sb(name, *shape, dt=F32):
            return ctx.enter_context(nc.sbuf_tensor(name, [P, *shape], dt))

        sems = {}

        def sem(name):
            if name not in sems:
                sems[name] = ctx.enter_context(nc.semaphore(name))
            return sems[name]

        h = sb("h", DT, T2)
        u = sb("u", DT, T2)
        ring = sb("ring", WSLOTS, UNIT)
        par = sb("par", NPAR)
        con = sb("con", NCON)
        sq = sb("sq", 2, T2)
        rs = sb("rs", T2)
        tmp = sb("tmp", 2, T2 + 4)
        mod = sb("mod", 48)
        modg = sb("modg", 2 * DT)
        work = sb("work", WORK)
        ps = ctx.enter_context(nc.psum_tensor("ps", [P, 8, 512], F32))

        def at(off, *shape):
            n = int(np.prod(shape))
            v = work[:, off:off + n]
            if len(shape) == 1:
                return v
            names = " ".join(f"d{i}" for i in range(len(shape)))
            return v.rearrange(f"p ({names}) -> p {names}", **{f"d{i}": s for i, s in enumerate(shape)})

        def pcol(name, i=0, n=1):
            return par[:, PCOL[name] + i:PCOL[name] + i + n]

        def ccol(name, i=0, n=1):
            return con[:, CCOL[name] + i:CCOL[name] + i + n]

        ident, ones, upto, eps = ccol("ident", 0, P), ccol("ones", 0, P), ccol("upto", 0, P), ccol("eps")

        def pair(q, half=0, n=512):
            return ps[:, 2 * (q % 2) + half, 0:n]

        def pair2(q):
            return ps[:, 2 * (q % 2):2 * (q % 2) + 2, 0:HALF]

        def halves(x):
            return x.rearrange("p (s n) -> p s n", s=2)

        cz = at(0, DT, 63)
        modrow = at(512, P)[0:32, :]
        mix = at(0, DT, SEQ)
        z1 = at(4096, HEADS, SEQ)
        qkv = at(6144, 12, SEQ)
        F1 = 12288
        us5 = at(F1, NS5, SEQ)
        y5 = at(F1 + 2048, NS5, SEQ)
        s5w = at(F1 + 4096, 2048)
        s5b = [at(F1 + 4096 + 512 * n, 4, P) for n in range(2)]
        s5c = [at(F1 + 4096 + 1024 + 512 * n, S5_TILES, 32) for n in range(2)]
        s5ck = [at(F1 + 6144 + 512 * n, S5_TILES, 32) for n in range(2)]
        fine = [at(F1 + 5120 + 512 * n, S5_TILES, 32) for n in range(2)]
        coarse = [at(F1 + 7168 + 256 * n, S5_TILES, 16) for n in range(2)]
        table = [[at(F1 + 7680 + 1024 * b + 512 * n, SEQ) for n in range(2)] for b in range(2)]
        tabt = [at(F1 + 9728 + 512 * n, SEQ) for n in range(2)]
        f5 = [at(F1 + 10752 + 512 * n, SEQ) for n in range(2)]
        z5 = [at(F1 + 11776 + 512 * n, SEQ) for n in range(2)]
        p5 = [at(F1 + 12800 + 512 * n, SEQ) for n in range(4)]
        st5 = [[at(F1 + 14848 + 1024 * b + 512 * n, SEQ) for n in range(2)] for b in range(2)]
        s5s = sb("s5s", 24, S5_TILES)
        sig = p5[0]
        cbuf = [tmp[:, b, 0:SEQ + 3] for b in range(2)]
        wgate = at(WORK - 64, DT, 8)
        beta, gate, csum, gtot, ecs, etail, egt, bcs, sp1, sp2, sp3, sp4 = [
            at(WORK - 64 - 16 * (n + 1), CHUNKS * HEADS) for n in range(12)]
        amat = at(F1, CHUNKS, HEADS, P)
        qk_d = at(F1 + 2048, CHUNKS, HEADS, P)
        q_dec = at(F1 + 4096, CHUNKS, HEADS, P)
        kb_g = at(F1 + 6144, CHUNKS, HEADS, P)
        k_tail = at(F1 + 8192, CHUNKS, HEADS, P)
        v_b = at(F1 + 10240, CHUNKS, HEADS, P)
        w_mat = at(F1 + 12288, CHUNKS, HEADS, P)
        a_lev = at(F1 + 14336, CHUNKS, HEADS, P)
        x_inv = at(6144, CHUNKS, HEADS, P)
        y_inv = at(8192, CHUNKS, HEADS, P)
        o_gdn = at(10240, HEADS, SEQ)
        val, kc = w_mat, a_lev
        state = [at(F1 + 16384, HEADS, P), at(6144, HEADS, P)]
        v_new = at(F1 + 16896, HEADS, P)
        dtmp = tmp[:, 0, 0:SEQ].rearrange("p (h n) -> p h n", h=HEADS)
        egb = tmp[:, 1, 0:SEQ].rearrange("p (h n) -> p h n", h=HEADS)

        wrouter = sb("wrouter", DT, GROUPS + EXPERTS)
        zeros = at(F1 + 16896, 512)
        xtok = at(0, CHUNKS, D)
        mw = [at(4096 + 3 * UNIT * p, 3 * UNIT) for p in range(2)]
        xb = [at(16384 + D * p, D) for p in range(2)]
        xbt = [at(18432 + D * p, DT, P) for p in range(2)]
        yb = [at(20480 + D * p, D) for p in range(2)]
        silu_b = at(22528, 2, D_EXPERT)
        h_b = at(23040, 2, D_EXPERT)
        ht_b = at(23552, 2, P)
        R0 = 23808
        logit = at(R0, CHUNKS, GROUPS + EXPERTS)
        r32 = [at(R0 + 144 + 128 * n, CHUNKS, EXPERTS) for n in range(6)]
        r4 = [at(R0 + 912 + 16 * n, CHUNKS, GROUPS) for n in range(4)]
        r1 = [at(R0 + 976 + 4 * n, CHUNKS) for n in range(12)]
        e32 = [at(R0 + 1024 + 32 * n, EXPERTS) for n in range(6)]
        slots = at(R0 + 1216, 2 * CHUNKS)
        slot_id = at(R0 + 1224, 2 * CHUNKS).bitcast(U32)
        eid = at(R0 + 1232, P).bitcast(I32)
        ecol = at(R0 + 1360, 2)
        y1, y2, moe = at(4096, CHUNKS, D), at(8192, CHUNKS, D), at(12288, CHUNKS, D)
        rows_in = nc.dram_tensor("rows_in", (BLOCKS * P, D), F32).ap()
        rows_out = nc.dram_tensor("rows_out", (BLOCKS * P, D), F32).ap()

        wdt = sb("wdt", DT, SSD_H)
        mix0 = at(0, 2 * LRU, T2)
        q_fm = at(8448, Q_TILES, T2)
        k_fm = at(12672, 2, T2)
        v_fm = at(13728, T2)
        v_tok = at(14256, len(CH2), P)
        g_lru, x_lru, r_lru, i_lru, a_lru, t_lru = [at(14900 + 2 * T2 * n, 2, T2) for n in range(6)]
        w_lru = at(21300, 2, LRU, P)
        lam8 = sb("lam8", 4, LRU)
        prob = at(23360, 2, 2, META + 2 * P)
        prob_t = at(24448, 2, 2, 3 * P)
        stat = at(25984, 2, 8, 2)
        m_out = at(16900, DT, T2)
        prod = at(0, FF, T2)
        gact = at(21200, T2)
        uact = at(21800, T2)
        pad = [tmp[:, b, 0:T2 + 3] for b in range(2)]
        z2 = at(0, SSD_X, T2)
        xbc = at(8448, SSD_X + 2 * SSD_G, T2)
        st2 = at(25344, SSD_H, HEAD)
        T0 = 27392
        xdd = at(T0, 2, 4, HEAD)
        b_tok = at(T0 + 512, 2, P)
        cbm = at(T0 + 768, 2, P)
        dt2, da2, cs2, gt2_, tail2, egt2, sa2, sb2, sc2 = [at(T0 + 1024 + 160 * n, len(CH2), SSD_H) for n in range(9)]
        uf = u[:, :, :].rearrange("p k n -> p (k n)")
        at_u = lambda off, n: uf[:, off:off + n]
        decay2 = [at_u(512 * n, 512).rearrange("p (h n) -> p h n", h=4) for n in range(2)]
        eg2 = [at_u(1024 + 512 * n, 512).rearrange("p (h n) -> p h n", h=4) for n in range(2)]
        cdec = [at_u(2048 + 512 * n, 512).rearrange("p (h n) -> p h n", h=4) for n in range(2)]
        xdt = [at_u(3072 + 256 * n, 256).rearrange("p (h n) -> p h n", h=4) for n in range(2)]
        m2_out = at(16896, DT, T2)
        gsq = [sq[:, e, :] for e in range(2)]
        groot = [at_u(T2 * n, T2) for n in range(2)]

        block = ctx.enter_context(nc.Block())

        @block.sync
        def _(sp):
            def load_unit(n, slot, waits=True):
                if waits:
                    name, count = ENDED[n - WSLOTS]
                    sp.wait_ge(sem(name), count)
                sp.dma_start(ring[:, slot, :], a["stream"][n]).then_inc(sem(f"unit_loaded{slot}"), 16)

            def stream_first(stage):
                n0, units = U0[stage], dict((s[0], s[1]) for s in STAGES)[stage]
                for n in range(n0, n0 + min(WSLOTS, units)):
                    load_unit(n, n % WSLOTS, n >= WSLOTS)

            def stream_rest(stage):
                n0, units = U0[stage] + WSLOTS, dict((s[0], s[1]) for s in STAGES)[stage] - WSLOTS
                trips = max(units, 0) // WSLOTS
                if trips > 1 and stage != "in1":
                    per = ENDED[n0][1] - ENDED[n0 - WSLOTS][1]
                    with sp.Fori(0, trips) as i:
                        for j in range(WSLOTS):
                            slot = (n0 + j) % WSLOTS
                            sp.wait_ge(sem("tile_done"), i * per + ENDED[n0 + j - WSLOTS][1])
                            sp.dma_start(ring[:, slot, :], a["stream"][i * WSLOTS + (n0 + j)]
                                         ).then_inc(sem(f"unit_loaded{slot}"), 16)
                else:
                    trips = 0
                for n in range(n0 + trips * WSLOTS, n0 + units):
                    load_unit(n, n % WSLOTS)

            sp.dma_start(par[:, :], a["params"]).then_inc(sem("inputs_loaded"), 16)
            sp.dma_start(con[:, :], a["consts"]).then_inc(sem("inputs_loaded"), 16)
            sp.dma_start(h[:, :, META:T2], a["x_fm"]).then_inc(sem("inputs_loaded"), 16)
            sp.dma_start(s5w, a["s5"]).then_inc(sem("inputs_loaded"), 16)
            sp.dma_start(wgate, a["w_gates"].rearrange("p (k n) -> p k n", k=DT)).then_inc(sem("inputs_loaded"), 16)
            sp.dma_start(wrouter[:, :, :], a["w_router"].rearrange("p (k n) -> p k n", k=DT)).then_inc(sem("inputs_loaded"), 16)
            sp.dma_start(h[:, :, 0:META], a["meta_fm"]).then_inc(sem("inputs_loaded"), 16)
            sp.dma_start(wdt[:, :, :], a["w_dt"].rearrange("p (k n) -> p k n", k=DT)).then_inc(sem("inputs_loaded"), 16)
            stream_first("mod1")
            stream_rest("mod1")
            for stage in ("in1", "glu"):
                stream_first(stage)
                stream_rest(stage)
            sp.wait_ge(sem("zeros_ready"), 1)
            sp.dma_start(rows_in.rearrange("(p r) n -> p (r n)", p=P).rearrange("p (m n) -> p m n", n=512),
                         zeros.unsqueeze(1).broadcast_to([P, 2 * BLOCKS, 512])).then_inc(sem("rows_zeroed"), 16)
            stream_first("out1")
            stream_first("in0")
            sp.wait_ge(sem("expert_ids"), 1)

            def load_rows(b, p):
                sp.dma_start(xb[p], rows_in[bass.ds(b * P, P), :]).then_inc(sem(f"rows_loaded{p}"), 16)

            def expert_rows(b):
                expert = sp.value_load(eid[0:1, bass.ds(b, 1)], min_val=0, max_val=EXPERTS - 1)
                return a["experts"][bass.ds(expert * P, P), :]

            def load_gate_up(rows, p):
                sp.dma_start(mw[p][:, 0:2 * UNIT], rows[:, 0:2 * UNIT]).then_inc(sem(f"gu_loaded{p}"), 16)

            def load_down(rows, p):
                sp.dma_start(mw[p][:, 2 * UNIT:], rows[:, 2 * UNIT:]).then_inc(sem(f"dn_loaded{p}"), 16)

            first, second = expert_rows(0), expert_rows(1)
            load_gate_up(first, 0)
            sp.wait_ge(sem("rows_scattered"), 16 * 8)
            load_rows(0, 0)
            load_rows(1, 1)
            load_down(first, 0)
            load_gate_up(second, 1)
            load_down(second, 1)

            def load_block(b, p):
                sp.wait_ge(sem("xt_done"), b - 1)
                load_rows(b, p)
                rows = expert_rows(b)
                sp.wait_ge(sem("gu_done"), b - 1)
                load_gate_up(rows, p)
                sp.wait_ge(sem("dn_done"), FREE + b - 1)
                load_down(rows, p)

            with sp.Fori(1, PAIRS) as i:
                for p in range(2):
                    load_block(i * 2 + p, p)
            load_block(BLOCKS - 1, 0)

            sp.wait_ge(sem("moe_added"), DT)
            sp.dma_start(w_lru, a["w_lru"].rearrange("p (m k n) -> p m k n", m=2, k=LRU)).then_inc(sem("lru_loaded"), 16)
            stream_rest("in0")
            for stage in ("out0", "up0", "down0", "in2", "out2", "up2", "down2"):
                stream_first(stage)
                stream_rest(stage)
            for k in range(DT):
                sp.wait_ge(sem("h_updated"), 3 * DT + k + 1)
                sp.dma_start(a["out"][:, k, :], h[:, k, META:T2]).then_inc(sem("out_stored"), 16)
            sp.wait_ge(sem("out_stored"), 16 * DT)

        INPUTS = 16 * 8

        @block.tensor
        def _(pe):
            def unit_wait(n):
                pe.wait_ge(sem(f"unit_loaded{n % WSLOTS}"), 16 * (n // WSLOTS + 1))

            def out_tile(q, n, b0, rhs, ncols, free, normed=None):
                pe.wait_ge(sem("tile_read"), free)
                if ncols <= 512:
                    parts = [(0, 0, ncols)]
                else:
                    parts = [(0, 0, ncols // 2), (1, ncols // 2, ncols // 2)]
                for half, lo, cnt in parts:
                    for k, x in enumerate(rhs):
                        b = b0 + k
                        if normed is not None and half == 0:
                            pe.wait_ge(sem("normed"), normed + k + 1)
                        m = pe.matmul(pair(q, half, cnt), ring[:, (n + b // 16) % WSLOTS, b % 16 * P:(b % 16 + 1) * P],
                                      x[:, lo:lo + cnt], start=(k == 0), stop=(k == len(rhs) - 1))
                m.then_inc(sem("tile_done"), 1)

            def sums(count, k, first, last, ncols, half_cols, ready=None):
                pe.wait_ge(sem("squares_ready"), count)
                for s in range(2 if half_cols else 1):
                    m = pe.matmul(ps[:, 6 + s, 0:ncols], ones, sq[:, k % 2, s * ncols:(s + 1) * ncols],
                                  start=first, stop=last)
                m.then_inc(sem("squares_used"), 1)

            def norm_sums(n, two):
                for k in range(DT):
                    sums(SQ0[n] + k + 1, k, k == 0, k == DT - 1, HALF if two else SEQ, two)

            pe.wait_ge(sem("inputs_loaded"), INPUTS)
            pe.wait_ge(sem("cz_ready"), 1)
            def mod_unit(n, t0, tiles, bank):
                unit_wait(n)
                for t in (t0, t0 + 1):
                    for k in range(DT):
                        b = 8 * (t - t0) + k
                        m = pe.matmul(ps[0:tiles, bank, 0:P], cz[:, k, 31 - t:31 - t + tiles],
                                      ring[:, n % WSLOTS, b * P:(b + 1) * P], start=(t == 0 and k == 0),
                                      stop=(t == tiles - 1 and k == DT - 1))
                m.then_inc(sem("mod_done"), 1)

            def mod_turned(count, tiles, bank):
                pe.wait_ge(sem("mod_copied"), count)
                pe.transpose(ps[:, bank, 256:256 + tiles], modrow[0:tiles, :], ident[0:tiles, 0:tiles]
                             ).then_inc(sem("mod_turned"), 1)

            norm_sums(0, False)
            for n in range(8):
                mod_unit(n, 2 * n, 16, 3)
            mod_turned(1, 16, 3)
            q0, n0 = Q0["in1"], U0["in1"]
            u1 = [u[:, k, 0:SEQ] for k in range(DT)]

            def in1(t):
                n = n0 + t // 2 if t < NS5 else IN1_UNIT[t - NS5]
                if t % 2 == 0:
                    unit_wait(n)
                out_tile(q0 + t, n, 8 * (t % 2), u1, SEQ, q0 + t + 1, None if t else 0)

            for t in range(NS5):
                in1(t)
            for c in range(CHUNKS):
                for k in range(DT):
                    m = pe.matmul(ps[:, 3, 384 + 8 * c:392 + 8 * c], u[:, k, c * P:(c + 1) * P], wgate[:, k, :],
                                  start=(k == 0), stop=(k == DT - 1))
            m.then_inc(sem("gates_done"), 1)

            def s5_in(j):
                if j == 0:
                    pe.wait_ge(sem("tile_read"), 2 + q0 + NS5)
                if j:
                    pe.wait_ge(sem("s5_in_read"), j)
                lo = 32 * (j % 4)
                for n in range(2):
                    m = pe.matmul(ps[:, 4 + n, 0:SEQ], s5b[n][lo:lo + 32, j // 4, :], us5[lo:lo + 32, j // 4, :],
                                  start=True, stop=True)
                m.then_inc(sem("s5_in_done"), 1)

            def s5_out(j):
                pe.wait_ge(sem("s5_state_ready"), j + 1)
                if j % 4 == 0 and j >= 8:
                    pe.wait_ge(sem("y5_ready"), j // 4 - 1)
                lo = 32 * (j % 4)
                for n in range(2):
                    m = pe.matmul(ps[lo:lo + 32, 6 + j // 4 % 2, 0:SEQ], s5ck[n][:, j, :], st5[j % 2][n],
                                  start=(n == 0), stop=(n == 1), tile_position=(0, lo))
                m.then_inc(sem("s5_out_done"), 1)

            for j in range(S5_TILES):
                in1(NS5 + j)
                s5_in(j)
                if j == 0:
                    pe.wait_ge(sem("mod_read"), 1)
                mod_unit(MOD2_UNIT[j], 2 * j, 32, 3)
                if j >= 8:
                    pe.wait_ge(sem("squares_ready"), j + 1)
                    if j > 8:
                        pe.wait_ge(sem("l2_read"), j - 8)
                    pe.matmul(ps[:, 1, 0:SEQ], ones, sq[:, j % 2, 0:SEQ], start=True, stop=True
                              ).then_inc(sem("squares_used"), 1)
                if j:
                    s5_out(j - 1)
            s5_out(S5_TILES - 1)
            mod_turned(2, 32, 3)
            unit_wait(U0["glu"])
            pe.wait_ge(sem("y5_gelu"), NS5)
            for t in range(NS5):
                out_tile(Q0["glu"] + t, U0["glu"], 4 * t, [y5[:, k, :] for k in range(NS5)], SEQ, Q0["glu"] + t + 1)
            pe.wait_ge(sem("gate_ready"), 1)
            pe.wait_ge(sem("beta_ready"), 1)
            pe.matmul(ps[:, 3, 448:464], upto, gate, start=True, stop=True)
            pe.matmul(ps[:, 3, 480:496], ones, gate, start=True, stop=True).then_inc(sem("csum_done"), 1)
            pe.wait_ge(sem("qk_ready"), 8)
            pe.wait_ge(sem("silu_qkv"), 12)
            pe.wait_ge(sem("csum_read"), 1)
            for c in range(CHUNKS):
                tok = slice(c * P, (c + 1) * P)
                if c >= 2:
                    pe.wait_ge(sem("turned_read"), c - 1)
                bank = 4 + 2 * (c % 2)
                for hd in range(HEADS):
                    o = slice(hd * P, (hd + 1) * P)
                    pe.transpose(ps[:, bank, o], qkv[:, 4 + hd, tok], ident)
                    m = pe.transpose(ps[:, bank + 1, o], qkv[:, 8 + hd, tok], ident)
                m.then_inc(sem("turned"), 1)
                if c:
                    pe.wait_ge(sem("egb_ready"), c)
                for hd in range(HEADS):
                    m = pe.matmul(ps[:, 2, hd * P:(hd + 1) * P], gate[:, 4 * c + hd:4 * c + hd + 1].broadcast_to([P, P]),
                                  upto, start=True, stop=True)
                m.then_inc(sem("sums_spread"), 1)
                if c:
                    pe.wait_ge(sem("chunk_read"), c)
                for hd in range(HEADS):
                    o = slice(hd * P, (hd + 1) * P)
                    pe.matmul(ps[:, 0, o], qkv[:, 4 + hd, tok], qkv[:, 4 + hd, tok], start=True, stop=True)
                    pe.matmul(ps[:, 1, o], qkv[:, 4 + hd, tok], qkv[:, hd, tok], start=True, stop=True)
                    m = pe.matmul(ps[:, 3, o], beta[:, 4 * c + hd:4 * c + hd + 1].broadcast_to([P, P]), ident,
                                  start=True, stop=True)
                m.then_inc(sem("chunk_done"), 1)
            pe.wait_ge(sem("chunk_read"), CHUNKS)
            pe.wait_ge(sem("turned_read"), CHUNKS)
            for v in range(LEVELS):
                for c in range(CHUNKS):
                    pe.wait_ge(sem("level_ready"), CHUNKS * v + c + 1)
                    pe.wait_ge(sem("inverse_ready"), CHUNKS * v + c + 1)
                    for hd in range(HEADS):
                        m = pe.matmul(ps[:, c, hd * P:(hd + 1) * P], a_lev[:, c, hd, :], x_inv[:, c, hd, :],
                                      start=True, stop=True)
                    m.then_inc(sem("ax_done"), 1)
                for c in range(CHUNKS):
                    pe.wait_ge(sem("ax_read"), CHUNKS * v + c + 1)
                    n = CHUNKS * v + c
                    if n >= 2:
                        pe.wait_ge(sem("inverse_ready"), CHUNKS + n - 1)
                    b = 4 + 2 * (c % 2)
                    for hd in range(HEADS):
                        o = slice(hd * P, (hd + 1) * P)
                        pe.matmul(ps[:, b, o], y_inv[:, c, hd, :], w_mat[:, c, hd, :], start=True, stop=True)
                        m = pe.matmul(ps[:, b + 1, o], w_mat[:, c, hd, :], y_inv[:, c, hd, :], start=True, stop=True)
                    m.then_inc(sem("xax_done"), 1)
            for c in range(CHUNKS):
                pe.wait_ge(sem("inverse_ready"), CHUNKS * LEVELS + CHUNKS)
                if c >= 2:
                    pe.wait_ge(sem("solved_read"), c - 1)
                b = 2 * (c % 2)
                for hd in range(HEADS):
                    o = slice(hd * P, (hd + 1) * P)
                    pe.matmul(ps[:, b, o], y_inv[:, c, hd, :], v_b[:, c, hd, :], start=True, stop=True)
                    m = pe.matmul(ps[:, b + 1, o], kb_g[:, c, hd, :], y_inv[:, c, hd, :], start=True, stop=True)
                m.then_inc(sem("solved"), 1)
            def out_sums(c):
                pe.wait_ge(sem("squares_ready"), 16 + c + 1)
                if c >= 2:
                    pe.wait_ge(sem("o_norm_read"), c - 1)
                pe.matmul(ps[:, c % 2, 0:SEQ], ones, sq[:, c % 2, 0:SEQ], start=True, stop=True
                          ).then_inc(sem("squares_used"), 1)

            for c in range(CHUNKS):
                tok = slice(c * P, (c + 1) * P)
                pe.wait_ge(sem("solved_read"), c + 1)
                pe.wait_ge(sem("state_ready"), c + 1)
                S = state[c % 2]
                for hd in range(HEADS):
                    m = pe.matmul(ps[:, 4, hd * P:(hd + 1) * P], kc[:, c, hd, :], S[:, hd, :], start=True, stop=True)
                m.then_inc(sem("seen_done"), 1)
                pe.wait_ge(sem("v_new_ready"), c + 1)
                if c < CHUNKS - 1:
                    for hd in range(HEADS):
                        m = pe.matmul(ps[:, 5, hd * P:(hd + 1) * P], k_tail[:, c, hd, :], v_new[:, hd, :],
                                      start=True, stop=True)
                    m.then_inc(sem("state_added"), 1)
                if c:
                    pe.wait_ge(sem("o_read"), c)
                for hd in range(HEADS):
                    o = slice(hd * P, (hd + 1) * P)
                    pe.matmul(ps[:, 6, o], S[:, hd, :], q_dec[:, c, hd, :], start=True, stop=False)
                    m = pe.matmul(ps[:, 6, o], v_new[:, hd, :], qk_d[:, c, hd, :], start=False, stop=True)
                m.then_inc(sem("chunk_out_done"), 1)
                if c:
                    out_sums(c - 1)
            out_sums(CHUNKS - 1)
            pe.wait_ge(sem("mix1_ready"), 8)
            for t in range(DT):
                if t % 2 == 0:
                    unit_wait(U0["out1"] + t // 2)
                out_tile(Q0["out1"] + t, U0["out1"] + t // 2, 8 * (t % 2), [mix[:, k, :] for k in range(DT)], SEQ,
                         Q0["out1"] + t + 1)

            norm_sums(1, False)
            for k in range(DT):
                pe.wait_ge(sem("normed"), DT + k + 1)
                for c in range(CHUNKS):
                    m = pe.matmul(ps[:, (0, 1, 4, 5)[c], 0:GROUPS + EXPERTS], u[:, k, c * P:(c + 1) * P], wrouter[:, k, :],
                                  start=(k == 0), stop=(k == DT - 1))
            m.then_inc(sem("router_done"), 1)
            for c in range(CHUNKS):
                for s in range(2):
                    if c >= 1:
                        pe.wait_ge(sem("xtok_read"), 2 * c + s - 1)
                    for k in range(4):
                        m = pe.transpose(ps[:, 2 + s, k * P:(k + 1) * P], u[:, 4 * s + k, c * P:(c + 1) * P], ident)
                    m.then_inc(sem("xtok_done"), 1)
            pe.wait_ge(sem("chosen_ready"), 1)
            for c in range(CHUNKS):
                for j in range(c + 1):
                    pe.matmul(ps[:, 1, 32 * c:32 * c + 32], ones if j < c else ccol("strict", 0, P), r32[5][:, j, :],
                              start=(j == 0), stop=(j == c))
            for j in range(CHUNKS):
                m = pe.matmul(ps[:, 1, 128:160], ones, r32[5][:, j, :], start=(j == 0), stop=(j == CHUNKS - 1))
            m.then_inc(sem("places_done"), 1)
            pe.wait_ge(sem("ecol_ready"), 1)
            pe.matmul(ps[0:1, 5, 0:P], ecol[:, 0:1], ident, start=True, stop=True).then_inc(sem("erow_done"), 1)
            pe.wait_ge(sem("erow_read"), 1)

            def rows_turned(b, p, wload):
                pe.wait_ge(sem(f"rows_loaded{p}"), wload)
                if b is not None:
                    pe.wait_ge(sem("xt_read"), b)
                for k in range(DT):
                    m = pe.transpose(ps[:, 2 + k // 4, k % 4 * P:(k % 4 + 1) * P], xb[p][:, k * P:(k + 1) * P], ident)
                m.then_inc(sem("xt_done"), 1)

            def gate_up(b, p, wload, waits=True):
                pe.wait_ge(sem("xt_read"), b + 1)
                pe.wait_ge(sem(f"gu_loaded{p}"), wload)
                if waits:
                    pe.wait_ge(sem("hidden_ready"), FREE + b - 1)
                for k in range(DT):
                    m = pe.matmul(ps[:, p, :], xbt[p][:, k, :], mw[p][:, k * 512:(k + 1) * 512],
                                  start=(k == 0), stop=(k == DT - 1))
                m.then_inc(sem("gu_done"), 1)

            def hidden_turned(b, p):
                pe.wait_ge(sem("hidden_ready"), FREE + b + 1)
                pe.wait_ge(sem("ht_read"), FREE + b)
                for k in range(2):
                    m = pe.transpose(ps[:, 4, k * P:(k + 1) * P], h_b[:, p, k * P:(k + 1) * P], ident)
                m.then_inc(sem("ht_done"), 1)

            def down(b, p, wload):
                pe.wait_ge(sem("ht_read"), FREE + b + 1)
                pe.wait_ge(sem(f"dn_loaded{p}"), wload)
                pe.wait_ge(sem("dn_read"), FREE + b)
                for s in range(2):
                    for k in range(2):
                        m = pe.matmul(ps[:, 5 + s, :], ht_b[:, k, :],
                                      mw[p][:, 2 * UNIT + k * D + 512 * s:2 * UNIT + k * D + 512 * (s + 1)],
                                      start=(k == 0), stop=(k == 1))
                m.then_inc(sem("dn_done"), 1)

            pe.drain().then_inc(sem("ht_done"), FREE)
            pe.drain().then_inc(sem("dn_done"), FREE)
            rows_turned(None, 0, 16)
            gate_up(0, 0, 16, False)
            rows_turned(1, 1, 16)
            with pe.Fori(0, PAIRS - 1) as i:
                for p in range(2):
                    b = i * 2 + p
                    gate_up(b + 1, 1 - p, i * 16 + 16 * (1 + p), True)
                    hidden_turned(b, p)
                    rows_turned(b + 2, p, i * 16 + 32)
                    down(b, p, i * 16 + 16)
            n = BLOCKS - 3
            gate_up(n + 1, 1, 16 * PAIRS)
            hidden_turned(n, 0)
            rows_turned(n + 2, 0, 16 * PAIRS + 16)
            down(n, 0, 16 * PAIRS)
            gate_up(n + 2, 0, 16 * PAIRS + 16)
            hidden_turned(n + 1, 1)
            down(n + 1, 1, 16 * PAIRS)
            hidden_turned(n + 2, 0)
            down(n + 2, 0, 16 * PAIRS + 16)
            pe.wait_ge(sem("moe_ready"), CHUNKS)
            for k in range(DT):
                if k >= 2:
                    pe.wait_ge(sem("moe_added"), k - 1)
                for c in range(CHUNKS):
                    m = pe.transpose(ps[:, k % 2, c * P:(c + 1) * P], moe[:, c, k * P:(k + 1) * P], ident)
                m.then_inc(sem("moe_turned"), 1)
            norm_sums(2, False)

            norm_sums(3, True)
            q0, n0 = Q0["in0"], U0["in0"]
            u2 = [u[:, k, :] for k in range(DT)]

            def in0(t):
                if t % 2 == 0:
                    unit_wait(n0 + t // 2)
                out_tile(q0 + t, n0 + t // 2, 8 * (t % 2), u2, T2, q0 + t + 1, None if t else 3 * DT)

            def lru_gates(i):
                pe.wait_ge(sem("lru_conv"), i + 1)
                if i == 0:
                    pe.wait_ge(sem("lru_loaded"), 16)
                if i:
                    pe.wait_ge(sem("lru_sig"), i)
                for n in range(2):
                    for s in range(2):
                        m = pe.matmul(ps[:, 4 + 2 * n + s, 0:HALF], w_lru[:, n, i, :],
                                      x_lru[:, i % 2, s * HALF:(s + 1) * HALF], start=True, stop=True)
                m.then_inc(sem("lru_gates"), 1)

            for i in range(LRU):
                in0(2 * i)
                in0(2 * i + 1)
                if i:
                    lru_gates(i - 1)
            for t in range(2 * LRU, 2 * LRU + Q_TILES + 3):
                in0(t)
                if t == 2 * LRU:
                    lru_gates(LRU - 1)
            pe.wait_ge(sem("tile_read"), q0 + 27 + 2)
            pe.wait_ge(sem("lru_sig"), LRU)
            for c, (lo, n) in enumerate(CH2):
                m = pe.transpose(ps[0:n, 4 + c // 4, c % 4 * P:(c % 4 + 1) * P], v_fm[:, lo:lo + n], ident)
            m.then_inc(sem("v_turned"), 1)
            ATT = [(c, hp) for c in range(len(CH2)) for hp in range(Q_TILES)]

            def scores(n):
                c, hp = ATT[n]
                lo, cnt = CH2[c]
                if n >= 2:
                    pe.wait_ge(sem("scores_read"), n - 1)
                for e in range(2):
                    rows = slice(64 * e, 64 * e + 64)
                    out = ps[0:cnt, 2 * (n % 2) + e, :]
                    kk = k_fm[rows, hp // 4, :]
                    qq = q_fm[rows, hp, lo:lo + cnt]
                    if c <= 2:
                        m = pe.matmul(out[:, 0:lo + cnt], qq, kk[:, 0:lo + cnt], start=True, stop=True)
                    else:
                        pe.matmul(out[:, 0:META], qq, kk[:, 0:META], start=True, stop=True)
                        m = pe.matmul(out[:, META:META + 2 * P], qq, kk[:, lo - P:lo + P], start=True, stop=True)
                m.then_inc(sem("scores_done"), 1)

            def key_parts(c):
                return [(0, META, 0)] + [(META + P * i, P, d) for i, d in enumerate(([], [1], [1, 2], [2, 3], [3, 4])[c])]

            def turn(n):
                c, hp = ATT[n]
                cnt = CH2[c][1]
                pe.wait_ge(sem("prob_ready"), n + 1)
                if n == 0:
                    pe.wait_ge(sem("v_read"), 1)
                if n:
                    pe.wait_ge(sem("prob_turned_read"), n)
                for e in range(2):
                    for i, (k0, kn, _) in enumerate(key_parts(c)):
                        m = pe.transpose(ps[0:kn, 4 + e, i * P:i * P + cnt], prob[0:cnt, n % 2, e, k0:k0 + kn],
                                         ident[0:cnt, 0:cnt])
                m.then_inc(sem("prob_turned"), 1)

            def attend(n):
                c, hp = ATT[n]
                cnt = CH2[c][1]
                pe.wait_ge(sem("prob_turned_read"), n + 1)
                if n >= 2:
                    pe.wait_ge(sem("attended_read"), n - 1)
                parts = key_parts(c)
                for e in range(2):
                    for i, (_, kn, vc) in enumerate(parts):
                        kv = hp // 4
                        m = pe.matmul(ps[64 * e:64 * e + 64, 6 + n % 2, 0:cnt], v_tok[0:kn, vc, 64 * kv:64 * kv + 64],
                                      prob_t[0:kn, n % 2, e, i * P:i * P + cnt], start=(i == 0),
                                      stop=(i == len(parts) - 1), tile_position=(0, 64 * e))
                m.then_inc(sem("attended"), 1)

            scores(0)
            for n in range(len(ATT) + 2):
                if n + 1 < len(ATT):
                    scores(n + 1)
                if 1 <= n <= len(ATT):
                    turn(n - 1)
                if n >= 2:
                    attend(n - 2)

            def out_product(stage, rhs, ready, n):
                pe.wait_ge(sem(ready[0]), ready[1])
                for t in range(DT):
                    unit_wait(U0[stage] + t)
                    out_tile(Q0[stage] + t, U0[stage] + t, 0, rhs, T2, Q0[stage] + t + 1)
                    if t:
                        sums(SQ0[n] + t, t - 1, t == 1, False, HALF, True)
                sums(SQ0[n] + DT, DT - 1, False, True, HALF, True)

            def ffn(up, down, n, normed):
                q0, n0 = Q0[up], U0[up]
                with pe.Fori(0, 5) as i:
                    for j in range(8):
                        if j % 2 == 0:
                            un = n0 + j // 2
                            pe.wait_ge(sem(f"unit_loaded{un % WSLOTS}"), i * 16 + 16 * (un // WSLOTS + 1))
                        out_tile(q0 + j, n0 + j // 2, 8 * (j % 2), u2, T2, i * 8 + (q0 + j + 1), None if j else normed)
                for j in range(40, 44):
                    if j % 2 == 0:
                        unit_wait(n0 + j // 2)
                    out_tile(q0 + j, n0 + j // 2, 8 * (j % 2), u2, T2, q0 + j + 1)
                q0, n0 = Q0[down], U0[down]
                pe.wait_ge(sem("prod_ready"), FF * (1 if n == 6 else 2))
                for t in range(DT):
                    unit_wait(n0 + 2 * t)
                    unit_wait(n0 + 2 * t + 1)
                    pe.wait_ge(sem("tile_read"), q0 + t + 1)
                    for s in range(2):
                        for k in range(FF):
                            slot = (n0 + 2 * t + k // DOWN_K) % WSLOTS
                            b = k % DOWN_K
                            m = pe.matmul(pair(q0 + t, s, HALF), ring[:, slot, b * P:(b + 1) * P],
                                          prod[:, k, s * HALF:(s + 1) * HALF], start=(k == 0), stop=(k == FF - 1))
                    m.then_inc(sem("tile_done"), 1)
                    if t:
                        sums(SQ0[n] + t, t - 1, t == 1, False, HALF, True)
                sums(SQ0[n] + DT, DT - 1, False, True, HALF, True)

            pe.wait_ge(sem("attended_read"), len(ATT))
            out_product("out0", [mix0[:, k, :] for k in range(2 * LRU)], ("lru_out", LRU), 4)
            norm_sums(5, True)
            ffn("up0", "down0", 6, 4 * DT)
            norm_sums(7, True)
            q0, n0 = Q0["in2"], U0["in2"]
            with pe.Fori(0, 6) as i:
                for j in range(8):
                    if j % 2 == 0:
                        un = n0 + j // 2
                        pe.wait_ge(sem(f"unit_loaded{un % WSLOTS}"), i * 16 + 16 * (un // WSLOTS + 1))
                    out_tile(q0 + j, n0 + j // 2, 8 * (j % 2), u2, T2, i * 8 + (q0 + j + 1), None if j else 5 * DT)
            for c, (lo, cnt) in enumerate(CH2):
                for k in range(DT):
                    m = pe.matmul(ps[:, 4, SSD_H * c:SSD_H * (c + 1)], u[:, k, lo:lo + P], wdt[:, k, :],
                                  start=(k == 0), stop=(k == DT - 1))
            m.then_inc(sem("dt_done"), 1)
            pe.wait_ge(sem("da_ready"), 1)
            for c, (lo, cnt) in enumerate(CH2):
                pe.matmul(ps[:, 5, SSD_H * c:SSD_H * (c + 1)], upto, da2[:, c, :], start=True, stop=True)
                m = pe.matmul(ps[:, 6, SSD_H * c:SSD_H * (c + 1)], ones[0:cnt, :], da2[0:cnt, c, :], start=True, stop=True)
            m.then_inc(sem("cs2_done"), 1)
            pe.wait_ge(sem("cs2_read"), 1)
            pe.wait_ge(sem("ssm_silu"), 2 * SSD_X)
            SSD = [(c, g) for c in range(len(CH2)) for g in range(SSD_G)]

            def ssd_in(n):
                c, g = SSD[n]
                lo, cnt = CH2[c]
                tok = slice(lo, lo + cnt)
                if n >= 2:
                    pe.wait_ge(sem("ssd_diff"), n - 1)
                b = 2 * (n % 2)
                for e in range(4):
                    pe.matmul(ps[:, b, P * e:P * e + cnt], da2[0:cnt, c, 4 * g + e:4 * g + e + 1].broadcast_to([cnt, P]),
                              upto[0:cnt, 0:cnt], start=True, stop=True)
                B, C = xbc[:, SSD_X + g, tok], xbc[:, SSD_X + SSD_G + g, tok]
                pe.matmul(ps[0:cnt, b + 1, 0:cnt], B, C, start=True, stop=True)
                pe.transpose(ps[0:cnt, b + 1, P:2 * P], B, ident)
                for e in range(2):
                    m = pe.transpose(ps[0:cnt, b + 1, (2 + e) * P:(3 + e) * P], xbc[:, 2 * g + e, tok], ident)
                m.then_inc(sem("ssd_in_done"), 1)

            def ssd_out(n):
                c, g = SSD[n]
                lo, cnt = CH2[c]
                pe.wait_ge(sem("ssd_dve"), n + 1)
                pe.wait_ge(sem("ssd_pool"), n + 1)
                if n >= 2:
                    pe.wait_ge(sem("ssd_out_read"), n - 1)
                if c:
                    pe.wait_ge(sem("st2_ready"), n - SSD_G + 1)
                for e in range(4):
                    out = ps[64 * (e % 2):64 * (e % 2) + 64, 4 + n % 2, P * (e // 2):P * (e // 2) + cnt]
                    pe.matmul(out, xdt[n % 2][0:cnt, e, :], decay2[n % 2][0:cnt, e, 0:cnt], start=True, stop=(c == 0),
                              tile_position=(0, 64 * (e % 2)))
                    if c:
                        pe.matmul(out, st2[:, 4 * g + e, :], cdec[n % 2][:, e, 0:cnt], start=False, stop=True,
                                  tile_position=(0, 64 * (e % 2)))
                pe.matmul(ps[:, 6 + n % 2, 0:256], b_tok[0:cnt, n % 2, :], xdd[0:cnt, n % 2].rearrange("p h n -> p (h n)"),
                          start=True, stop=True).then_inc(sem("ssd_out_done"), 1)

            ssd_in(0)
            for n in range(len(SSD) + 1):
                if n + 1 < len(SSD):
                    ssd_in(n + 1)
                if n:
                    ssd_out(n - 1)
            for g in range(SSD_G):
                pe.wait_ge(sem("group_squares"), 2 * g + 2)
                if g >= 2:
                    pe.wait_ge(sem("group_root"), g - 1)
                if g < 2:
                    pe.wait_ge(sem("ssd_diff"), len(SSD))
                for e in range(2):
                    for s in range(2):
                        m = pe.matmul(ps[:, 2 * (g % 2) + s, 0:HALF], ones, gsq[e][:, s * HALF:(s + 1) * HALF],
                                      start=(e == 0), stop=(e == 1))
                m.then_inc(sem("group_sums"), 1)
            out_product("out2", [xbc[:, k, :] for k in range(SSD_X)], ("mix2_ready", SSD_X), 8)
            norm_sums(9, True)
            ffn("up2", "down2", 10, 6 * DT)

        @block.scalar
        def _(act):
            def norm_squares(n, src, ready, count0, ncols):
                for k in range(DT):
                    s, v = ready(k)
                    act.wait_ge(sem(s), v)
                    if SQ0[n] + k >= 2:
                        act.wait_ge(sem("squares_used"), SQ0[n] + k - 1)
                    act.activation(sq[:, k % 2, 0:ncols], src(k), ACT.Square).then_inc(sem("squares_ready"), 1)

            def norm_root(n, ncols, banks=None):
                act.wait_ge(sem("squares_used"), SQ0[n] + DT)
                if n:
                    act.wait_ge(sem("norm_applied"), n)
                if ncols > 512:
                    act.activation(halves(rs[:, 0:ncols]), ps[:, 6:8, 0:HALF], ACT.Sqrt, bias=eps, scale=1.0 / D
                                   ).then_inc(sem("root_ready"), 1)
                else:
                    act.activation(rs[:, 0:ncols], ps[:, 6, 0:ncols], ACT.Sqrt, bias=eps, scale=1.0 / D
                                   ).then_inc(sem("root_ready"), 1)

            act.wait_ge(sem("inputs_loaded"), INPUTS)
            act.wait_ge(sem("cz_zeroed"), 1)
            act.activation(cz[:, :, 31], pcol("c", 0, DT), ACT.Silu).then_inc(sem("cz_ready"), 1)
            norm_squares(0, lambda k: h[:, k, META:T2], lambda k: ("inputs_loaded", INPUTS), 0, SEQ)
            norm_root(0, SEQ)
            act.activation(s5s[:, 0, :], pcol("log_step", 0, 16), ACT.Exp).then_inc(sem("s5_step"), 1)
            act.wait_ge(sem("s5_angle"), 1)
            act.activation(s5s[:, 6, :], s5s[:, 5, :], ACT.Exp)
            act.activation(s5s[:, 8, :], s5s[:, 3, :], ACT.Sin)
            act.activation(s5s[:, 7, :], s5s[:, 4, :], ACT.Sin).then_inc(sem("s5_trig"), 1)
            act.wait_ge(sem("mod_done"), 8)
            act.activation(modrow[0:16, :], ps[0:16, 3, 0:P], ACT.Copy).then_inc(sem("mod_copied"), 1)
            def head_root(i):
                act.wait_ge(sem("squares_used"), DT + i + 1)
                if i:
                    act.wait_ge(sem("qk_ready"), i)
                else:
                    act.wait_ge(sem("norm_applied"), 1)
                act.activation(rs[:, 0:SEQ], ps[:, 1, 0:SEQ], ACT.Sqrt, bias=eps).then_inc(sem("l2_read"), 1)

            q0 = Q0["in1"]
            for t in range(NS5):
                act.wait_ge(sem("tile_done"), q0 + t + 1)
                act.activation(us5[:, t, :], pair(q0 + t), ACT.Copy).then_inc(sem("tile_read"), 1)
            for j in range(16):
                q = q0 + NS5 + j
                act.wait_ge(sem("tile_done"), q + 1)
                if j < 12:
                    if j >= 2:
                        act.wait_ge(sem("conv_done"), j - 1)
                    else:
                        act.wait_ge(sem("pads_ready"), 1)
                    act.activation(cbuf[j % 2][:, 3:], pair(q), ACT.Copy).then_inc(sem("tile_read"), 1)
                else:
                    act.activation(z1[:, j - 12, :], pair(q), ACT.Silu).then_inc(sem("tile_read"), 1)
                if 1 <= j < 13:
                    act.wait_ge(sem("conv_done"), j)
                    act.activation(qkv[:, j - 1, :], qkv[:, j - 1, :], ACT.Silu).then_inc(sem("silu_qkv"), 1)
                if j >= 8:
                    act.wait_ge(sem("silu_qkv"), j - 7)
                    act.wait_ge(sem("squares_used"), j - 1)
                    act.activation(sq[:, j % 2, 0:SEQ], qkv[:, j - 8, :], ACT.Square).then_inc(sem("squares_ready"), 1)
                    if j > 8:
                        head_root(j - 9)
            head_root(7)
            act.wait_ge(sem("mod_done"), 24)
            act.activation(modrow, ps[0:32, 3, 0:P], ACT.Copy).then_inc(sem("mod_copied"), 1)
            for t in range(NS5):
                act.wait_ge(sem("y5_ready"), t + 1)
                act.activation(y5[:, t, :], y5[:, t, :], ACT.Gelu_apprx_tanh).then_inc(sem("y5_gelu"), 1)
            act.wait_ge(sem("softplus_arg"), 1)
            act.activation(sp2, sp2, ACT.Exp).then_inc(sem("softplus_exp"), 1)
            act.wait_ge(sem("softplus_one"), 1)
            act.activation(sp3, sp3, ACT.Ln)
            act.activation(sp4[:, 0:HEADS], pcol("a_log", 0, HEADS), ACT.Exp).then_inc(sem("softplus_ln"), 1)
            act.activation(beta.rearrange("p (c h) -> p c h", c=CHUNKS),
                           ps[:, 3, 384:416].rearrange("p (c h) -> p c h", c=CHUNKS)[:, :, HEADS:8], ACT.Sigmoid
                           ).then_inc(sem("beta_ready"), 1)
            for t in range(NS5):
                act.wait_ge(sem("tile_done"), Q0["glu"] + t + 1)
                if t:
                    act.wait_ge(sem("mix1_ready"), t)
                act.activation(sig, pair(Q0["glu"] + t), ACT.Sigmoid, bias=pcol("b_glu", t)
                               ).then_inc(sem("tile_read"), 1)
            act.wait_ge(sem("csum_copied"), 1)
            act.activation(ecs, csum, ACT.Exp)
            act.activation(egt, gtot, ACT.Exp)
            act.activation(etail, etail, ACT.Exp).then_inc(sem("gate_exps"), 1)
            for c in range(CHUNKS):
                act.wait_ge(sem("diff_ready"), c + 1)
                act.activation(dtmp, dtmp, ACT.Exp).then_inc(sem("decay_ready"), 1)
                act.activation(egb, ps[:, 2, :].rearrange("p (h n) -> p h n", h=HEADS), ACT.Exp
                               ).then_inc(sem("egb_ready"), 1)
            for v in range(LEVELS):
                for c in range(CHUNKS):
                    act.wait_ge(sem("ax_done"), CHUNKS * v + c + 1)
                    if v:
                        act.wait_ge(sem("inverse_ready"), CHUNKS * v + c + 1)
                    act.activation(w_mat[:, c], ps[:, c, :].rearrange("p (h n) -> p h n", h=HEADS), ACT.Copy
                                   ).then_inc(sem("ax_read"), 1)
            for c in range(CHUNKS):
                act.wait_ge(sem("solved"), c + 1)
                b = 2 * (c % 2)
                act.activation(val[:, c], ps[:, b, :].rearrange("p (h n) -> p h n", h=HEADS), ACT.Copy)
                act.activation(kc[:, c], ps[:, b + 1, :].rearrange("p (h n) -> p h n", h=HEADS), ACT.Copy
                               ).then_inc(sem("solved_read"), 1)
            def out_root(c):
                act.wait_ge(sem("squares_used"), 16 + c + 1)
                if c:
                    act.wait_ge(sem("mix1_ready"), NS5 + c)
                act.activation(rs[:, 0:SEQ], ps[:, c % 2, 0:SEQ], ACT.Sqrt, bias=eps, scale=1.0 / P
                               ).then_inc(sem("o_norm_read"), 1)

            for c in range(CHUNKS):
                act.wait_ge(sem("chunk_out_done"), c + 1)
                act.wait_ge(sem("squares_used"), 16 + c - 1)
                act.activation(sq[:, c % 2, 0:SEQ], ps[:, 6, :], ACT.Square).then_inc(sem("squares_ready"), 1)
                act.activation(o_gdn[:, :, c * P:(c + 1) * P], ps[:, 6, :].rearrange("p (h n) -> p h n", h=HEADS),
                               ACT.Copy).then_inc(sem("o_read"), 1)
                if c:
                    out_root(c - 1)
            out_root(CHUNKS - 1)

            norm_squares(1, lambda k: h[:, k, META:T2], lambda k: ("tile_read", Q0["out1"] + k + 3), 0, SEQ)
            norm_root(1, SEQ)
            for c in range(CHUNKS):
                for s in range(2):
                    act.wait_ge(sem("xtok_done"), 2 * c + s + 1)
                    act.activation(xtok[:, c, 512 * s:512 * (s + 1)], ps[:, 2 + s, :], ACT.Copy
                                   ).then_inc(sem("xtok_read"), 1)
            act.wait_ge(sem("grp_arg"), 1)
            act.activation(r4[1], r4[1], ACT.Exp).then_inc(sem("grp_exp"), 1)
            act.wait_ge(sem("top_arg"), 1)
            act.activation(r1[6], r1[6], ACT.Exp).then_inc(sem("top_exp"), 1)

            def rows_out_of_psum(b, p, count, waits=True):
                act.wait_ge(sem("xt_done"), count)
                if waits:
                    act.wait_ge(sem("gu_done"), b - 1)
                act.wait_ge(sem("top_exp"), 1)
                act.activation(xbt[p].rearrange("p k n -> p (k n)").rearrange("p (s n) -> p s n", s=2), ps[:, 2:4, :],
                               ACT.Copy).then_inc(sem("xt_read"), 1)

            def gate_silu(b, p):
                act.wait_ge(sem("gu_done"), b + 1)
                if not isinstance(b, int) or b >= 2:
                    act.wait_ge(sem("hidden_ready"), FREE + b - 1)
                act.wait_ge(sem("top_exp"), 1)
                act.activation(silu_b[:, p, :], ps[:, p, 0:D_EXPERT], ACT.Silu).then_inc(sem("silu_ready"), 1)

            def store_block(b, p):
                act.wait_ge(sem("dn_read"), FREE + b + 1)
                act.dma_start(rows_out[bass.ds(b * P, P), :], yb[p]).then_inc(sem(f"rows_stored{p}"), 16)

            rows_out_of_psum(0, 0, 1, False)
            gate_silu(0, 0)
            rows_out_of_psum(1, 1, 2, False)
            with act.Fori(0, PAIRS - 1) as i:
                for p in range(2):
                    b = i * 2 + p
                    act.wait_ge(sem("hidden_ready"), FREE + b)
                    act.wait_ge(sem("gu_done"), b + 2)
                    act.wait_ge(sem("top_exp"), 1)
                    act.activation(silu_b[:, 1 - p, :], ps[:, 1 - p, 0:D_EXPERT], ACT.Silu).then_inc(sem("silu_ready"), 1)
                    rows_out_of_psum(b + 2, p, b + 3)
                    store_block(b, p)
            n = BLOCKS - 3
            gate_silu(n + 1, 1)
            rows_out_of_psum(n + 2, 0, n + 3)
            store_block(n, 0)
            gate_silu(n + 2, 0)
            store_block(n + 1, 1)
            store_block(n + 2, 0)
            act.wait_ge(sem("softplus_arg"), 2)
            act.activation(lam8[:, 1, :], lam8[:, 1, :], ACT.Exp).then_inc(sem("softplus_exp"), 1)
            act.wait_ge(sem("softplus_one"), 2)
            act.activation(lam8[:, 2, :], lam8[:, 2, :], ACT.Ln).then_inc(sem("softplus_ln"), 1)
            norm_squares(2, lambda k: h[:, k, META:T2], lambda k: ("moe_added", k + 1), 0, SEQ)
            norm_root(2, SEQ)

            norm_squares(3, lambda k: h[:, k, :], lambda k: ("normed", 2 * DT + k + 1), 0, T2)
            norm_root(3, T2)
            q0 = Q0["in0"]

            def tile_copy(q, out, func=ACT.Copy, scale=1.0):
                act.wait_ge(sem("tile_done"), q + 1)
                act.activation(halves(out), pair2(q), func, scale=scale).then_inc(sem("tile_read"), 1)

            def lru_functions(i):
                b = i % 2
                act.wait_ge(sem("lru_gates"), i + 1)
                if i >= 2:
                    act.wait_ge(sem("lru_out"), i - 1)
                act.activation(halves(r_lru[:, b, :]), ps[:, 4:6, 0:HALF], ACT.Sigmoid, bias=pcol("b_a", i))
                act.activation(halves(i_lru[:, b, :]), ps[:, 6:8, 0:HALF], ACT.Sigmoid, bias=pcol("b_x", i)
                               ).then_inc(sem("lru_sig"), 1)
                act.drain()
                act.activation(a_lru[:, b, :], r_lru[:, b, :], ACT.Exp, scale=lam8[:, 0, i:i + 1])
                act.activation(t_lru[:, b, :], r_lru[:, b, :], ACT.Tanh, scale=lam8[:, 3, i:i + 1]
                               ).then_inc(sem("lru_decay"), 1)
                act.wait_ge(sem("lru_square"), i + 1)
                act.activation(t_lru[:, b, :], t_lru[:, b, :], ACT.Sqrt).then_inc(sem("lru_root"), 1)

            for i in range(LRU):
                if i >= 2:
                    act.wait_ge(sem("lru_out"), i - 1)
                tile_copy(q0 + 2 * i, g_lru[:, i % 2, :], ACT.Gelu_apprx_tanh)
                if i >= 2:
                    act.wait_ge(sem("lru_conv"), i - 1)
                else:
                    act.wait_ge(sem("pads_ready"), 2)
                tile_copy(q0 + 2 * i + 1, pad[i % 2][:, 3:])
                if i:
                    lru_functions(i - 1)
            for t in range(Q_TILES):
                tile_copy(q0 + 2 * LRU + t, q_fm[:, t, :], scale=HEAD ** -0.5)
                if t == 0:
                    lru_functions(LRU - 1)
            for t in range(2):
                tile_copy(q0 + 24 + t, k_fm[:, t, :])
            tile_copy(q0 + 26, v_fm)
            act.wait_ge(sem("v_turned"), 1)
            act.activation(v_tok[0:META, 0, :], ps[0:META, 4, 0:P], ACT.Copy)
            act.activation(v_tok[:, 1:4, :], ps[:, 4, P:].rearrange("p (c n) -> p c n", c=3), ACT.Copy)
            act.activation(v_tok[:, 4, :], ps[:, 5, 0:P], ACT.Copy).then_inc(sem("v_read"), 1)
            ATT = [(c, hp) for c in range(len(CH2)) for hp in range(Q_TILES)]
            for n in range(len(ATT) + 2):
                if n < len(ATT):
                    c, hp = ATT[n]
                    cnt, nk, b = CH2[c][1], (META, META + P, META + 2 * P, META + 2 * P, META + 2 * P)[c], n % 2
                    act.wait_ge(sem("max_ready"), n + 1)
                    for e in range(2):
                        x = prob[0:cnt, b, e, 0:nk]
                        nm = stat[0:cnt, b, 1, e:e + 1]
                        act.activation(x, x, ACT.Exp, bias=nm, accum_out=stat[0:cnt, b, 2, e:e + 1])
                        m = act.activation(stat[0:cnt, b, 3, e:e + 1], pcol("sinks", 2 * hp + e)[0:cnt, :], ACT.Exp, bias=nm)
                    m.then_inc(sem("exp_ready"), 1)
                if 1 <= n <= len(ATT):
                    c, hp = ATT[n - 1]
                    cnt, b = CH2[c][1], (n - 1) % 2
                    act.wait_ge(sem("prob_turned"), n)
                    if n >= 3:
                        act.wait_ge(sem("attended"), n - 2)
                    m = act.activation(prob_t[0:META, b, :, 0:cnt], ps[0:META, 4:6, 0:cnt], ACT.Copy)
                    if c:
                        w = P if c == 1 else 2 * P
                        m = act.activation(prob_t[:, b, :, P:P + w], ps[:, 4:6, P:P + w], ACT.Copy)
                    m.then_inc(sem("prob_turned_read"), 1)
                if n >= 2:
                    c, hp = ATT[n - 2]
                    lo, cnt = CH2[c]
                    act.wait_ge(sem("attended"), n - 1)
                    act.activation(mix0[:, LRU + hp, lo:lo + cnt], ps[:, 6 + n % 2, 0:cnt], ACT.Copy
                                   ).then_inc(sem("attended_read"), 1)

            def product_out(stage, dst, n):
                for t in range(DT):
                    q = Q0[stage] + t
                    act.wait_ge(sem("tile_done"), q + 1)
                    act.wait_ge(sem("squares_used"), SQ0[n] + t - 1)
                    act.activation(halves(sq[:, t % 2, :]), pair2(q), ACT.Square).then_inc(sem("squares_ready"), 1)
                    act.activation(halves(dst[:, t, :]), pair2(q), ACT.Copy).then_inc(sem("tile_read"), 1)
                norm_root(n, T2)

            def ffn(up, down, n, run):
                norm_squares(n - 1, lambda k: h[:, k, :], lambda k: ("h_updated", DT * (n - 6) // 2 + k + 1), 0, T2)
                norm_root(n - 1, T2)
                q0, c0 = Q0[up], 2 + 2 * FF * run
                with act.Fori(0, FF // 2) as i:
                    for j in range(2):
                        for e in range(2):
                            act.wait_ge(sem("tile_done"), i * 4 + (q0 + 2 * j + e + 1))
                            act.wait_ge(sem("ffn_conv"), i * 4 + (c0 + 2 * j + e - 1))
                            act.wait_ge(sem("pads_ready"), 2)
                            act.activation(halves(pad[e][:, 3:]), pair2(q0 + e), ACT.Copy).then_inc(sem("tile_read"), 1)
                        act.wait_ge(sem("ffn_conv"), i * 4 + (c0 + 2 * j + 1))
                        act.wait_ge(sem("pads_ready"), 2)
                        act.activation(gact, gact, ACT.Gelu_apprx_tanh).then_inc(sem("ffn_gelu"), 1)
                product_out(down, m_out, n)

            product_out("out0", m_out, 4)
            ffn("up0", "down0", 6, 0)
            norm_squares(7, lambda k: h[:, k, :], lambda k: ("h_updated", DT + k + 1), 0, T2)
            norm_root(7, T2)
            q0 = Q0["in2"]
            with act.Fori(0, SSD_X // 2) as i:
                for j in range(2):
                    act.wait_ge(sem("tile_done"), i * 2 + (q0 + j + 1))
                    act.wait_ge(sem("pads_ready"), 2)
                    act.activation(halves(z2[:, bass.ds(i * 2 + j, 1), :].rearrange("p o n -> p (o n)")), pair2(q0 + j), ACT.Silu
                                   ).then_inc(sem("tile_read"), 1)
            q0 += SSD_X

            def ssm_tile(t, par):
                act.wait_ge(sem("tile_done"), t + (q0 + 1))
                act.wait_ge(sem("ssm_conv"), t + 1)
                act.wait_ge(sem("pads_ready"), 2)
                act.activation(halves(pad[par][:, 3:]), pair2(q0 + par), ACT.Copy).then_inc(sem("tile_read"), 1)

            def ssm_silu(t):
                act.wait_ge(sem("ssm_conv"), t + 3)
                act.wait_ge(sem("pads_ready"), 2)
                x = xbc[:, t, :] if isinstance(t, int) else xbc[:, bass.ds(t, 1), :].rearrange("p o n -> p (o n)")
                act.activation(x, x, ACT.Silu).then_inc(sem("ssm_silu"), 1)

            ssm_tile(0, 0)
            with act.Fori(0, SSD_X - 1) as i:
                for j in range(2):
                    ssm_tile(i * 2 + (j + 1), 1 - j)
                    ssm_silu(i * 2 + j)
            ssm_tile(2 * SSD_X - 1, 1)
            ssm_silu(2 * SSD_X - 2)
            ssm_silu(2 * SSD_X - 1)
            act.wait_ge(sem("softplus_arg"), 3)
            act.activation(sb2, sb2, ACT.Exp).then_inc(sem("softplus_exp"), 1)
            act.wait_ge(sem("softplus_one"), 3)
            act.activation(sc2, sc2, ACT.Ln)
            act.activation(egt2[:, 0, :], pcol("a_log2", 0, SSD_H), ACT.Exp).then_inc(sem("softplus_ln"), 1)
            act.wait_ge(sem("tail_arg"), 1)
            act.activation(tail2, tail2, ACT.Exp)
            act.activation(egt2, gt2_, ACT.Exp).then_inc(sem("tail_ready"), 1)
            SSD = [(c, g) for c in range(len(CH2)) for g in range(SSD_G)]
            for n, (c, g) in enumerate(SSD):
                cnt = CH2[c][1]
                bank = ps[:, 2 * (n % 2), :].rearrange("p (h n) -> p h n", h=4)
                act.wait_ge(sem("ssd_in_done"), n + 1)
                if n >= 2:
                    act.wait_ge(sem("ssd_pool"), n - 1)
                act.activation(eg2[n % 2][:, :, 0:cnt], bank[:, :, 0:cnt], ACT.Exp).then_inc(sem("ssd_eg"), 1)
                act.wait_ge(sem("ssd_diff"), n + 1)
                d = decay2[n % 2][0:cnt, :, 0:cnt]
                act.activation(d, d, ACT.Exp).then_inc(sem("ssd_decay"), 1)
            for g in range(SSD_G):
                for e in range(2):
                    act.wait_ge(sem("gated"), 2 * g + e + 1)
                    if g:
                        act.wait_ge(sem("group_sums"), g)
                    act.activation(gsq[e], xbc[:, 2 * g + e, :], ACT.Square).then_inc(sem("group_squares"), 1)
                act.wait_ge(sem("group_sums"), g + 1)
                if g >= 2:
                    act.wait_ge(sem("mix2_ready"), 2 * (g - 1))
                act.activation(halves(groot[g % 2]), ps[:, 2 * (g % 2):2 * (g % 2) + 2, 0:HALF], ACT.Sqrt, bias=eps,
                               scale=1.0 / (2 * P)).then_inc(sem("group_root"), 1)
            product_out("out2", m2_out, 8)
            ffn("up2", "down2", 10, 1)

        INV_2PI = float(np.float32(1 / (2 * np.pi)))
        ROUND = 12582912.0
        PI_A = 6.28125
        PI_B = float(np.float32(np.floor((2 * np.pi - PI_A) * 2 ** 21) / 2 ** 21))
        PI_C = float(np.float32(2 * np.pi - PI_A - PI_B))

        @block.vector
        def _(dve):
            def ts(out, x, s1, s2, op0, op1=None):
                return dve.tensor_scalar(out, x, s1, s2, op0, op1) if op1 is not None else dve.tensor_scalar(out, x, s1, None, op0)

            def tt(out, x, y, op):
                return dve.tensor_tensor(out, x, y, op)

            def stt(out, x, s, y, op0, op1):
                return dve.scalar_tensor_tensor(out=out, in0=x, scalar=s, in1=y, op0=op0, op1=op1)

            mul, add, sub, lo_, hi_ = ALU.mult, ALU.add, ALU.subtract, ALU.min, ALU.max

            def norm_apply(n, gain, src, dst, ncols, shift=None):
                dve.wait_ge(sem("root_ready"), n + 1)
                dve.reciprocal(rs[:, 0:ncols], rs[:, 0:ncols])
                dve.drain()
                if shift is None:
                    for k in range(DT):
                        stt(dst(k), src(k), gain(k), rs[:, 0:ncols], mul, mul).then_inc(sem("normed"), 1)
                else:
                    stt(dst(0), src(0), gain(0), rs[:, 0:ncols], mul, mul)
                    for k in range(DT):
                        if k + 1 < DT:
                            stt(dst(k + 1), src(k + 1), gain(k + 1), rs[:, 0:ncols], mul, mul)
                        dve.drain()
                        ts(dst(k), dst(k), shift(k), None, add).then_inc(sem("normed"), 1)
                dve.drain().then_inc(sem("norm_applied"), 1)

            def conv(out, buf, taps, w, bias, ncols):
                n = taps - 1
                if bias is None:
                    ts(out, buf[:, n:n + ncols], w(n), None, mul)
                else:
                    ts(out, buf[:, n:n + ncols], w(n), bias, mul, add)
                for t in range(n - 1, -1, -1):
                    dve.drain()
                    m = stt(out, buf[:, t:t + ncols], w(t), out, mul, add)
                return m

            def log1p_args(x, m, e):
                ts(m, x, 0.0, None, hi_)
                ts(e, x, -1.0, None, mul)
                dve.drain()
                return tt(e, e, x, lo_)

            dve.memset(cz, 0.0).then_inc(sem("cz_zeroed"), 1)
            dve.memset(zeros, 0.0).then_inc(sem("zeros_ready"), 1)
            dve.memset(tmp[:, 0, 0:3], 0.0).then_inc(sem("tile_read"), 1)
            dve.memset(tmp[:, 1, 0:3], 0.0).then_inc(sem("tile_read"), 1)
            dve.drain().then_inc(sem("pads_ready"), 1)
            dve.wait_ge(sem("inputs_loaded"), INPUTS)
            S = lambda n: s5s[:, n, :]
            lr, li = pcol("lam_re", 0, 16), pcol("lam_im", 0, 16)
            dve.wait_ge(sem("s5_step"), 1)
            tt(S(5), lr, S(0), mul)
            tt(S(1), li, S(0), mul)
            dve.drain()
            ts(S(2), S(1), INV_2PI, ROUND, mul, add)
            dve.drain()
            ts(S(2), S(2), -ROUND, None, add)
            dve.drain()
            for part in (PI_A, PI_B, PI_C):
                stt(S(1), S(2), -part, S(1), mul, add)
                dve.drain()
            ts(S(3), S(1), float(np.float32(3.1415925)), -float(np.float32(3.1415925)), lo_, hi_)
            dve.drain()
            ts(S(4), S(3), -1.0, None, mul)
            dve.drain()
            tt(S(4), S(4), S(3), hi_)
            dve.drain()
            ts(S(4), S(4), -1.0, float(np.float32(np.pi / 2)), mul, add).then_inc(sem("s5_angle"), 1)
            dve.wait_ge(sem("s5_trig"), 1)
            tt(S(15), S(6), S(7), mul)
            tt(S(10), S(6), S(8), mul)
            tt(S(11), lr, lr, mul)
            tt(S(17), li, li, mul)
            dve.drain()
            ts(S(9), S(15), -1.0, None, add)
            tt(S(11), S(11), S(17), add)
            dve.drain()
            dve.reciprocal(S(12), S(11))
            tt(S(17), S(9), lr, mul)
            tt(S(18), S(10), li, mul)
            tt(S(19), S(10), lr, mul)
            tt(S(20), S(9), li, mul)
            dve.drain()
            tt(S(17), S(17), S(18), add)
            tt(S(19), S(19), S(20), sub)
            dve.drain()
            tt(S(13), S(17), S(12), mul)
            tt(S(14), S(19), S(12), mul)
            dve.drain()
            wide = lambda x: x.unsqueeze(2).broadcast_to([P, S5_TILES, 32])
            for n, (p_, q_) in enumerate(((13, 14), (14, 13))):
                t1, t2 = p5[0].rearrange("p (j n) -> p j n", n=32), p5[1].rearrange("p (j n) -> p j n", n=32)
                tt(t1, s5c[0], wide(S(p_)), mul)
                tt(t2, s5c[1], wide(S(q_)), mul)
                dve.drain()
                if n == 0:
                    tt(s5ck[0], t1, t2, sub)
                else:
                    tt(t1, t1, t2, add)
                    dve.drain()
                    ts(s5ck[1], t1, -1.0, None, mul)
                dve.drain()
            dve.wait_ge(sem("mod_turned"), 1)
            tt(mod[:, 0:16], ps[:, 3, 256:272], pcol("b_ada", 0, 16), add).then_inc(sem("mod_read"), 1)
            dve.drain()
            stt(modg[:, 0:DT], mod[:, DT:2 * DT], 1.0, pcol("norm1_g", 0, DT), add, mul)
            dve.drain()
            norm_apply(0, lambda k: modg[:, k:k + 1], lambda k: h[:, k, META:T2], lambda k: u[:, k, 0:SEQ], SEQ,
                       lambda k: mod[:, k:k + 1])
            dve.tensor_copy(S(15), S(7))
            dve.tensor_copy(S(16), S(8))
            for tab, size in ((fine, 32), (coarse, 16)):
                dve.memset(tab[0][:, :, 0:1], 1.0)
                dve.memset(tab[1][:, :, 0:1], 0.0)
                n = 1
                while n < size:
                    dve.drain()
                    wc, ws = (S(x).unsqueeze(2).broadcast_to([P, S5_TILES, n]) for x in (15, 16))
                    t = [p5[x][:, 0:S5_TILES * n].rearrange("p (j n) -> p j n", n=n) for x in range(4)]
                    tt(t[0], tab[0][:, :, 0:n], wc, mul)
                    tt(t[1], tab[1][:, :, 0:n], ws, mul)
                    tt(t[2], tab[0][:, :, 0:n], ws, mul)
                    tt(t[3], tab[1][:, :, 0:n], wc, mul)
                    tt(S(17), S(15), S(15), mul)
                    tt(S(18), S(16), S(16), mul)
                    tt(S(19), S(15), S(16), mul)
                    dve.drain()
                    tt(tab[0][:, :, n:2 * n], t[0], t[1], sub)
                    tt(tab[1][:, :, n:2 * n], t[2], t[3], add)
                    tt(S(15), S(17), S(18), sub)
                    ts(S(16), S(19), 2.0, None, mul)
                    n *= 2
                dve.drain()
            dve.drain().then_inc(sem("powers_ready"), 1)
            def head_normed(i):
                dve.wait_ge(sem("l2_read"), i + 1)
                dve.reciprocal(rs[:, 0:SEQ], rs[:, 0:SEQ])
                dve.drain()
                stt(qkv[:, i, :], qkv[:, i, :], float(P) ** -0.5 if i < HEADS else 1.0, rs[:, 0:SEQ], mul, mul
                    ).then_inc(sem("qk_ready"), 1)

            q0 = Q0["in1"]
            for j in range(S5_TILES):
                if j < 12:
                    dve.wait_ge(sem("tile_read"), q0 + NS5 + j + 3)
                    conv(qkv[:, j, :], cbuf[j % 2], CONV_C, lambda t: pcol("conv_w", 12 * t + j), None, SEQ
                         ).then_inc(sem("conv_done"), 1)
                dve.wait_ge(sem("table_ready"), j + 1)
                dve.wait_ge(sem("s5_in_done"), j + 1)
                C, Sn = table[j % 2]
                dve.drain()
                bu, bw = ps[:, 4, 0:SEQ], ps[:, 5, 0:SEQ]
                tt(f5[0], bu, C, mul)
                tt(p5[0], bw, Sn, mul)
                tt(f5[1], bw, C, mul)
                tt(p5[1], bu, Sn, mul).then_inc(sem("s5_in_read"), 1)
                dve.drain()
                tt(f5[0], f5[0], p5[0], add)
                tt(f5[1], f5[1], p5[1], sub)
                dve.drain()
                rho = s5s[:, 6, j:j + 1].broadcast_to([P, SEQ])
                dve.tensor_tensor_scan(z5[0], rho, f5[0], 0.0, mul, add)
                dve.tensor_tensor_scan(z5[1], rho, f5[1], 0.0, mul, add)
                dve.drain()
                tt(p5[0], z5[0], C, mul)
                tt(p5[1], z5[1], Sn, mul)
                tt(p5[2], z5[0], Sn, mul)
                tt(p5[3], z5[1], C, mul).then_inc(sem("table_used"), 1)
                dve.drain()
                if j >= 2:
                    dve.wait_ge(sem("s5_out_done"), j - 1)
                tt(st5[j % 2][0], p5[0], p5[1], sub)
                tt(st5[j % 2][1], p5[2], p5[3], add).then_inc(sem("s5_state_ready"), 1)
                if j >= 9:
                    head_normed(j - 9)
                if j >= 4 and j % 4 == 0:
                    t = j // 4 - 1
                    dve.wait_ge(sem("s5_out_done"), 4 * t + 4)
                    stt(y5[:, t, :], us5[:, t, :], pcol("s5_d", t), ps[:, 6 + t % 2, 0:SEQ], mul, add
                        ).then_inc(sem("y5_ready"), 1)
            head_normed(7)
            dve.wait_ge(sem("s5_out_done"), S5_TILES)
            stt(y5[:, 3, :], us5[:, 3, :], pcol("s5_d", 3), ps[:, 7, 0:SEQ], mul, add).then_inc(sem("y5_ready"), 1)
            dve.wait_ge(sem("mod_turned"), 2)
            tt(mod[:, 16:48], ps[:, 3, 256:288], pcol("b_ada", 16, 32), add).then_inc(sem("mod_read"), 1)
            dve.drain()
            stt(modg[:, DT:2 * DT], mod[:, 4 * DT:5 * DT], 1.0, pcol("norm2_g", 0, DT), add, mul)
            ab = ps[:, 3, 384:416].rearrange("p (c h) -> p c h", c=CHUNKS)
            ch = lambda x: x.rearrange("p (c h) -> p c h", c=CHUNKS)
            per_head = lambda x: x.unsqueeze(1).broadcast_to([P, CHUNKS, HEADS])
            dve.wait_ge(sem("gates_done"), 1)
            tt(ch(sp1), ab[:, :, 0:HEADS], per_head(pcol("dt_bias", 0, HEADS)), add)
            dve.drain()
            ts(gate, sp1, 0.0, None, hi_)
            ts(sp2, sp1, -1.0, None, mul)
            dve.drain()
            tt(sp2, sp2, sp1, lo_).then_inc(sem("softplus_arg"), 1)
            dve.wait_ge(sem("softplus_exp"), 1)
            ts(sp3, sp2, 1.0, None, add)
            dve.drain()
            stt(bcs, sp3, -1.0, sp2, add, sub)
            dve.reciprocal(etail, sp3)
            dve.drain()
            tt(bcs, bcs, etail, mul).then_inc(sem("softplus_one"), 1)
            dve.wait_ge(sem("softplus_ln"), 1)
            tt(sp3, sp3, bcs, sub)
            dve.drain()
            tt(gate, gate, sp3, add)
            dve.drain()
            stt(ch(gate), ch(gate), -1.0, per_head(sp4[:, 0:HEADS]), mul, mul).then_inc(sem("gate_ready"), 1)
            for t in range(NS5):
                dve.wait_ge(sem("tile_read"), Q0["glu"] + t + 3)
                tt(mix[:, t, :], y5[:, t, :], sig, mul).then_inc(sem("mix1_ready"), 1)
            dve.wait_ge(sem("csum_done"), 1)
            dve.wait_ge(sem("beta_ready"), 1)
            dve.tensor_copy(csum, ps[:, 3, 448:464])
            dve.tensor_copy(gtot, ps[:, 3, 480:496]).then_inc(sem("csum_read"), 1)
            dve.drain()
            tt(etail, gtot, csum, sub).then_inc(sem("csum_copied"), 1)
            dve.wait_ge(sem("gate_exps"), 1)
            tt(bcs, beta, ecs, mul)
            dve.drain()
            heads = lambda b: ps[:, b, :].rearrange("p (h n) -> p h n", h=HEADS)
            for c in range(CHUNKS):
                per_tok = lambda x: x[:, 4 * c:4 * c + 4].unsqueeze(2).broadcast_to([P, HEADS, P])
                all_heads = lambda x: x.unsqueeze(1).broadcast_to([P, HEADS, P])
                dve.wait_ge(sem("sums_spread"), c + 1)
                if c:
                    dve.drain()
                tt(dtmp, heads(2), per_tok(csum), sub)
                dve.drain()
                ts(dtmp, dtmp, 0.0, None, lo_).then_inc(sem("diff_ready"), 1)
                dve.wait_ge(sem("turned"), c + 1)
                bank = 4 + 2 * (c % 2)
                tt(kb_g[:, c], heads(bank), per_tok(bcs), mul)
                tt(k_tail[:, c], heads(bank), per_tok(etail), mul)
                tt(v_b[:, c], heads(bank + 1), per_tok(beta), mul).then_inc(sem("turned_read"), 1)
                dve.wait_ge(sem("decay_ready"), c + 1)
                dve.wait_ge(sem("chunk_done"), c + 1)
                tt(amat[:, c], dtmp, heads(0), mul)
                tt(qk_d[:, c], dtmp, heads(1), mul)
                dve.drain()
                tt(qk_d[:, c], qk_d[:, c], all_heads(upto), mul)
                tt(amat[:, c], amat[:, c], heads(3), mul).then_inc(sem("a_ready"), 1)
                dve.wait_ge(sem("egb_ready"), c + 1)
                tt(q_dec[:, c], qkv[:, 0:HEADS, c * P:(c + 1) * P], egb, mul).then_inc(sem("chunk_read"), 1)
            dve.drain()
            dve.wait_ge(sem("turned"), CHUNKS)
            dve.wait_ge(sem("chunk_done"), CHUNKS)
            for c in range(CHUNKS):
                for x in (x_inv, y_inv):
                    m = dve.tensor_copy(x[:, c], ident.unsqueeze(1).broadcast_to([P, HEADS, P]))
                m.then_inc(sem("inverse_ready"), 1)
            dve.drain()
            for v in range(LEVELS):
                for c in range(CHUNKS):
                    dve.wait_ge(sem("xax_done"), CHUNKS * v + c + 1)
                    b = 4 + 2 * (c % 2)
                    tt(x_inv[:, c], x_inv[:, c], heads(b), sub)
                    tt(y_inv[:, c], y_inv[:, c], heads(b + 1), sub).then_inc(sem("inverse_ready"), 1)
                dve.drain()
            dve.memset(state[0], 0.0).then_inc(sem("state_ready"), 1)
            dve.wait_ge(sem("rows_zeroed"), 16)
            def out_normed(c):
                tok = slice(c * P, (c + 1) * P)
                dve.wait_ge(sem("o_norm_read"), c + 1)
                dve.reciprocal(rs[:, 0:SEQ], rs[:, 0:SEQ])
                dve.drain()
                stt(mix[:, NS5:, tok], o_gdn[:, :, tok], pcol("gdn_norm_g"),
                    rs[:, 0:SEQ].rearrange("p (h n) -> p h n", h=HEADS), mul, mul)
                dve.drain()
                tt(mix[:, NS5:, tok], mix[:, NS5:, tok], z1[:, :, tok], mul).then_inc(sem("mix1_ready"), 1)

            for c in range(CHUNKS):
                dve.wait_ge(sem("seen_done"), c + 1)
                if c:
                    dve.wait_ge(sem("chunk_out_done"), c)
                tt(v_new, val[:, c], heads(4), sub).then_inc(sem("v_new_ready"), 1)
                if c < CHUNKS - 1:
                    dve.wait_ge(sem("state_added"), c + 1)
                    for hd in range(HEADS):
                        m = stt(state[(c + 1) % 2][:, hd, :], state[c % 2][:, hd, :], egt[:, 4 * c + hd:4 * c + hd + 1],
                                ps[:, 5, hd * P:(hd + 1) * P], mul, add)
                    m.then_inc(sem("state_ready"), 1)
                    dve.drain()
                if c:
                    out_normed(c - 1)
            out_normed(CHUNKS - 1)
            for t in range(DT):
                dve.wait_ge(sem("tile_done"), Q0["out1"] + t + 1)
                stt(h[:, t, META:T2], pair(Q0["out1"] + t), mod[:, 2 * DT + t:2 * DT + t + 1], h[:, t, META:T2], mul, add
                    ).then_inc(sem("tile_read"), 1)

            norm_apply(1, lambda k: modg[:, DT + k:DT + k + 1], lambda k: h[:, k, META:T2], lambda k: u[:, k, 0:SEQ], SEQ,
                       lambda k: mod[:, 3 * DT + k:3 * DT + k + 1])
            dve.wait_ge(sem("router_done"), 1)
            for s in range(2):
                dve.tensor_copy(logit[:, 2 * s:2 * s + 2, :], ps[:, 4 * s:4 * s + 2, 0:GROUPS + EXPERTS])
            dve.drain()
            lg, le = logit[:, :, 0:GROUPS], logit[:, :, GROUPS:]
            over = lambda x, n: x.unsqueeze(2).broadcast_to([P, CHUNKS, n])
            const = lambda name, n: ccol(name, 0, n).unsqueeze(1).broadcast_to([P, CHUNKS, n])

            def first_max(x, n, rank, m, one, t, r):
                dve.tensor_reduce(m, x, AX, hi_)
                dve.drain()
                tt(t, x, over(m, n), ALU.is_equal)
                dve.drain()
                tt(t, t, const(rank, n), mul)
                dve.drain()
                dve.tensor_reduce(r, t, AX, hi_)
                dve.drain()
                tt(one, t, over(r, n), ALU.is_equal)

            first_max(lg, GROUPS, "grp_rank", r1[0], r4[0], r4[2], r1[1])
            tt(r4[1], lg, over(r1[0], GROUPS), sub).then_inc(sem("grp_arg"), 1)
            dve.drain()
            ts(r4[2], r4[0], -1.0, FAR, add, mul)
            dve.drain()
            eight = lambda x: x.unsqueeze(3).broadcast_to([P, CHUNKS, GROUPS, 8])
            by_group = lambda x: x.rearrange("p c (g e) -> p c g e", g=GROUPS)
            tt(by_group(r32[0]), by_group(le), eight(r4[0]), mul)
            dve.drain()
            tt(by_group(r32[0]), by_group(r32[0]), eight(r4[2]), add)
            dve.drain()
            first_max(r32[0], EXPERTS, "exp_rank", r1[2], r32[1], r32[4], r1[1])
            dve.drain()
            stt(r32[2], r32[1], -2.0 * FAR, r32[0], mul, add)
            dve.drain()
            first_max(r32[2], EXPERTS, "exp_rank", r1[3], r32[3], r32[4], r1[1])
            tt(r1[6], r1[3], r1[2], sub).then_inc(sem("top_arg"), 1)
            dve.drain()
            tt(r32[5], r32[1], r32[3], add).then_inc(sem("chosen_ready"), 1)
            dve.wait_ge(sem("grp_exp"), 1)
            dve.tensor_reduce(r1[4], r4[1], AX, add)
            dve.wait_ge(sem("top_exp"), 1)
            ts(r1[5], r1[6], 1.0, None, add)
            dve.drain()
            tt(r1[4], r1[4], r1[5], mul)
            dve.drain()
            dve.reciprocal(r1[7], r1[4])
            dve.drain()
            tt(r1[8], r1[7], r1[6], mul)
            dve.wait_ge(sem("places_done"), 1)
            dve.tensor_copy(e32[0], ps[:, 1, 128:160])
            dve.memset(e32[4], 1.0)
            dve.drain()
            ts(e32[1], e32[0], 0.0, None, ALU.is_gt)
            for v in (1, 2, 3):
                dve.drain()
                stt(e32[1], e32[0], 128.0 * v, e32[1], ALU.is_gt, add)
            dve.drain()
            dve.tensor_tensor_scan(e32[2], e32[4], e32[1], 0.0, mul, add)
            dve.drain()
            tt(e32[2], e32[2], e32[1], sub)
            dve.drain()
            ts(e32[3], e32[2], ccol("row"), None, ALU.is_le)
            ts(e32[5], e32[2], float(P), None, mul)
            dve.drain()
            dve.tensor_reduce(ecol[:, 1:2], e32[3], AX, add)
            dve.drain()
            ts(ecol[:, 0:1], ecol[:, 1:2], -1.0, None, add).then_inc(sem("ecol_ready"), 1)
            tt(r32[4], ps[:, 1, 0:128].rearrange("p (c n) -> p c n", c=CHUNKS),
               e32[5].unsqueeze(1).broadcast_to([P, CHUNKS, EXPERTS]), add)
            dve.drain()
            tt(r32[0], r32[4], r32[1], mul)
            tt(r32[2], r32[4], r32[3], mul)
            dve.drain()
            dve.tensor_reduce(slots[:, 0:CHUNKS], r32[0], AX, add)
            dve.tensor_reduce(slots[:, CHUNKS:], r32[2], AX, add)
            dve.drain()
            dve.tensor_copy(slot_id, slots).then_inc(sem("slots_ready"), 1)
            dve.wait_ge(sem("erow_done"), 1)
            dve.tensor_copy(eid[0:1, :], ps[0:1, 5, 0:P]).then_inc(sem("expert_ids"), 1)
            dve.drain().then_inc(sem("erow_read"), 1)

            def hidden(b, p, count):
                dve.wait_ge(sem("silu_ready"), count)
                if not isinstance(b, int) or b >= 2:
                    dve.wait_ge(sem("ht_done"), FREE + b - 1)
                tt(h_b[:, p, :], silu_b[:, p, :], ps[:, p, D_EXPERT:], mul).then_inc(sem("hidden_ready"), 1)

            def hidden_out_of_psum(b):
                dve.wait_ge(sem("ht_done"), FREE + b + 1)
                dve.wait_ge(sem("dn_done"), FREE + b)
                dve.tensor_copy(ht_b, ps[:, 4, 0:2 * P].rearrange("p (k n) -> p k n", k=2)).then_inc(sem("ht_read"), 1)

            def rows_ready(b, p, stored):
                dve.wait_ge(sem("dn_done"), FREE + b + 1)
                dve.wait_ge(sem(f"rows_stored{p}"), stored)
                dve.tensor_copy(yb[p].rearrange("p (s n) -> p s n", s=2), ps[:, 5:7, :]).then_inc(sem("dn_read"), 1)

            dve.drain().then_inc(sem("rows_stored0"), 16 * FREE)
            dve.drain().then_inc(sem("rows_stored1"), 16 * FREE)
            dve.drain().then_inc(sem("hidden_ready"), FREE)
            dve.drain().then_inc(sem("ht_read"), FREE)
            dve.drain().then_inc(sem("dn_read"), FREE)
            hidden(0, 0, 1)
            with dve.Fori(0, PAIRS - 1) as i:
                for p in range(2):
                    b = i * 2 + p
                    hidden_out_of_psum(b)
                    dve.wait_ge(sem("silu_ready"), b + 2)
                    dve.wait_ge(sem("ht_done"), FREE + b)
                    tt(h_b[:, 1 - p, :], silu_b[:, 1 - p, :], ps[:, 1 - p, D_EXPERT:], mul
                       ).then_inc(sem("hidden_ready"), 1)
                    rows_ready(b, p, i * 16 + 16 * FREE)
            n = BLOCKS - 3
            hidden_out_of_psum(n)
            hidden(n + 1, 1, n + 2)
            rows_ready(n, 0, 16 * (PAIRS - 1) + 16 * FREE)
            hidden_out_of_psum(n + 1)
            hidden(n + 2, 0, n + 3)
            rows_ready(n + 1, 1, 16 * (PAIRS - 1) + 16 * FREE)
            hidden_out_of_psum(n + 2)
            rows_ready(n + 2, 0, 16 * PAIRS + 16 * FREE)
            L = lambda n: lam8[:, n, :]
            ts(L(3), pcol("lam", 0, LRU), -1.0, None, mul)
            dve.drain()
            log1p_args(L(3), L(0), L(1)).then_inc(sem("softplus_arg"), 1)
            dve.wait_ge(sem("softplus_exp"), 2)
            ts(L(2), L(1), 1.0, None, add)
            dve.drain()
            stt(L(3), L(2), -1.0, L(1), add, sub)
            dve.drain()
            dve.reciprocal(L(1), L(2))
            dve.drain()
            tt(L(3), L(3), L(1), mul).then_inc(sem("softplus_one"), 1)
            dve.wait_ge(sem("softplus_ln"), 2)
            tt(L(2), L(2), L(3), sub)
            dve.drain()
            tt(L(2), L(2), L(0), add)
            dve.drain()
            ts(L(0), L(2), -8.0, None, mul)
            ts(L(3), L(2), 8.0, None, mul)
            for c in range(CHUNKS):
                dve.wait_ge(sem("rows_gathered"), 16 * 8)
                ts(moe[:, c, :], y1[:, c, :], r1[7][:, c:c + 1], None, mul)
                dve.drain()
                stt(moe[:, c, :], y2[:, c, :], r1[8][:, c:c + 1], moe[:, c, :], mul, add).then_inc(sem("moe_ready"), 1)
            for k in range(DT):
                dve.wait_ge(sem("moe_turned"), k + 1)
                stt(h[:, k, META:T2], ps[:, k % 2, :], mod[:, 5 * DT + k:5 * DT + k + 1], h[:, k, META:T2], mul, add
                    ).then_inc(sem("moe_added"), 1)
            dve.drain()
            norm_apply(2, lambda k: pcol("normf_g", k), lambda k: h[:, k, META:T2], lambda k: h[:, k, META:T2], SEQ)

            norm_apply(3, lambda k: pcol("pre0", k), lambda k: h[:, k, :], lambda k: u[:, k, :], T2)
            for b in range(2):
                dve.memset(tmp[:, b, 0:3], 0.0)
            dve.drain().then_inc(sem("pads_ready"), 1)
            dve.drain().then_inc(sem("ffn_conv"), 2)
            dve.drain().then_inc(sem("ssm_conv"), 2)
            q0 = Q0["in0"]

            def lru_tail(i):
                b = i % 2
                dve.wait_ge(sem("lru_decay"), i + 1)
                tt(r_lru[:, b, :], a_lru[:, b, :], a_lru[:, b, :], mul)
                tt(i_lru[:, b, :], i_lru[:, b, :], x_lru[:, b, :], mul)
                dve.drain()
                stt(t_lru[:, b, :], r_lru[:, b, :], 1.0, t_lru[:, b, :], add, mul).then_inc(sem("lru_square"), 1)
                dve.wait_ge(sem("lru_root"), i + 1)
                tt(i_lru[:, b, :], i_lru[:, b, :], t_lru[:, b, :], mul)
                dve.drain()
                dve.tensor_tensor_scan(r_lru[:, b, :], a_lru[:, b, :], i_lru[:, b, :], 0.0, mul, add)
                dve.drain()
                tt(mix0[:, i, :], g_lru[:, b, :], r_lru[:, b, :], mul).then_inc(sem("lru_out"), 1)

            for i in range(LRU):
                dve.wait_ge(sem("tile_read"), q0 + 2 * i + 1 + 3)
                dve.drain()
                conv(x_lru[:, i % 2, :], pad[i % 2], CONV_C, lambda t: pcol("lru_w", 8 * t + i), pcol("lru_b", i), T2
                     ).then_inc(sem("lru_conv"), 1)
                if i:
                    lru_tail(i - 1)
            lru_tail(LRU - 1)
            ATT = [(c, hp) for c in range(len(CH2)) for hp in range(Q_TILES)]
            slope = lambda head: float(np.float32(2.0) ** np.float32(-8.0 * (head + 1) / Q_HEADS))

            def normalize(n):
                c, hp = ATT[n]
                cnt, nk, b = CH2[c][1], (META, META + P, META + 2 * P, META + 2 * P, META + 2 * P)[c], n % 2
                st = lambda k: stat[0:cnt, b, k, :]
                dve.wait_ge(sem("exp_ready"), n + 1)
                tt(st(2), st(2), st(3), add)
                dve.drain()
                dve.reciprocal(st(4), st(2))
                dve.drain()
                for e in range(2):
                    x = prob[0:cnt, b, e, 0:nk]
                    m = ts(x, x, stat[0:cnt, b, 4, e:e + 1], None, mul)
                m.then_inc(sem("prob_ready"), 1)

            for n in range(len(ATT) + 1):
                if n < len(ATT):
                    c, hp = ATT[n]
                    cnt, nk, b = CH2[c][1], (META, META + P, META + 2 * P, META + 2 * P, META + 2 * P)[c], n % 2
                    dist = ccol(("dist0", "dist1", "dist2", "dist2", "dist2")[c], 0, nk)[0:cnt, :]
                    dve.wait_ge(sem("scores_done"), n + 1)
                    if n >= 2:
                        dve.wait_ge(sem("prob_turned"), n - 1)
                    for e in range(2):
                        m = stt(prob[0:cnt, b, e, 0:nk], dist, -slope(2 * hp + e), ps[0:cnt, 2 * b + e, 0:nk], mul, add)
                    m.then_inc(sem("scores_read"), 1)
                    dve.drain()
                    st = lambda k: stat[0:cnt, b, k, :]
                    dve.tensor_reduce(st(0), prob[0:cnt, b, :, 0:nk], AX, hi_)
                    dve.drain()
                    tt(st(0), st(0), pcol("sinks", 2 * hp, 2)[0:cnt, :], hi_)
                    dve.drain()
                    ts(st(1), st(0), -1.0, None, mul).then_inc(sem("max_ready"), 1)
                if n:
                    normalize(n - 1)

            def residual(n, src, gain):
                dve.wait_ge(sem("root_ready"), n + 1)
                dve.wait_ge(sem("tile_read"), tiles_of[n])
                dve.reciprocal(rs[:, :], rs[:, :])
                dve.drain()
                stt(src[:, 0, :], src[:, 0, :], gain(0), rs[:, :], mul, mul)
                for k in range(DT):
                    if k + 1 < DT:
                        stt(src[:, k + 1, :], src[:, k + 1, :], gain(k + 1), rs[:, :], mul, mul)
                    dve.drain()
                    tt(h[:, k, :], h[:, k, :], src[:, k, :], add).then_inc(sem("h_updated"), 1)
                dve.drain().then_inc(sem("norm_applied"), 1)

            tiles_of = {4: Q0["out0"] + DT + 2, 6: Q0["down0"] + DT + 2, 8: Q0["out2"] + DT + 2, 10: Q0["down2"] + DT + 2}

            def conv_dyn(out, buf, taps, cols, n_cols, bias, i):
                n = taps - 1
                col = lambda c: par[:, bass.ds(i + c, 1)]
                ts(out, buf[:, n:n + T2], col(cols + n * n_cols), col(bias), mul, add)
                for t in range(n - 1, -1, -1):
                    dve.drain()
                    m = stt(out, buf[:, t:t + T2], col(cols + t * n_cols), out, mul, add)
                return m

            def ffn(up, n, layer, run):
                norm_apply(n - 1, lambda k: pcol(f"fpre{layer}", k), lambda k: h[:, k, :], lambda k: u[:, k, :], T2)
                q0 = Q0[up]
                with dve.Fori(0, FF // 2) as i:
                    for j in range(2):
                        for e in range(2):
                            dve.drain()
                            dve.wait_ge(sem("tile_read"), i * 4 + (q0 + 2 * j + e + 3))
                            conv_dyn((gact, uact)[e], pad[e][:, 1:], CONV_F, PCOL[f"fw{layer}"] + 2 * j + e, 2 * FF,
                                     PCOL[f"fb{layer}"] + 2 * j + e, i * 4).then_inc(sem("ffn_conv"), 1)
                        dve.drain()
                        dve.wait_ge(sem("ffn_gelu"), i * 2 + (FF * run + j + 1))
                        tt(prod[:, bass.ds(i * 2 + j, 1), :].rearrange("p o n -> p (o n)"), gact, uact, mul
                           ).then_inc(sem("prod_ready"), 1)
                residual(n, m_out, lambda k: pcol(f"fpost{layer}", k))

            residual(4, m_out, lambda k: pcol("post0", k))
            ffn("up0", 6, 0, 0)
            norm_apply(7, lambda k: pcol("pre2", k), lambda k: h[:, k, :], lambda k: u[:, k, :], T2)
            q0 = Q0["in2"] + SSD_X
            with dve.Fori(0, SSD_X) as i:
                for j in range(2):
                    dve.wait_ge(sem("tile_read"), i * 2 + (q0 + j + 3))
                    conv_dyn(xbc[:, bass.ds(i * 2 + j, 1), :].rearrange("p o n -> p (o n)"), pad[j], CONV_C,
                             PCOL["ssm_w"] + j, 2 * SSD_X, PCOL["ssm_b"] + j, i * 2).then_inc(sem("ssm_conv"), 1)
            nc5 = len(CH2)
            chunks = lambda x: x.unsqueeze(1).broadcast_to([P, nc5, SSD_H])
            psd = lambda b: ps[:, b, 0:nc5 * SSD_H].rearrange("p (c n) -> p c n", c=nc5)
            dve.wait_ge(sem("dt_done"), 1)
            tt(sa2, psd(4), chunks(pcol("dt_bias2", 0, SSD_H)), add)
            dve.drain()
            log1p_args(sa2, dt2, sb2).then_inc(sem("softplus_arg"), 1)
            dve.wait_ge(sem("softplus_exp"), 3)
            ts(sc2, sb2, 1.0, None, add)
            dve.drain()
            stt(sa2, sc2, -1.0, sb2, add, sub)
            dve.reciprocal(tail2, sc2)
            dve.drain()
            tt(sa2, sa2, tail2, mul).then_inc(sem("softplus_one"), 1)
            dve.wait_ge(sem("softplus_ln"), 3)
            tt(sc2, sc2, sa2, sub)
            dve.drain()
            tt(dt2, dt2, sc2, add)
            dve.drain()
            stt(da2, dt2, -1.0, chunks(egt2[:, 0, :]), mul, mul).then_inc(sem("da_ready"), 1)
            dve.wait_ge(sem("cs2_done"), 1)
            dve.tensor_copy(cs2, psd(5))
            dve.tensor_copy(gt2_, psd(6)).then_inc(sem("cs2_read"), 1)
            dve.drain()
            tt(tail2, gt2_, cs2, sub)
            dve.drain()
            ts(tail2, tail2, 0.0, None, lo_).then_inc(sem("tail_arg"), 1)
            SSD = [(c, g) for c in range(nc5) for g in range(SSD_G)]

            def ssd_mask(n):
                c, g = SSD[n]
                cnt, b = CH2[c][1], n % 2
                dve.wait_ge(sem("ssd_decay"), n + 1)
                d = decay2[b][0:cnt, :, 0:cnt]
                tt(d, d, cbm[0:cnt, b, 0:cnt].unsqueeze(1).broadcast_to([cnt, 4, cnt]), mul).then_inc(sem("ssd_dve"), 1)

            def ssd_result(n):
                c, g = SSD[n]
                (lo, cnt), b = CH2[c], n % 2
                dve.wait_ge(sem("ssd_out_done"), n + 1)
                st = st2[:, 4 * g:4 * g + 4, :]
                new = ps[:, 6 + b, 0:256].rearrange("p (h n) -> p h n", h=4)
                for e in range(2):
                    x = xbc[:, 2 * g + e, lo:lo + cnt]
                    stt(x, x, pcol("d_skip", 2 * g + e), ps[:, 4 + b, P * e:P * e + cnt], mul, add)
                if c:
                    for e in range(4):
                        head = 4 * g + e
                        m = stt(st[:, e, :], st[:, e, :], egt2[:, c, head:head + 1], new[:, e, :], mul, add)
                else:
                    m = dve.tensor_copy(st, new)
                m.then_inc(sem("st2_ready"), 1)
                dve.drain().then_inc(sem("ssd_out_read"), 1)

            dve.wait_ge(sem("tail_ready"), 1)
            for n in range(len(SSD) + 2):
                if n < len(SSD):
                    c, g = SSD[n]
                    (lo, cnt), b = CH2[c], n % 2
                    dve.wait_ge(sem("ssd_in_done"), n + 1)
                    if n >= 2:
                        dve.wait_ge(sem("ssd_out_done"), n - 1)
                    bank = ps[:, 2 * b + 1, :]
                    tt(cbm[0:cnt, b, 0:cnt], bank[0:cnt, 0:cnt], upto[0:cnt, 0:cnt], mul)
                    dve.tensor_copy(b_tok[0:cnt, b, :], bank[0:cnt, P:2 * P])
                    tt(xdt[b][0:cnt], bank[0:cnt, 2 * P:].rearrange("p (h n) -> p h n", h=4),
                       dt2[0:cnt, c, 4 * g:4 * g + 4].unsqueeze(2).broadcast_to([cnt, 4, HEAD]), mul
                       ).then_inc(sem("ssd_xdt"), 1)
                    dve.wait_ge(sem("ssd_eg"), n + 1)
                    d = decay2[b][0:cnt, :, 0:cnt]
                    for e in range(4):
                        m = ts(d[:, e, :], ps[0:cnt, 2 * b, P * e:P * e + cnt], cs2[0:cnt, c, 4 * g + e:4 * g + e + 1],
                               0.0, sub, lo_)
                    m.then_inc(sem("ssd_diff"), 1)
                if 1 <= n <= len(SSD):
                    ssd_mask(n - 1)
                if n >= 2:
                    ssd_result(n - 2)
            for t in range(SSD_X):
                tt(xbc[:, t, :], xbc[:, t, :], z2[:, t, :], mul).then_inc(sem("gated"), 1)
            for g in range(SSD_G):
                dve.wait_ge(sem("group_root"), g + 1)
                dve.reciprocal(groot[g % 2], groot[g % 2])
                dve.drain()
                for e in range(2):
                    x = xbc[:, 2 * g + e, :]
                    stt(x, x, pcol("gate_norm", 2 * g + e), groot[g % 2], mul, mul).then_inc(sem("mix2_ready"), 1)
            residual(8, m2_out, lambda k: pcol("post2", k))
            ffn("up2", 10, 2, 1)

        @block.gpsimd
        def _(pool):
            pool.wait_ge(sem("powers_ready"), 1)
            for j in range(S5_TILES):
                if j >= 2:
                    pool.wait_ge(sem("table_used"), j - 1)
                C, Sn = (x.rearrange("p (a b) -> p a b", b=32) for x in table[j % 2])
                t1, t2 = (x.rearrange("p (a b) -> p a b", b=32) for x in tabt)
                f = [x[:, j, :].unsqueeze(1).broadcast_to([P, 16, 32]) for x in fine]
                g = [x[:, j, :].unsqueeze(2).broadcast_to([P, 16, 32]) for x in coarse]
                pool.tensor_tensor(t1, g[0], f[0], ALU.mult)
                pool.tensor_tensor(t2, g[1], f[1], ALU.mult)
                pool.drain()
                pool.tensor_tensor(C, t1, t2, ALU.subtract)
                pool.drain()
                pool.tensor_tensor(t1, g[0], f[1], ALU.mult)
                pool.tensor_tensor(t2, g[1], f[0], ALU.mult)
                pool.drain()
                pool.tensor_tensor(Sn, t1, t2, ALU.add).then_inc(sem("table_ready"), 1)
                pool.drain()
            for v in range(LEVELS):
                mask = ccol("levels", v * P, P).unsqueeze(1).broadcast_to([P, HEADS, P])
                for c in range(CHUNKS):
                    if v == 0:
                        pool.wait_ge(sem("a_ready"), c + 1)
                    else:
                        pool.wait_ge(sem("ax_done"), CHUNKS * (v - 1) + c + 1)
                    pool.tensor_tensor(a_lev[:, c], amat[:, c], mask, ALU.mult).then_inc(sem("level_ready"), 1)

            pool.wait_ge(sem("slots_ready"), 1)
            pool.wait_ge(sem("xtok_read"), 8)
            pool.wait_ge(sem("rows_zeroed"), 16)
            for n in range(2 * CHUNKS):
                pool.indirect_dma_start(out=rows_in, out_offset=bass.IndirectOffsetOnAxis(ap=slot_id[:, n:n + 1], axis=0),
                                        in_=xtok[:, n % CHUNKS, :], in_offset=None).then_inc(sem("rows_scattered"), 16)
            pool.wait_ge(sem("rows_stored0"), 16 * FREE + 16 * PAIRS + 16)
            pool.wait_ge(sem("rows_stored1"), 16 * FREE + 16 * PAIRS)
            for n in range(2 * CHUNKS):
                pool.indirect_dma_start(out=(y1 if n < CHUNKS else y2)[:, n % CHUNKS, :], out_offset=None, in_=rows_out,
                                        in_offset=bass.IndirectOffsetOnAxis(ap=slot_id[:, n:n + 1], axis=0)
                                        ).then_inc(sem("rows_gathered"), 16)

            for n in range(len(CH2) * SSD_G):
                c, g = n // SSD_G, n % SSD_G
                (lo, cnt), b = CH2[c], n % 2
                if n >= 2:
                    pool.wait_ge(sem("ssd_out_done"), n - 1)
                pool.wait_ge(sem("ssd_xdt"), n + 1)
                pool.tensor_tensor(xdd[0:cnt, b], xdt[b][0:cnt], tail2[0:cnt, c, 4 * g:4 * g + 4].unsqueeze(2).broadcast_to(
                    [cnt, 4, HEAD]), ALU.mult)
                pool.wait_ge(sem("ssd_eg"), n + 1)
                C = xbc[:, SSD_X + SSD_G + g, lo:lo + cnt]
                pool.tensor_tensor(cdec[b][:, :, 0:cnt], eg2[b][:, :, 0:cnt], C.unsqueeze(1).broadcast_to([P, 4, cnt]),
                                   ALU.mult).then_inc(sem("ssd_pool"), 1)


def _units(blocks):
    n = len(blocks) // 16
    return blocks.reshape(n, 16, P, P).transpose(0, 2, 1, 3).reshape(n, P, UNIT)


def _blocks(w, order=None):
    k, m = w.shape[0] // P, w.shape[1] // P
    b = w.reshape(k, P, m, P).transpose(2, 0, 1, 3)
    if order is not None:
        b = b[order]
    return b.reshape(-1, P, P)


def _pad(blocks):
    return np.concatenate([blocks, np.zeros(((-len(blocks)) % 16, P, P), np.float32)])


def _down(w):
    b = _blocks(w).reshape(-1, DOWN_K, P, P)
    return np.concatenate([b, np.zeros((len(b), 16 - DOWN_K, P, P), np.float32)], 1).reshape(-1, P, P)


def _stream(a):
    pairs = [t for i in range(FF) for t in (i, FF + i)]
    w0 = a["l0_w_in_2"]
    q0 = 2 * LRU * P
    kv = q0 + Q_TILES * P
    kdup = [w0[:, kv + HEAD * h:kv + HEAD * (h + 1)] for h in (0, 0, 1, 1)]
    w0 = np.concatenate([w0[:, :kv], *kdup, w0[:, kv + P:kv + 2 * P]], 1)
    order0 = [t for i in range(LRU) for t in (i, LRU + i)] + list(range(2 * LRU, 2 * LRU + Q_TILES + 3))
    ada, in1 = _blocks(a["w_ada"][0]), _blocks(np.ascontiguousarray(a["w_in"][0][:, :20 * P]))
    mixed = [x for m in range(8) for x in (in1[32 + 16 * m:48 + 16 * m], ada[128 + 32 * m:160 + 32 * m])]
    parts = [ada[:128], in1[:32], *mixed,
             _blocks(a["w_glu"][0]), _blocks(a["w_out"][0]),
             _pad(_blocks(w0, order0)), _blocks(a["l0_w_out_2"]),
             _blocks(a["l0_ffn_w_up_2"], pairs), _down(a["l0_ffn_w_down_2"]),
             _blocks(np.ascontiguousarray(a["l1_w_in_2"][:, :48 * P])), _blocks(a["l1_w_out_2"]),
             _blocks(a["l1_ffn_w_up_2"], pairs), _down(a["l1_ffn_w_down_2"])]
    out = _units(np.concatenate(parts))
    assert len(out) == UNITS, (len(out), UNITS)
    return out


def _columns(v):
    return np.asarray(v).reshape(-1, P).T


def _taps(w):
    return np.concatenate([_columns(t) for t in w], 1)


def _params(a):
    pairs = np.array([t for i in range(FF) for t in (i, FF + i)])
    rows = lambda v: np.broadcast_to(np.asarray(v).reshape(1, -1), (P, np.asarray(v).size))
    ffw = lambda w: np.concatenate([_columns(t)[:, pairs] for t in w], 1)
    state = lambda v: np.repeat(np.asarray(v).reshape(-1), 64).reshape(S5_TILES, P).T
    values = {
        "c": _columns(a["c"][0]), "b_ada": _columns(a["b_ada"][0]), "norm1_g": _columns(a["norm1_g"][0]),
        "norm2_g": _columns(a["norm2_g"][0]), "normf_g": _columns(a["normf_g"]), "s5_d": _columns(a["s5_d"][0]),
        "b_glu": _columns(a["b_glu"][0]), "conv_w": _taps(a["conv_w"][0]), "gdn_norm_g": _columns(a["gdn_norm_g"][0]),
        "lam_re": a["lam_re"][0].reshape(S5_TILES, P).T, "lam_im": a["lam_im"][0].reshape(S5_TILES, P).T,
        "log_step": state(a["log_step"][0]), "a_log": rows(a["a_log"][0]), "dt_bias": rows(a["dt_bias"][0]),
        "pre0": _columns(a["l0_mix_pre_norm_2"]), "post0": _columns(a["l0_mix_post_norm_2"]),
        "lru_w": _taps(a["l0_lru_conv_w_2"]), "lru_b": _columns(a["l0_lru_conv_b_2"]),
        "b_a": _columns(a["l0_lru_b_a_2"]), "b_x": _columns(a["l0_lru_b_x_2"]), "lam": _columns(a["l0_lru_lambda_2"]),
        "fpre0": _columns(a["l0_ffn_pre_norm_2"]), "fpost0": _columns(a["l0_ffn_post_norm_2"]),
        "fw0": ffw(a["l0_ffn_conv_w_2"]), "fb0": _columns(a["l0_ffn_conv_b_2"])[:, pairs], "sinks": rows(a["l0_attn_sinks_2"]),
        "pre2": _columns(a["l1_mix_pre_norm_2"]), "post2": _columns(a["l1_mix_post_norm_2"]),
        "ssm_w": _taps(a["l1_ssm_conv_w_2"]), "ssm_b": _columns(a["l1_ssm_conv_b_2"]),
        "gate_norm": _columns(a["l1_gate_norm_2"]), "d_skip": _columns(np.repeat(a["l1_d_skip_2"], 64)),
        "dt_bias2": rows(a["l1_dt_bias_2"]), "a_log2": rows(a["l1_a_log_2"]),
        "fpre2": _columns(a["l1_ffn_pre_norm_2"]), "fpost2": _columns(a["l1_ffn_post_norm_2"]),
        "fw2": ffw(a["l1_ffn_conv_w_2"]), "fb2": _columns(a["l1_ffn_conv_b_2"])[:, pairs],
    }
    return np.concatenate([values[name] for name, _ in PARAMS], 1)


def _s5(a):
    b, c = np.zeros((2, P, 4, P), np.float32), np.zeros((2, P, S5_TILES, 32), np.float32)
    for n, (wb, wc) in enumerate((("s5_b_re", "s5_c_re"), ("s5_b_im", "s5_c_im"))):
        wb, wc = a[wb][0], a[wc][0]
        for g in range(32):
            j, r = g // 2, g % 2
            row = 32 * (j % 4) + 16 * r
            b[n, row:row + 16, j // 4, 64 * r:64 * r + 64] = wb[g].T
            c[n, 64 * r:64 * r + 64, j, 16 * r:16 * r + 16] = wc[g].T
    return np.concatenate([b[0].reshape(P, -1), b[1].reshape(P, -1), c[0].reshape(P, -1), c[1].reshape(P, -1)], 1)


def _rows8(w):
    return w.reshape(DT, P, -1).transpose(1, 0, 2).reshape(P, -1)


def _experts(a):
    gu = np.concatenate([a["w_gate"][0], a["w_up"][0]], 2).reshape(EXPERTS, DT, P, 2 * D_EXPERT).transpose(0, 2, 1, 3)
    dn = a["w_down"][0].reshape(EXPERTS, 2, P, D).transpose(0, 2, 1, 3)
    return np.concatenate([gu.reshape(EXPERTS, P, -1), dn.reshape(EXPERTS, P, -1)], 2).reshape(EXPERTS * P, 3 * UNIT)


def layout(inputs):
    a = {k: np.asarray(v) for k, v in inputs.items()}
    return {
        "x_fm": np.ascontiguousarray(a["x"][0].T.reshape(DT, P, SEQ).transpose(1, 0, 2)),
        "meta_fm": np.ascontiguousarray(a["meta_tokens_2"].T.reshape(DT, P, META).transpose(1, 0, 2)),
        "stream": _stream(a),
        "params": np.ascontiguousarray(_params(a)),
        "consts": shape_constants(),
        "s5": _s5(a),
        "w_gates": _rows8(np.ascontiguousarray(a["w_in"][0][:, 20 * P:])),
        "w_router": _rows8(np.concatenate([a["w_router_grp"][0], a["w_router_exp"][0]], 1)),
        "w_lru": np.ascontiguousarray(np.concatenate([a["l0_lru_w_a_2"], a["l0_lru_w_x_2"]], 0).transpose(1, 0, 2)).reshape(P, -1),
        "w_dt": _rows8(np.ascontiguousarray(a["l1_w_in_2"][:, 48 * P:])),
        "experts": _experts(a),
    }


def kernel(**inputs):
    import concourse.bacc as _bacc
    from concourse.bass_utils import run_bass_kernel_spmd as _run

    nc = _bacc.Bacc("TRN2", target_bir_lowering=False, num_devices=1)
    arrays, args = {}, {}
    for name, v in layout(inputs).items():
        arrays[f"in_{name}"] = v
        args[name] = nc.dram_tensor(f"in_{name}", v.shape, mybir.dt.from_np(v.dtype), kind="ExternalInput").ap()
    args["out"] = nc.dram_tensor("out_fm", (P, DT, SEQ), F32, kind="ExternalOutput").ap()
    program(nc, args)
    got = _run(nc, [arrays], core_ids=[0]).results[0]["out_fm"]
    return np.ascontiguousarray(got.transpose(2, 1, 0).reshape(1, SEQ, D))
```
